# Optimizing a Trainium2 kernel written in Bass

```python
import math
import jax, jax.numpy as jnp
from jax import lax
import numpy as np

D_MODEL = 1024
BATCH = 1
SEQ = 512
DEPTH = 2

N_A = DEPTH // 2
N_B = DEPTH - N_A
HG_DK = 128
HG_HEADS = D_MODEL // HG_DK
HG_DV = D_MODEL // HG_HEADS
HG_WIDTH = HG_HEADS * HG_DK
HG_VWIDTH = HG_HEADS * HG_DV
HG_CHUNK = 64
ATT_HD = 64
ATT_QH = D_MODEL // ATT_HD
ATT_KVH = 4
ATT_G = ATT_QH // ATT_KVH
WINDOW = 128
FFN_HIDDEN = -(-8 * D_MODEL // (3 * 256)) * 256
PLE_DIM = 256
DEEPNORM_ALPHA = (2.0 * DEPTH) ** 0.25
DEEPNORM_BETA = (8.0 * DEPTH) ** -0.25
LN_EPS = 1e-5
RMS_EPS = 1e-6

kernel_name = 'yoco_hgrn2_swa_sink_alibi_deepnorm'

def layer_norm(x, g, b):
    xf = x.astype(jnp.float32)
    mu = jnp.mean(xf, axis=-1, keepdims=True)
    var = jnp.mean(jnp.square(xf - mu), axis=-1, keepdims=True)
    return ((xf - mu) * lax.rsqrt(var + LN_EPS) * g.astype(jnp.float32) + b.astype(jnp.float32)).astype(x.dtype)

def rms_norm(x, g):
    xf = x.astype(jnp.float32)
    return xf * lax.rsqrt(jnp.mean(jnp.square(xf), axis=-1, keepdims=True) + RMS_EPS) * g.astype(jnp.float32)

def hgrn2_mixer(x, w_in, lb, norm_gain, w_out):
    B, S, _ = x.shape
    f32 = jnp.float32
    proj = x @ w_in
    q = proj[..., :HG_WIDTH]
    f = proj[..., HG_WIDTH:2 * HG_WIDTH].astype(f32)
    v = proj[..., 2 * HG_WIDTH:2 * HG_WIDTH + HG_VWIDTH].astype(f32)
    g = proj[..., 2 * HG_WIDTH + HG_VWIDTH:]
    lb = lb.astype(f32)
    forget = lb + (1.0 - lb) * jax.nn.sigmoid(f)
    log_f = jnp.log(forget)
    k = (1.0 - lb) * jax.nn.sigmoid(-f)
    q = jax.nn.silu(q.astype(f32)) * (HG_DK ** -0.5)
    nc = S // HG_CHUNK

    def to_chunks(t, d):
        return t.reshape(B, nc, HG_CHUNK, HG_HEADS, d).transpose(1, 0, 3, 2, 4)

    causal = jnp.tril(jnp.ones((HG_CHUNK, HG_CHUNK), dtype=bool))[:, :, None]

    def step(state, inp):
        qc, kc, gc, vc = inp
        b = jnp.cumsum(gc, axis=2)
        diff = b[:, :, :, None, :] - b[:, :, None, :, :]
        decay = jnp.exp(jnp.where(causal, diff, -jnp.inf))
        scores = jnp.einsum('bhtc,bhsc,bhtsc->bhts', qc, kc, decay)
        o = jnp.einsum('bhts,bhsv->bhtv', scores, vc) + jnp.einsum('bhtc,bhcv->bhtv', qc * jnp.exp(b), state)
        b_last = b[:, :, -1:, :]
        state = jnp.exp(b_last[:, :, 0, :, None]) * state + jnp.einsum('bhsc,bhsv->bhcv', kc * jnp.exp(b_last - b), vc)
        return state, o

    s0 = jnp.zeros((B, HG_HEADS, HG_DK, HG_DV), f32)
    _, o = lax.scan(step, s0, (to_chunks(q, HG_DK), to_chunks(k, HG_DK), to_chunks(log_f, HG_DK), to_chunks(v, HG_DV)))
    o = o.transpose(1, 0, 3, 2, 4).reshape(B, S, HG_HEADS, HG_DV)
    o = rms_norm(o, norm_gain) * jax.nn.silu(g.astype(f32)).reshape(B, S, HG_HEADS, HG_DV)
    return o.reshape(B, S, HG_VWIDTH).astype(x.dtype) @ w_out

def shared_kv(h, kv_w, kv_b):
    B, S, _ = h.shape
    kv = h @ kv_w + kv_b
    kdim = ATT_KVH * ATT_HD
    return kv[..., :kdim].reshape(B, S, ATT_KVH, ATT_HD), kv[..., kdim:].reshape(B, S, ATT_KVH, ATT_HD)

def band_blocks(t):
    B, S = t.shape[:2]
    tp = jnp.pad(t, ((0, 0), (WINDOW, 0), (0, 0), (0, 0)))
    tr = tp.reshape(B, S // WINDOW + 1, WINDOW, ATT_KVH, ATT_HD)
    return jnp.concatenate([tr[:, :-1], tr[:, 1:]], axis=2)

def alibi_slopes(n_heads):
    return jnp.exp2(-8.0 * jnp.arange(1, n_heads + 1, dtype=jnp.float32) / n_heads)

def swa_sink_mixer(x, k_blocks, v_blocks, w_q, b_q, sinks, w_out, b_out):
    B, S, _ = x.shape
    nb = S // WINDOW
    f32 = jnp.float32
    q = (x @ w_q + b_q).reshape(B, nb, WINDOW, ATT_KVH, ATT_G, ATT_HD)
    s = jnp.einsum('bnqkgd,bnskd->bnkgqs', q, k_blocks).astype(f32) * (ATT_HD ** -0.5)
    qi = jnp.arange(WINDOW)[:, None]
    si = jnp.arange(2 * WINDOW)[None, :]
    dist = qi - si + WINDOW
    blk = jnp.arange(nb)[:, None, None]
    valid = (dist >= 0) & (dist < WINDOW) & (blk * WINDOW - WINDOW + si >= 0)
    slopes = alibi_slopes(ATT_QH).reshape(ATT_KVH, ATT_G)
    s = s - slopes[:, :, None, None] * dist.astype(f32)
    s = jnp.where(valid[None, :, None, None], s, -jnp.inf)
    sink = jnp.broadcast_to(sinks.astype(f32).reshape(ATT_KVH, ATT_G)[None, None, :, :, None, None], s.shape[:-1] + (1,))
    probs = jax.nn.softmax(jnp.concatenate([s, sink], axis=-1), axis=-1)[..., :-1]
    o = jnp.einsum('bnkgqs,bnskd->bnqkgd', probs.astype(v_blocks.dtype), v_blocks).reshape(B, S, ATT_QH * ATT_HD)
    return o @ w_out + b_out

def swiglu(x, w_gate_up, w_down):
    gu = x @ w_gate_up
    return (jax.nn.silu(gu[..., :FFN_HIDDEN]) * gu[..., FFN_HIDDEN:]) @ w_down

def per_layer_embedding(x, p_i, w_up, w_gate, b_gate):
    return jax.nn.sigmoid(x @ w_gate + b_gate) * (p_i @ w_up)

def setup_inputs(seed: int = 0) -> dict:
    key = jax.random.key(seed)
    ks = jax.random.split(key, 24)
    D = D_MODEL
    nrm = lambda k, shape, scale: jax.random.normal(k, shape, jnp.float32) * scale
    kvd = ATT_KVH * ATT_HD
    qd = ATT_QH * ATT_HD
    return {
        'x': nrm(ks[0], (BATCH, SEQ, D), 1.0),
        'p': nrm(ks[1], (DEPTH, BATCH, SEQ, PLE_DIM), 1.0),
        'a_w_in': jnp.concatenate([
            nrm(ks[2], (N_A, D, 2 * HG_WIDTH), D ** -0.5),
            nrm(ks[3], (N_A, D, HG_VWIDTH), D ** -0.5 * DEEPNORM_BETA),
            nrm(ks[4], (N_A, D, HG_VWIDTH), D ** -0.5)], axis=-1),
        'a_lower_bound': nrm(ks[5], (N_A + 1, HG_WIDTH), 0.5),
        'a_norm_gain': 1.0 + nrm(ks[6], (N_A, HG_DV), 0.05),
        'a_w_out': nrm(ks[7], (N_A, HG_VWIDTH, D), HG_VWIDTH ** -0.5 * DEEPNORM_BETA),
        'kv_w': jnp.concatenate([
            nrm(ks[8], (D, kvd), D ** -0.5),
            nrm(ks[9], (D, kvd), D ** -0.5 * DEEPNORM_BETA)], axis=-1),
        'kv_b': nrm(ks[10], (2 * kvd,), 0.02),
        'b_w_q': nrm(ks[11], (N_B, D, qd), D ** -0.5),
        'b_b_q': nrm(ks[12], (N_B, qd), 0.02),
        'b_sinks': nrm(ks[13], (N_B, ATT_QH), 1.0),
        'b_w_out': nrm(ks[14], (N_B, qd, D), qd ** -0.5 * DEEPNORM_BETA),
        'b_b_out': nrm(ks[15], (N_B, D), 0.02),
        'ffn_w_gate_up': nrm(ks[16], (DEPTH, D, 2 * FFN_HIDDEN), D ** -0.5),
        'ffn_w_down': nrm(ks[17], (DEPTH, FFN_HIDDEN, D), FFN_HIDDEN ** -0.5 * DEEPNORM_BETA),
        'ple_w_up': nrm(ks[18], (DEPTH, PLE_DIM, D), PLE_DIM ** -0.5 * DEEPNORM_BETA),
        'ple_w_gate': nrm(ks[19], (DEPTH, D, D), D ** -0.5),
        'ple_b_gate': nrm(ks[20], (DEPTH, D), 0.02),
        'ln_gain': 1.0 + nrm(ks[21], (DEPTH, 3, D), 0.05),
        'ln_bias': nrm(ks[22], (DEPTH, 3, D), 0.02),
    }

def reference(x, p, a_w_in, a_lower_bound, a_norm_gain, a_w_out, kv_w, kv_b, b_w_q, b_b_q, b_sinks, b_w_out, b_b_out,
              ffn_w_gate_up, ffn_w_down, ple_w_up, ple_w_gate, ple_b_gate, ln_gain, ln_bias):
    lower_bounds = jnp.cumsum(jax.nn.softmax(a_lower_bound.astype(jnp.float32), axis=0), axis=0)
    k_blocks = None
    v_blocks = None
    for i in range(DEPTH):
        if i < N_A:
            h = hgrn2_mixer(x, a_w_in[i], lower_bounds[i], a_norm_gain[i], a_w_out[i])
        else:
            if i == N_A:
                k_sh, v_sh = shared_kv(x, kv_w, kv_b)
                k_blocks = band_blocks(k_sh)
                v_blocks = band_blocks(v_sh)
            j = i - N_A
            h = swa_sink_mixer(x, k_blocks, v_blocks, b_w_q[j], b_b_q[j], b_sinks[j], b_w_out[j], b_b_out[j])
        x = layer_norm(DEEPNORM_ALPHA * x + h, ln_gain[i, 0], ln_bias[i, 0])
        x = layer_norm(DEEPNORM_ALPHA * x + swiglu(x, ffn_w_gate_up[i], ffn_w_down[i]), ln_gain[i, 1], ln_bias[i, 1])
        x = layer_norm(DEEPNORM_ALPHA * x + per_layer_embedding(x, p[i], ple_w_up[i], ple_w_gate[i], ple_b_gate[i]),
                       ln_gain[i, 2], ln_bias[i, 2])
    return x


_drawn_inputs = setup_inputs


def setup_inputs(seed=0):
    import zlib

    import numpy as np

    out = dict(_drawn_inputs(seed))
    spreads = {}
    factors = {'a_lower_bound': 4.652,
     'a_norm_gain': 5.055,
     'kv_b': 8.0,
     'b_b_q': 64.0,
     'b_sinks': 7.24,
     'b_b_out': 4.05,
     'ple_b_gate': 27.74}
    for name, (base, spread) in spreads.items():
        noise = np.random.default_rng([zlib.crc32(name.encode()), seed]).standard_normal(out[name].shape)
        drawn = base * np.exp(spread * noise) if base else spread * noise
        out[name] = __import__('jax').numpy.asarray(drawn.astype(out[name].dtype))
    for name, factor in factors.items():
        out[name] = (out[name] * factor).astype(out[name].dtype)
    return out
```

```python
from contextlib import ExitStack

import concourse.bass as bass
from concourse import mybir

F32 = mybir.dt.float32
F32R = mybir.dt.float32r
BF16 = mybir.dt.bfloat16
U16 = mybir.dt.uint16
ALU = mybir.AluOpType
ACT = mybir.ActivationFunctionType
AX_X = mybir.AxisListType.X

P = 128


def yoco_trunk(nc, x_in, p_in, a_w_in, a_lb, a_gain, a_w_out, kv_w, kv_b, w_q, b_q, sinks, w_o, b_o,
               w_gu, w_dn, w_up, w_gate, b_gate, ln_g, ln_b, out):
    S, D = x_in.shape[1:]
    NT = D // P
    TT = S // P
    HEADS = NT
    KVD = kv_w.shape[1] // 2
    KVH, HD = 4, 64
    G = D // HD // KVH
    QH = KVH * G
    WIN = P
    F = w_dn.shape[1]
    PT = w_up.shape[1] // P
    LAYERS = w_gu.shape[0]
    ALPHA = (2.0 * LAYERS) ** 0.25
    QSCALE = float(P) ** -0.5
    ASCALE = float(HD) ** -0.5
    LEVELS = P.bit_length() - 1
    FT = F // P
    PARTS = [8, 8, FT - 16]
    KMAX = NT + PT
    FAR = 1e30
    assert S == 512 and TT == 4 and NT == 8 and PARTS[2] % 2 == 0

    R_HG = 0
    R_WO = R_HG + HEADS
    at = R_WO + NT // 4
    R_GU, R_DN, R_PLE = [], [], []
    for layer in range(LAYERS):
        if layer == 1:
            R_KV = at
            R_Q = R_KV + 1
            R_AO = R_Q + 2
            at = R_AO + 2
        R_GU.append([])
        R_DN.append([])
        for n in PARTS:
            R_GU[layer].append(at)
            R_DN[layer].append(at + n // 2)
            at += n // 2 + 2
        R_PLE.append(at)
        at += 2
    ROUNDS = at
    M_HG, M_GU, M_AT = 0, [[8, 16, 24], [38, 46, 54]], 30

    with ExitStack() as ctx:
        def sb(name, shape, dt=F32):
            return ctx.enter_context(nc.sbuf_tensor(name, shape, dt))

        def sem(name):
            return ctx.enter_context(nc.semaphore(name))

        bank = ctx.enter_context(nc.psum_tensor("bank", [P, 8, S], F32))

        x = sb("x", [P, NT, S])
        x_hi = sb("x_hi", [P, NT, S], F32R)
        x_lo = sb("x_lo", [P, NT, S], F32R)
        mid_hi = sb("mid_hi", [P, NT, S], F32R)
        mid_lo = sb("mid_lo", [P, NT, S], F32R)
        w_raw = sb("w_raw", [P, 4, KMAX * P])
        w_hi = sb("w_hi", [P, 4, KMAX * P], F32R)
        w_lo = sb("w_lo", [P, 4, KMAX * P], F32R)
        p_rows = sb("p_rows", [P, TT, PT * P])
        pe_hi = sb("pe_hi", [P, PT, S], F32R)
        pe_lo = sb("pe_lo", [P, PT, S], F32R)
        ident = sb("ident", [P, P])
        ones_d = sb("ones_d", [P, P])
        ones_v = sb("ones_v", [P, P])
        vec = sb("vec", [P, 160])
        lbs = sb("lbs", [P, 3, HEADS])
        sink = sb("sink", [P, QH])
        stat = sb("stat", [P, 2, 5, TT])
        arena = sb("arena", [P, 12288])

        taken = [0]

        def carve(words):
            taken[0] += words
            assert taken[0] <= 12288
            return arena[:, taken[0] - words:taken[0]]

        q_t, f_t, k_raw, k_dec, q_dec, g_t = (carve(S) for _ in range(6))
        s_q, s_f, s_n, v_t, s_g = (carve(S) for _ in range(5))
        v_row = carve(S).rearrange("p (c v) -> p c v", c=TT)
        a_mat = carve(S)
        kd_row = carve(3 * P).rearrange("p (c k) -> p c k", c=3)
        state = carve(3 * P).rearrange("p (c v) -> p c v", c=3)
        tot = [f_t] + [carve(S >> l) for l in range(1, LEVELS + 1)]
        o_sq, o_rms, o_inv, o_n, o_g = (carve(S) for _ in range(5))
        eye_m = carve(S // 2).bitcast(BF16)
        lvl_m = [carve(S // 4).bitcast(BF16) for _ in range(LEVELS)]
        x_rows = arena[:, 0:TT * D].rearrange("p (t d) -> p t d", t=TT)
        vec_rows = arena[:, TT * D:TT * D + 2 * P].rearrange("p (a c) -> p a c", a=2)
        taken[0] = 0
        k_pad = carve(KVH * (WIN + S)).rearrange("p (h s) -> p h s", h=KVH)
        v_all = carve(TT * KVD).rearrange("p (b v) -> p b v", b=TT)
        dist = carve(TT * 2 * WIN)
        shared = taken[0]
        scores = [carve(TT * 2 * WIN).rearrange("p (b s) -> p b s", b=TT) for _ in range(2)]
        p_t = carve(TT * 2 * WIN).rearrange("p (b h t) -> p b h t", b=TT, h=2)
        q_s = [carve(2 * S).rearrange("p (u t) -> p u t", u=2) for _ in range(2)]
        v_cols = p_t[:, :, :, :].rearrange("p b h t -> p (b h t)").rearrange("p (u t) -> p u t", u=2)
        taken[0] = shared
        sq = [carve(S) for _ in range(2)]
        act_t = [carve(S) for _ in range(2)]
        hid = [carve(S) for _ in range(2)]
        sum_y, sum_sq, mean, mean_sq, var, rstd = (carve(S) for _ in range(6))
        out_rows = arena[:, 0:TT * D].rearrange("p (t d) -> p t d", t=TT)

        C_G, C_B = 0, LAYERS * 3 * NT
        C_KV = 2 * LAYERS * 3 * NT
        C_BQ = C_KV + 2 * KVD // P
        C_BO = C_BQ + NT
        N_A = C_BO + NT
        C_PG = N_A
        C_LB = C_PG + LAYERS * NT
        C_NG = C_LB + 2 * NT
        N_ALL = C_NG + 1

        w_landed = [sem(f"w_landed{s}") for s in range(4)]
        up_landed = [sem(f"up_landed{s}") for s in range(4)]
        w_hi_ready, w_lo_ready = sem("w_hi_ready"), sem("w_lo_ready")
        unit_done = sem("unit_done")
        bank_free = [sem("bank_free0"), sem("bank_free1")]
        rows_landed, vecs_landed, sink_landed = sem("rows_landed"), sem("vecs_landed"), sem("sink_landed")
        p_landed = [sem("p_landed0"), sem("p_landed1")]
        consts, masks, far_ready = sem("consts"), sem("masks"), sem("far_ready")
        turned, turn_read = sem("turned"), sem("turn_read")
        lb_ready = sem("lb_ready")
        p_hi_ready, p_lo_ready = sem("p_hi_ready"), sem("p_lo_ready")
        x_f32, x_hi_ready, x_ready = sem("x_f32"), sem("x_hi_ready"), sem("x_ready")
        mid_ready = sem("mid_ready")
        sq_r, sf_r, sn_r, sg_r, vt_r = (sem(n) for n in ("sig_q", "sig_f", "sig_n", "sig_g", "v_copied"))
        q_r, f_r, k_r, g_r = (sem(n) for n in ("q_ready", "forget_ready", "k_ready", "gate_ready"))
        kd0_r, kd_r, qd_r, tot_r = (sem(n) for n in ("kdec_begun", "kdec_ready", "qdec_ready", "totals"))
        pe_vtr, vrow_r, pe_diag, pe_lvl, a_r = (sem(n) for n in
                                                ("v_turned", "v_rows", "diag_done", "level_done", "a_ready"))
        pe_kt, kt_r, pe_ds, st_r, pe_o = (sem(n) for n in
                                          ("k_turned", "k_rows", "state_terms", "states", "o_done"))
        osq_r, pe_ms, rms_r, oinv_r, on_r, og_r, oh_r = (
            sem(n) for n in ("o_squared", "o_mean_sq", "o_rms_r", "o_inv_r", "o_normed", "o_gated", "o_hi"))
        silu_r = [sem(f"silu{i}") for i in range(LAYERS)]
        hhi_r = [sem(f"hidden_hi{i}") for i in range(LAYERS)]
        gate_r = sem("ple_gate")
        biased = sem("ao_biased")
        y_r, sq_done, sumy_r, sumsq_r = (sem(n) for n in ("y_ready", "y_squared", "sum_y_r", "sum_sq_r"))
        stat_mm, mean_r, msq_r, var_r, std_r, rstd_r = (
            sem(n) for n in ("stat_mm", "mean_r", "mean_sq_r", "var_r", "std_r", "rstd_r"))
        cen_r, nrm_r = sem("centred"), sem("normed")
        k_w, k_ok, v_w, v_turn, v_ok = (sem(n) for n in ("k_biased", "k_both", "v_biased", "v_turned_b", "v_ok"))
        s_done, sc_r, mx_r, nmx_r, exp_r, den_r, rden_r, p_r = (
            sem(n) for n in ("scores_done", "scores_r", "max_r", "neg_max_r", "exp_r", "den_r", "rden_r", "p_r"))
        t_done, pta_r, ptb_r, pv_done, ohi_r = (sem(n) for n in ("p_turned", "pt_a", "pt_b", "pv_done", "att_hi"))
        fin_t, fin_c, stored = sem("out_turned"), sem("out_copied"), sem("stored")

        block = ctx.enter_context(nc.Block())

        def freed(r):
            return r - (HEADS - 1)

        def f32(ap):
            return ap.bitcast(F32)

        def second(ap, l):
            return ap.rearrange("p (b two r) -> p b two r", two=2, r=1 << l)[:, :, 1, :]

        def first(ap, l):
            return ap.rearrange("p (b two r) -> p b two r", two=2, r=1 << l)[:, :, 0, :]

        def totals(l, which):
            t = tot[l].rearrange("p (b two) -> p b two", two=2)[:, :, which:which + 1]
            return t.to_broadcast([P, S >> (l + 1), 1 << l])

        @block.sync
        def _(sp):
            sp.dma_start(vec_rows[0:C_B, 0, :], ln_g.rearrange("l c (t p) -> (l c t) p", p=P)
                         ).then_inc(vecs_landed, 16)
            sp.dma_start(vec_rows[C_B:C_KV, 0, :], ln_b.rearrange("l c (t p) -> (l c t) p", p=P)
                         ).then_inc(vecs_landed, 16)
            sp.dma_start(vec_rows[C_KV:C_BQ, 0, :], kv_b.rearrange("(t p) -> t p", p=P)).then_inc(vecs_landed, 16)
            sp.dma_start(vec_rows[C_BQ:C_BO, 0, :], b_q.rearrange("l (t p) -> (l t) p", p=P)
                         ).then_inc(vecs_landed, 16)
            sp.dma_start(vec_rows[C_BO:N_A, 0, :], b_o.rearrange("l (t p) -> (l t) p", p=P)
                         ).then_inc(vecs_landed, 16)
            sp.dma_start(vec_rows[0:C_LB - N_A, 1, :], b_gate.rearrange("l (t p) -> (l t) p", p=P)
                         ).then_inc(vecs_landed, 16)
            sp.dma_start(vec_rows[C_LB - N_A:C_NG - N_A, 1, :], a_lb.rearrange("l (t p) -> (l t) p", p=P)
                         ).then_inc(vecs_landed, 16)
            sp.dma_start(vec_rows[C_NG - N_A:N_ALL - N_A, 1, :], a_gain).then_inc(vecs_landed, 16)
            sp.dma_start(x_rows, x_in.rearrange("b (t p) d -> p (b t) d", p=P)).then_inc(rows_landed, 16)

            def load(r, par, u, src, kt):
                s = 2 * par + u
                if not (isinstance(r, int) and r == 0):
                    sp.wait_ge(w_lo_ready, 4 * r + s - 3)
                sp.dma_start(w_raw[:, s, 0:kt * P].rearrange("p (k n) -> p k n", k=kt), src
                             ).then_inc(w_landed[s], 16)

            def tile_of(w, n, k0, kt):
                return w[k0 * P:(k0 + kt) * P, bass.ds(n, P)].rearrange("(k p) n -> p k n", p=P)

            def square(r, w):
                for i in range(2):
                    for s in range(4):
                        load(r + i, s // 2, s % 2, tile_of(w, (4 * i + s) * P, 0, NT), NT)

            def head_units(h):
                for s in range(4):
                    load(h, s // 2, s % 2, tile_of(a_w_in[0], s * D + h * P, 0, NT), NT)

            head_units(0)
            sp.dma_start(p_rows[:, :, :], p_in[0].rearrange("b (t p) d -> p (b t) d", p=P)).then_inc(p_landed[0], 16)
            sp.dma_start(sink[:, :], sinks[0:1, :].to_broadcast([P, QH])).then_inc(sink_landed, 16)
            with sp.Fori(1, HEADS) as h:
                head_units(h)
            square(R_WO, a_w_out[0])
            for layer in range(LAYERS):
                if layer == 1:
                    for s in range(4):
                        load(R_KV, s // 2, s % 2, tile_of(kv_w, s * P, 0, NT), NT)
                    square(R_Q, w_q[0])
                    square(R_AO, w_o[0])
                    sp.wait_ge(p_lo_ready, PT)
                    sp.dma_start(p_rows[:, :, :], p_in[1].rearrange("b (t p) d -> p (b t) d", p=P)
                                 ).then_inc(p_landed[1], 16)
                j0 = 0
                for part, n in enumerate(PARTS):
                    with sp.Fori(0, n // 2) as i:
                        for s in range(4):
                            col = (s % 2) * F + (j0 + s // 2) * P
                            load(R_GU[layer][part] + i, s // 2, s % 2,
                                 tile_of(w_gu[layer], i * (2 * P) + col, 0, NT), NT)
                    for i in range(2):
                        for s in range(4):
                            load(R_DN[layer][part] + i, s // 2, s % 2,
                                 tile_of(w_dn[layer], (4 * i + s) * P, j0, n), n)
                    j0 += n
                for i in range(2):
                    for s in range(4):
                        n0 = (4 * i + s) * P
                        load(R_PLE[layer] + i, s // 2, s % 2, tile_of(w_gate[layer], n0, 0, NT), NT)
                        sp.dma_start(w_raw[:, s, NT * P:KMAX * P].rearrange("p (k n) -> p k n", k=PT),
                                     tile_of(w_up[layer], n0, 0, PT)).then_inc(up_landed[s], 16)
            for half in range(2):
                for t in range(TT):
                    sp.wait_ge(fin_c, TT * half + t + 1)
                    sp.dma_start(out[0, t * P:(t + 1) * P, half * S:(half + 1) * S],
                                 out_rows[:, t, half * S:(half + 1) * S]).then_inc(stored, 16)
            sp.wait_ge(stored, 16 * 2 * TT)

        @block.gpsimd
        def _(pool):
            pool.memset(ident[:, :], 0.0).then_inc(consts, 1)
            pool.memset(ones_d[:, :], 1.0 / D).then_inc(consts, 1)
            pool.memset(ones_v[:, :], 1.0 / P).then_inc(consts, 1)
            pool.wait_ge(consts, 3)
            pool.affine_select(out=ident[:, :], in_=ident[:, :], compare_op=ALU.not_equal, fill=1.0, base=0,
                               pattern=[[-1, P]], channel_multiplier=1).then_inc(consts, 1)
            pool.memset(eye_m, 0.0).then_inc(masks, 1)
            for l in range(LEVELS):
                pool.memset(lvl_m[l], 1.0).then_inc(masks, 1)
            pool.wait_ge(masks, 1 + LEVELS)
            pool.affine_select(out=eye_m, in_=eye_m, compare_op=ALU.not_equal, fill=1.0, base=0,
                               pattern=[[0, TT], [-1, P]], channel_multiplier=1).then_inc(masks, 1)
            for l in range(LEVELS):
                pool.affine_select(out=lvl_m[l], in_=lvl_m[l], compare_op=ALU.is_ge, fill=0.0, base=0,
                                   pattern=[[0, TT], [-(2 << l), 64 >> l], [0, 1 << l]],
                                   channel_multiplier=1).then_inc(masks, 1)
            pool.wait_ge(masks, 2 + 2 * LEVELS)
            for l in range(LEVELS):
                pool.affine_select(out=lvl_m[l], in_=lvl_m[l], compare_op=ALU.is_ge, fill=0.0,
                                   base=(1 << l) - 1, pattern=[[0, TT], [2 << l, 64 >> l], [0, 1 << l]],
                                   channel_multiplier=-1).then_inc(masks, 1)

            def head(h):
                pool.wait_ge(k_r, h + 1)
                if not isinstance(h, int):
                    pool.wait_ge(pe_kt, h)
                    pool.wait_ge(st_r, 3 * h)
                for l in range(LEVELS):
                    if l == 0:
                        pool.wait_ge(f_r, h + 1)
                    else:
                        pool.wait_ge(tot_r, LEVELS * h + l)
                    pair = tot[l].rearrange("p (b two) -> p b two", two=2)
                    pool.tensor_tensor(tot[l + 1], pair[:, :, 0], pair[:, :, 1], ALU.mult).then_inc(tot_r, 1)
                    if l == 0:
                        pool.tensor_copy(k_dec, k_raw).then_inc(kd0_r, 1)

            head(0)
            with pool.Fori(1, HEADS) as h:
                head(h)

            def centre(n):
                pool.wait_ge(mean_r, n + 1)
                for k in range(NT):
                    pool.tensor_tensor(x[:, k, :], x[:, k, :], mean, ALU.subtract).then_inc(cen_r, 1)

            for n in range(3 * LAYERS):
                centre(n)
                if n == 0:
                    pool.wait_ge(x_ready, 2 * NT)
                    pool.memset(k_pad[:, :, 0:WIN], 0.0).then_inc(far_ready, 1)
                    d = dist.rearrange("p (b s) -> p b s", b=TT)
                    pool.iota(dist, pattern=[[0, TT], [-1, 2 * WIN]], base=WIN, channel_multiplier=1,
                              allow_small_or_imprecise_dtypes=True).then_inc(far_ready, 1)
                    pool.wait_ge(far_ready, 2)
                    pool.affine_select(out=dist, in_=dist, compare_op=ALU.is_ge, fill=FAR, base=WIN,
                                       pattern=[[0, TT], [-1, 2 * WIN]], channel_multiplier=1
                                       ).then_inc(far_ready, 1)
                    pool.wait_ge(far_ready, 3)
                    pool.affine_select(out=dist, in_=dist, compare_op=ALU.is_ge, fill=FAR, base=-1,
                                       pattern=[[0, TT], [1, 2 * WIN]], channel_multiplier=-1
                                       ).then_inc(far_ready, 1)
                    pool.wait_ge(far_ready, 4)
                    pool.memset(d[:, 0, 0:WIN], FAR).then_inc(far_ready, 1)

        @block.scalar
        def _(act):
            def split_hi(r, par, kt):
                for u in range(2):
                    s = 2 * par + u
                    act.wait_ge(w_landed[s], 16 * (r + 1))
                    if kt > NT:
                        layer = R_PLE.index(r if r in R_PLE else r - 1)
                        act.wait_ge(up_landed[s], 16 * (2 * layer + r - R_PLE[layer] + 1))
                    if not (isinstance(r, int) and r == 0):
                        act.wait_ge(unit_done, 4 * r + 2 * par - 2)
                    act.activation(w_hi[:, s, 0:kt * P], w_raw[:, s, 0:kt * P], ACT.Copy).then_inc(w_hi_ready, 1)

            split_hi(0, 0, NT)
            act.wait_ge(lb_ready, 1)
            act.activation(lbs[:, 0, :], lbs[:, 2, :], ACT.Sigmoid).then_inc(lb_ready, 1)
            for k in range(NT):
                act.wait_ge(x_f32, k + 1)
                act.activation(x_hi[:, k, :], x[:, k, :], ACT.Copy).then_inc(x_hi_ready, 1)

            def embedding_hi(layer):
                for k in range(PT):
                    act.wait_ge(turned, 1 + NT + PT * layer + k + 1)
                    act.activation(pe_hi[:, k, :], bank[:, 4 + k, :], ACT.Copy).then_inc(p_hi_ready, 1)

            embedding_hi(0)

            def project(i):
                act.wait_ge(unit_done, 4 * i + 2)
                act.activation(s_q, bank[:, 0, :], ACT.Sigmoid).then_inc(sq_r, 1)
                act.activation(s_f, bank[:, 1, :], ACT.Sigmoid).then_inc(sf_r, 1)
                act.activation(s_n, bank[:, 1, :], ACT.Sigmoid, scale=-1.0).then_inc(sn_r, 1)

            def project_vg(i):
                act.wait_ge(unit_done, 4 * i + 4)
                act.activation(v_t, bank[:, 2, :], ACT.Copy).then_inc(vt_r, 1)
                act.activation(s_g, bank[:, 3, :], ACT.Sigmoid).then_inc(sg_r, 1)

            def keys(h):
                act.wait_ge(pe_kt, h + 1)
                act.activation(kd_row[:, :, :], bank[:, 6, 0:3 * P].rearrange("p (c k) -> p c k", c=3), ACT.Copy
                               ).then_inc(kt_r, 1)

            def readout(h):
                act.wait_ge(pe_o, h + 1)
                act.activation(o_sq, bank[:, 6, :], ACT.Square).then_inc(osq_r, 1)
                act.wait_ge(pe_ms, h + 1)
                act.activation(o_rms, bank[:, 7, :], ACT.Sqrt, bias=eps_rms).then_inc(rms_r, 1)
                act.wait_ge(og_r, h + 1)
                act.activation(mid_hi[:, bass.ds(h, 1), :].rearrange("p a s -> p (a s)"), o_g, ACT.Copy
                               ).then_inc(oh_r, 1)

            eps_rms = vec[:, N_ALL:N_ALL + 1]

            split_hi(0, 1, NT)
            split_hi(1, 0, NT)
            project(0)
            project_vg(0)
            with act.Fori(1, HEADS) as i:
                split_hi(i, 1, NT)
                split_hi(i + 1, 0, NT)
                act.wait_ge(q_r, i)
                act.wait_ge(k_r, i)
                project(i)
                keys(i - 1)
                readout(i - 1)
                act.wait_ge(pe_vtr, i)
                act.wait_ge(g_r, i)
                project_vg(i)
            keys(HEADS - 1)
            readout(HEADS - 1)

            def squares(n, r, par):
                pp = 2 * r + par
                for u in range(2):
                    j = 2 * pp + u
                    act.wait_ge(y_r, NT * n + j + 1)
                    if pp:
                        act.wait_ge(sumsq_r, 7 * n + (1 if pp == 1 else 2 * pp - 1) - (1 - u if pp > 1 else 0))
                    act.activation(sq[u], x[:, j, :], ACT.Square).then_inc(sq_done, 1)

            def norm(n):
                act.wait_ge(mean_r, n + 1)
                act.activation(mean_sq, mean, ACT.Square).then_inc(msq_r, 1)
                act.wait_ge(var_r, 2 * n + 2)
                act.activation(rstd, var, ACT.Sqrt).then_inc(std_r, 1)
                for k in range(NT):
                    c = NT * n + k
                    act.wait_ge(nrm_r, c + 1)
                    act.activation(x[:, k, :], x[:, k, :], ACT.Identity, scale=vec[:, C_G + c:C_G + c + 1],
                                   bias=vec[:, C_B + c:C_B + c + 1]).then_inc(x_f32, 1)
                    if n < 3 * LAYERS - 1:
                        act.wait_ge(x_f32, NT * (n + 1) + k + 1)
                        act.activation(x_hi[:, k, :], x[:, k, :], ACT.Copy).then_inc(x_hi_ready, 1)

            def rounds(r0, n, kt, next_kt, take):
                for i in range(n):
                    split_hi(r0 + i, 1, kt)
                    take(i, 0)
                    if next_kt is not None or i < n - 1:
                        split_hi(r0 + i + 1, 0, kt if i < n - 1 else next_kt)
                    take(i, 1)

            def hidden(layer, part, i, par):
                r = R_GU[layer][part] + i
                n = sum(PARTS[:part]) + 2 * i + par
                act.wait_ge(unit_done, 4 * r + 2 * par + 2)
                act.activation(act_t[par], bank[:, 2 * par, :], ACT.Silu).then_inc(silu_r[layer], 1)
                act.wait_ge(bank_free[par], freed(r + 1))
                act.activation(mid_hi[:, bass.ds(2 * i + par, 1), :].rearrange("p a s -> p (a s)"), hid[par],
                               ACT.Copy).then_inc(hhi_r[layer], 1)

            def gate(layer, i, par):
                r = R_PLE[layer] + i
                act.wait_ge(unit_done, 4 * r + 2 * par + 2)
                if i or par:
                    act.wait_ge(bank_free[1 - par], freed(r + par))
                for u in range(2):
                    c = C_PG + NT * layer + 4 * i + 2 * par + u
                    act.activation(act_t[u], bank[:, 2 * par + u, :], ACT.Sigmoid, bias=vec[:, c:c + 1]
                                   ).then_inc(gate_r, 1)

            rounds(R_WO, 2, NT, NT, lambda i, par: squares(0, i, par))
            norm(0)
            for layer in range(LAYERS):
                if layer == 1:
                    split_hi(R_KV, 1, NT)
                    act.wait_ge(unit_done, 4 * R_KV + 2)
                    act.wait_ge(far_ready, 1)
                    for u in range(2):
                        for half in range(2):
                            at_ = slice(HD * half, HD * half + HD)
                            ins = act.activation(k_pad[at_, 2 * u + half, WIN:], bank[at_, u, :], ACT.Identity,
                                                 bias=vec[at_, C_KV + u:C_KV + u + 1])
                            ins.then_inc(bank_free[0] if u and half else k_w, 1)
                    split_hi(R_Q, 0, NT)
                    act.wait_ge(unit_done, 4 * R_KV + 4)
                    for u in range(2):
                        act.activation(v_cols[:, u, :], bank[:, 2 + u, :], ACT.Identity,
                                       bias=vec[:, C_KV + 2 + u:C_KV + 3 + u]
                                       ).then_inc(bank_free[1] if u else v_w, 1)
                    for n in range(QH + 3):
                        if n % G == 0 and n < QH:
                            g = n // G + 1
                            split_hi(R_Q + g // 2, g % 2, NT)
                        if 2 <= n < QH + 2:
                            act.wait_ge(t_done, n - 1)
                            if n > 2:
                                act.wait_ge(pv_done, n - 2)
                            act.activation(p_t[:, 0:2, :, :].rearrange("p b h t -> p (b h t)"), bank[:, 4, :],
                                           ACT.Copy).then_inc(pta_r, 1)
                        if n < QH:
                            b = n % 2
                            act.wait_ge(nmx_r, n + 1)
                            act.activation(stat[:, b, 3, :], stat[:, b, 1, :], ACT.Exp, bias=sink[:, n:n + 1])
                            for blk in range(TT):
                                ins = act.activation(scores[b][:, blk, :], scores[b][:, blk, :], ACT.Exp,
                                                     bias=stat[:, b, 1, blk:blk + 1],
                                                     accum_out=stat[:, b, 2, blk:blk + 1])
                            ins.then_inc(exp_r, 1)
                        if n >= 3 and (n - 3) % 2 == 1:
                            t = (n - 3) // 2
                            act.wait_ge(pv_done, 2 * t + 2)
                            act.activation(mid_hi[:, t, :], bank[:, 6 + t % 2, :], ACT.Copy).then_inc(ohi_r, 1)
                    def project_out(i, par):
                        r = R_AO + i
                        act.wait_ge(unit_done, 4 * r + 2 * par + 2)
                        for u in range(2):
                            j = 4 * i + 2 * par + u
                            if i or par:
                                act.wait_ge(y_r, NT * 3 + j - 1)
                            act.activation(act_t[u], bank[:, 2 * par + u, :], ACT.Identity,
                                           bias=vec[:, C_BO + j:C_BO + j + 1]).then_inc(biased, 1)
                        squares(3, i, par)
                    rounds(R_AO, 2, NT, NT, project_out)
                    norm(3)
                    embedding_hi(1)
                for part, n in enumerate(PARTS):
                    r = R_GU[layer][part]

                    def gate_up(i, next_kt):
                        split_hi(r + i, 1, NT)
                        hidden(layer, part, i, 0)
                        split_hi(r + i + 1, 0, next_kt)
                        hidden(layer, part, i, 1)
                    with act.Fori(0, n // 2 - 1) as i:
                        gate_up(i, NT)
                    gate_up(n // 2 - 1, n)
                    last = part == len(PARTS) - 1
                    rounds(R_DN[layer][part], 2, n, KMAX if last else NT,
                           lambda i, par: squares(3 * layer + 1, i, par) if last else None)
                norm(3 * layer + 1)
                def embed(i, par):
                    gate(layer, i, par)
                    squares(3 * layer + 2, i, par)
                rounds(R_PLE[layer], 2, KMAX, NT if layer == 0 else None, embed)
                norm(3 * layer + 2)

        @block.vector
        def _(dve):
            def split_lo(r, par, kt):
                for u in range(2):
                    s = 2 * par + u
                    dve.wait_ge(w_hi_ready, 4 * r + s + 1)
                    dve.tensor_tensor(w_lo[:, s, 0:kt * P], w_raw[:, s, 0:kt * P], f32(w_hi[:, s, 0:kt * P]),
                                      ALU.subtract).then_inc(w_lo_ready, 1)

            dve.memset(vec[:, N_ALL:N_ALL + 1], 1e-6)
            dve.wait_ge(turned, 1)
            dve.tensor_copy(vec[:, 0:N_A], bank[:, 4, 0:N_A])
            dve.tensor_copy(vec[:, N_A:N_ALL], bank[:, 4, P:P + N_ALL - N_A]).then_inc(turn_read, 1)
            dve.wait_ge(turn_read, 1)
            dve.tensor_tensor(lbs[:, 2, :], vec[:, C_LB:C_LB + NT], vec[:, C_LB + NT:C_LB + 2 * NT], ALU.subtract
                              ).then_inc(lb_ready, 1)
            for k in range(NT):
                dve.wait_ge(turned, 2 + k)
                dve.tensor_copy(x[:, k, :], bank[:, 4 + (k + 1) % 4, :]).then_inc(x_f32, 1)
                dve.wait_ge(x_hi_ready, k + 1)
                dve.tensor_tensor(x_lo[:, k, :], x[:, k, :], f32(x_hi[:, k, :]), ALU.subtract).then_inc(x_ready, 1)
            split_lo(0, 0, NT)
            dve.wait_ge(lb_ready, 2)
            dve.tensor_scalar(lbs[:, 1, :], lbs[:, 0, :], -1.0, 1.0, ALU.mult, ALU.add).then_inc(lb_ready, 1)

            def embedding_lo(layer):
                for k in range(PT):
                    dve.wait_ge(p_hi_ready, PT * layer + k + 1)
                    dve.tensor_tensor(pe_lo[:, k, :], bank[:, 4 + k, :], f32(pe_hi[:, k, :]), ALU.subtract
                                      ).then_inc(p_lo_ready, 1)

            embedding_lo(0)
            dve.memset(a_mat, 0.0).then_inc(a_r, 1)
            dve.wait_ge(lb_ready, 3)

            def project(i):
                dve.wait_ge(sq_r, i + 1)
                dve.scalar_tensor_tensor(q_t, bank[:, 0, :], QSCALE, s_q, ALU.mult, ALU.mult).then_inc(q_r, 1)
                dve.wait_ge(sf_r, i + 1)
                dve.tensor_scalar(f_t, s_f, lbs[:, 1, bass.ds(i, 1)], lbs[:, 0, bass.ds(i, 1)], ALU.mult, ALU.add
                                  ).then_inc(f_r, 1)
                dve.wait_ge(sn_r, i + 1)
                dve.tensor_scalar(k_raw, s_n, lbs[:, 1, bass.ds(i, 1)], None, ALU.mult).then_inc(k_r, 1)

            def project_vg(i):
                dve.wait_ge(sg_r, i + 1)
                dve.tensor_tensor(g_t, bank[:, 3, :], s_g, ALU.mult).then_inc(g_r, 1)
                dve.wait_ge(q_r, i + 1)
                dve.wait_ge(f_r, i + 1)
                dve.tensor_tensor(q_dec, q_t, f_t, ALU.mult).then_inc(qd_r, 1)

            def scores_of(h):
                dve.wait_ge(pe_diag, h + 1)
                dve.tensor_copy(v_row[:, :, :].rearrange("p c v -> p (c v)"), bank[:, 6, :]).then_inc(vrow_r, 1)
                dve.copy_predicated(a_mat, eye_m.bitcast(U16), bank[:, 7, :]).then_inc(a_r, 1)
                dve.wait_ge(kd0_r, h + 1)
                for l in range(LEVELS):
                    dve.wait_ge(pe_lvl, LEVELS * h + l + 1)
                    dve.wait_ge(a_r, (LEVELS + 1) * h + l + 2)
                    if l:
                        dve.wait_ge(tot_r, LEVELS * h + l)
                        dve.wait_ge(kd_r, LEVELS * h + l)
                    dve.wait_ge(qd_r, (LEVELS + 1) * h + l + 1)
                    dve.tensor_tensor(second(q_dec, l), second(q_dec, l), totals(l, 0), ALU.mult).then_inc(qd_r, 1)
                    dve.tensor_tensor(first(k_dec, l), first(k_dec, l), totals(l, 1), ALU.mult).then_inc(kd_r, 1)
                    shape = "p (b r) -> p b r"
                    dve.copy_predicated(second(a_mat, l), lvl_m[l].bitcast(U16).rearrange(shape, r=1 << l),
                                        bank[:, 4 + l % 2, 0:S // 2].rearrange(shape, r=1 << l)).then_inc(a_r, 1)

            def states(h):
                dve.wait_ge(pe_ds, h + 1)
                dve.wait_ge(tot_r, LEVELS * h + LEVELS)
                term = bank[:, 7, 0:3 * P].rearrange("p (c v) -> p c v", c=3)
                dve.tensor_copy(state[:, 0, :], term[:, 0, :]).then_inc(st_r, 1)
                for c in (1, 2):
                    dve.wait_ge(st_r, 3 * h + c)
                    dve.scalar_tensor_tensor(state[:, c, :], state[:, c - 1, :], tot[LEVELS][:, c:c + 1],
                                             term[:, c, :], ALU.mult, ALU.add).then_inc(st_r, 1)

            def readout(h):
                dve.wait_ge(rms_r, h + 1)
                dve.reciprocal(o_inv, o_rms).then_inc(oinv_r, 1)
                dve.wait_ge(oinv_r, h + 1)
                dve.tensor_tensor(o_n, bank[:, 6, :], o_inv, ALU.mult).then_inc(on_r, 1)
                dve.wait_ge(on_r, h + 1)
                dve.scalar_tensor_tensor(o_g, o_n, vec[:, C_NG:C_NG + 1], g_t, ALU.mult, ALU.mult
                                         ).then_inc(og_r, 1)
                dve.wait_ge(oh_r, h + 1)
                at_ = bass.ds(h, 1)
                dve.tensor_tensor(mid_lo[:, at_, :].rearrange("p a s -> p (a s)"), o_g,
                                  f32(mid_hi[:, at_, :]).rearrange("p a s -> p (a s)"), ALU.subtract
                                  ).then_inc(mid_ready, 1)

            split_lo(0, 1, NT)
            dve.wait_ge(masks, 2 + 3 * LEVELS)
            split_lo(1, 0, NT)
            project(0)
            project_vg(0)
            with dve.Fori(1, HEADS) as i:
                split_lo(i, 1, NT)
                scores_of(i - 1)
                split_lo(i + 1, 0, NT)
                dve.wait_ge(pe_diag, i)
                project(i)
                states(i - 1)
                readout(i - 1)
                project_vg(i)
            dve.wait_ge(k_r, HEADS)
            dve.engine_nop().then_inc(bank_free[0], 1)
            dve.wait_ge(g_r, HEADS)
            dve.engine_nop().then_inc(bank_free[1], 1)
            scores_of(HEADS - 1)
            states(HEADS - 1)
            readout(HEADS - 1)

            def sums(n, i, par):
                pp = 2 * i + par
                j = 2 * pp
                dve.wait_ge(y_r, NT * n + j + 2)
                if pp == 0:
                    dve.tensor_tensor(sum_y, x[:, 0, :], x[:, 1, :], ALU.add).then_inc(sumy_r, 1)
                    dve.wait_ge(sq_done, NT * n + 2)
                    dve.tensor_tensor(sum_sq, sq[0], sq[1], ALU.add).then_inc(sumsq_r, 1)
                else:
                    for u in range(2):
                        dve.wait_ge(sumy_r, 7 * n + 2 * pp - 1 + u)
                        dve.tensor_tensor(sum_y, sum_y, x[:, j + u, :], ALU.add).then_inc(sumy_r, 1)
                    for u in range(2):
                        dve.wait_ge(sq_done, NT * n + j + u + 1)
                        dve.wait_ge(sumsq_r, 7 * n + 2 * pp - 1 + u)
                        dve.tensor_tensor(sum_sq, sum_sq, sq[u], ALU.add).then_inc(sumsq_r, 1)

            def free_bank(par):
                dve.engine_nop().then_inc(bank_free[par], 1)

            def norm(n):
                dve.wait_ge(stat_mm, 2 * n + 1)
                dve.tensor_copy(mean, bank[:, 6, :]).then_inc(mean_r, 1)
                dve.wait_ge(stat_mm, 2 * n + 2)
                dve.wait_ge(msq_r, n + 1)
                dve.tensor_tensor(var, bank[:, 7, :], mean_sq, ALU.subtract).then_inc(var_r, 1)
                dve.wait_ge(var_r, 2 * n + 1)
                dve.tensor_scalar(var, var, 0.0, 1e-5, ALU.max, ALU.add).then_inc(var_r, 1)
                dve.wait_ge(std_r, n + 1)
                dve.reciprocal(rstd, rstd).then_inc(rstd_r, 1)
                dve.wait_ge(rstd_r, n + 1)

                def low(k):
                    dve.wait_ge(x_hi_ready, NT * (n + 1) + k + 1)
                    dve.tensor_tensor(x_lo[:, k, :], x[:, k, :], f32(x_hi[:, k, :]), ALU.subtract
                                      ).then_inc(x_ready, 1)
                for k in range(NT):
                    dve.wait_ge(cen_r, NT * n + k + 1)
                    dve.tensor_tensor(x[:, k, :], x[:, k, :], rstd, ALU.mult).then_inc(nrm_r, 1)
                    if n < 3 * LAYERS - 1 and k:
                        low(k - 1)
                if n < 3 * LAYERS - 1:
                    low(NT - 1)

            def rounds(r0, n, kt, next_kt, take):
                for i in range(n):
                    split_lo(r0 + i, 1, kt)
                    take(i, 0)
                    if next_kt is not None or i < n - 1:
                        split_lo(r0 + i + 1, 0, kt if i < n - 1 else next_kt)
                    take(i, 1)

            def add_to_stream(n, r0, scale, final):
                def take(i, par):
                    r = r0 + i
                    for u in range(2):
                        j = 4 * i + 2 * par + u
                        dve.wait_ge(unit_done, 4 * r + 2 * par + 2)
                        ins = dve.scalar_tensor_tensor(x[:, j, :], x[:, j, :], scale, bank[:, 2 * par + u, :],
                                                       ALU.mult, ALU.add)
                        if final:
                            ins.then_inc(y_r, 1)
                    if final:
                        dve.wait_ge(y_r, NT * n + 4 * i + 2 * par + 2)
                        free_bank(par)
                        sums(n, i, par)
                    else:
                        ins.then_inc(bank_free[par], 1)
                return take

            def hidden(layer, part, i, par):
                r = R_GU[layer][part] + i
                n = sum(PARTS[:part]) + 2 * i + par
                dve.wait_ge(silu_r[layer], n + 1)
                dve.tensor_tensor(hid[par], bank[:, 2 * par + 1, :], act_t[par], ALU.mult
                                  ).then_inc(bank_free[par], 1)
                dve.wait_ge(hhi_r[layer], n + 1)
                at_ = bass.ds(2 * i + par, 1)
                dve.tensor_tensor(mid_lo[:, at_, :].rearrange("p a s -> p (a s)"), hid[par],
                                  f32(mid_hi[:, at_, :]).rearrange("p a s -> p (a s)"), ALU.subtract
                                  ).then_inc(mid_ready, 1)

            rounds(R_WO, 2, NT, NT, add_to_stream(0, R_WO, ALPHA, True))
            norm(0)
            for layer in range(LAYERS):
                if layer == 1:
                    split_lo(R_KV, 1, NT)
                    dve.wait_ge(k_w, 3)
                    dve.wait_ge(bank_free[0], freed(R_KV + 1))
                    for kvh in range(KVH):
                        own, other = HD * (kvh % 2), HD * (1 - kvh % 2)
                        dve.tensor_copy(k_pad[other:other + HD, kvh, WIN:], k_pad[own:own + HD, kvh, WIN:]
                                        ).then_inc(k_ok, 1)
                    split_lo(R_Q, 0, NT)
                    dve.wait_ge(v_turn, 1)
                    for u in range(2):
                        dve.tensor_copy(v_all[:, 2 * u:2 * u + 2, :].rearrange("p b v -> p (b v)"),
                                        bank[:, 4 + u, :]).then_inc(v_ok, 1)
                    dve.wait_ge(far_ready, 5)
                    dve.wait_ge(sink_landed, 16)
                    for n in range(QH + 3):
                        b = n % 2
                        if n % G == 0 and n < QH:
                            g = n // G + 1
                            split_lo(R_Q + g // 2, g % 2, NT)
                            g -= 1
                            par = g % 2
                            dve.wait_ge(unit_done, 4 * R_Q + 2 * g + 2)
                            for u in range(2):
                                ins = dve.tensor_scalar(q_s[par][:, u, :], bank[:, 2 * par + u, :],
                                                        vec[:, C_BQ + 2 * g + u:C_BQ + 2 * g + u + 1], ASCALE,
                                                        ALU.add, ALU.mult)
                            ins.then_inc(bank_free[par], 1)
                        if n < QH:
                            slope = 2.0 ** (-8.0 * (n + 1) / QH)
                            dve.wait_ge(s_done, n + 1)
                            if n >= 2:
                                dve.wait_ge(t_done, n - 1)
                            dve.scalar_tensor_tensor(scores[b].rearrange("p b s -> p (b s)"), dist, -slope,
                                                     bank[:, 2 * b:2 * b + 2, :].rearrange("p a s -> p (a s)"),
                                                     ALU.mult, ALU.add).then_inc(sc_r, 1)
                            dve.wait_ge(sc_r, n + 1)
                            dve.tensor_reduce(stat[:, b, 0, :], scores[b], AX_X, ALU.max).then_inc(mx_r, 1)
                            dve.wait_ge(mx_r, n + 1)
                            dve.tensor_scalar(stat[:, b, 1, :], stat[:, b, 0, :], sink[:, n:n + 1], -1.0,
                                              ALU.max, ALU.mult).then_inc(nmx_r, 1)
                        if 2 <= n < QH + 2:
                            dve.wait_ge(t_done, n - 1)
                            if n > 2:
                                dve.wait_ge(pv_done, n - 2)
                            dve.tensor_copy(p_t[:, 2:4, :, :].rearrange("p b h t -> p (b h t)"), bank[:, 5, :]
                                            ).then_inc(ptb_r, 1)
                        if 1 <= n <= QH:
                            m, c = n - 1, (n - 1) % 2
                            dve.wait_ge(exp_r, m + 1)
                            dve.tensor_tensor(stat[:, c, 3, :], stat[:, c, 3, :], stat[:, c, 2, :], ALU.add
                                              ).then_inc(den_r, 1)
                            dve.wait_ge(den_r, m + 1)
                            dve.reciprocal(stat[:, c, 4, :], stat[:, c, 3, :]).then_inc(rden_r, 1)
                            dve.wait_ge(rden_r, m + 1)
                            for blk in range(TT):
                                ins = dve.tensor_scalar(scores[c][:, blk, :], scores[c][:, blk, :],
                                                        stat[:, c, 4, blk:blk + 1], None, ALU.mult)
                            ins.then_inc(p_r, 1)
                        if n >= 3 and (n - 3) % 2 == 1:
                            t = (n - 3) // 2
                            dve.wait_ge(ohi_r, t + 1)
                            dve.tensor_tensor(mid_lo[:, t, :], bank[:, 6 + t % 2, :], f32(mid_hi[:, t, :]),
                                              ALU.subtract).then_inc(mid_ready, 1)

                    def project_out(i, par):
                        for u in range(2):
                            j = 4 * i + 2 * par + u
                            dve.wait_ge(biased, j + 1)
                            dve.scalar_tensor_tensor(x[:, j, :], x[:, j, :], ALPHA, act_t[u], ALU.mult, ALU.add
                                                     ).then_inc(y_r, 1)
                        free_bank(par)
                        sums(3, i, par)
                    rounds(R_AO, 2, NT, NT, project_out)
                    norm(3)
                    embedding_lo(1)
                for part, n in enumerate(PARTS):
                    r = R_GU[layer][part]

                    def gate_up(i, next_kt):
                        split_lo(r + i, 1, NT)
                        hidden(layer, part, i, 0)
                        split_lo(r + i + 1, 0, next_kt)
                        hidden(layer, part, i, 1)
                    with dve.Fori(0, n // 2 - 1) as i:
                        gate_up(i, NT)
                    gate_up(n // 2 - 1, n)
                    last = part == len(PARTS) - 1
                    rounds(R_DN[layer][part], 2, n, KMAX if last else NT,
                           add_to_stream(3 * layer + 1, R_DN[layer][part], ALPHA if part == 0 else 1.0, last))
                norm(3 * layer + 1)

                def embed(i, par):
                    for u in range(2):
                        j = 4 * i + 2 * par + u
                        dve.wait_ge(gate_r, NT * layer + j + 1)
                        ins = dve.tensor_tensor(hid[u], bank[:, 4 + u, :], act_t[u], ALU.mult)
                    ins.then_inc(bank_free[par], 1)
                    dve.wait_ge(bank_free[par], freed(R_PLE[layer] + i + 1))
                    for u in range(2):
                        j = 4 * i + 2 * par + u
                        dve.scalar_tensor_tensor(x[:, j, :], x[:, j, :], ALPHA, hid[u], ALU.mult, ALU.add
                                                 ).then_inc(y_r, 1)
                    sums(3 * layer + 2, i, par)
                rounds(R_PLE[layer], 2, KMAX, NT if layer == 0 else None, embed)
                norm(3 * layer + 2)
            for half in range(2):
                for t in range(TT):
                    dve.wait_ge(fin_t, half + 1)
                    dve.tensor_copy(out_rows[:, t, half * S:(half + 1) * S], bank[:, 4 * half + t, :]
                                    ).then_inc(fin_c, 1)

        @block.tensor
        def _(pe):
            def product(to, s, k, hi, lo, start, stop):
                cols = slice(k * P, (k + 1) * P)
                pe.matmul(to, w_hi[:, s, cols], hi, start=start, stop=False)
                pe.matmul(to, w_hi[:, s, cols], lo, start=False, stop=False)
                return pe.matmul(to, w_lo[:, s, cols], hi, start=False, stop=stop)

            def pair(r, par, kt, hi, lo, ready, base, also=None, taken=None):
                if taken is not None:
                    pe.wait_ge(taken, r)
                elif not isinstance(r, int) or r > 0:
                    pe.wait_ge(bank_free[par], freed(r))
                for k in range(kt):
                    pe.wait_ge(ready, base + k + 1)
                    for u in range(2):
                        s = 2 * par + u
                        if k == 0:
                            pe.wait_ge(w_lo_ready, 4 * r + s + 1)
                        ins = product(bank[:, s, :], s, k, hi[:, k, :], lo[:, k, :], k == 0, k == kt - 1)
                        if k == kt - 1:
                            ins.then_inc(unit_done, 1)
                    if also is not None:
                        also(k)

            pe.wait_ge(consts, 4)
            pe.wait_ge(vecs_landed, 16 * 8)
            pe.transpose(bank[:, 4, 0:N_A], vec_rows[0:N_A, 0, :], ident[0:N_A, 0:N_A])
            pe.transpose(bank[:, 4, P:P + N_ALL - N_A], vec_rows[0:N_ALL - N_A, 1, :],
                         ident[0:N_ALL - N_A, 0:N_ALL - N_A]).then_inc(turned, 1)
            pe.wait_ge(rows_landed, 16)
            for k in range(NT):
                if k == 3:
                    pe.wait_ge(turn_read, 1)
                if k >= 4:
                    pe.wait_ge(x_f32, k - 3)
                for t in range(TT):
                    ins = pe.transpose(bank[:, 4 + (k + 1) % 4, t * P:(t + 1) * P],
                                       x_rows[:, t, k * P:(k + 1) * P], ident[:, :])
                ins.then_inc(turned, 1)

            def turn_embedding(layer):
                pe.wait_ge(p_landed[layer], 16)
                for k in range(PT):
                    for t in range(TT):
                        ins = pe.transpose(bank[:, 4 + k, t * P:(t + 1) * P], p_rows[:, t, k * P:(k + 1) * P],
                                           ident[:, :])
                    ins.then_inc(turned, 1)

            pe.wait_ge(x_f32, NT)
            turn_embedding(0)
            pe.wait_ge(p_lo_ready, PT)

            def recur(h, step):
                if step == 0:
                    pe.wait_ge(vt_r, h + 1)
                    pe.wait_ge(g_r, h + 1)
                    for c in range(TT):
                        ins = pe.transpose(bank[:, 6, c * P:(c + 1) * P], v_t[:, c * P:(c + 1) * P], ident[:, :])
                    ins.then_inc(pe_vtr, 1)
                    pe.wait_ge(k_r, h + 1)
                    pe.wait_ge(q_r, h + 1)
                    for c in range(TT):
                        at_ = slice(c * P, (c + 1) * P)
                        ins = pe.matmul(bank[:, 7, at_], k_raw[:, at_], q_t[:, at_], start=True, stop=True)
                    ins.then_inc(pe_diag, 1)
                elif step <= LEVELS:
                    l = step - 1
                    pe.wait_ge(qd_r, (LEVELS + 1) * h + l + 1)
                    if l == 0:
                        pe.wait_ge(kd0_r, h + 1)
                    else:
                        pe.wait_ge(kd_r, LEVELS * h + l)
                    pe.wait_ge(a_r, (LEVELS + 1) * h + (l + 1 if l >= 2 else 1))
                    for c in range(TT):
                        at_ = slice(c * P, (c + 1) * P)
                        ins = pe.matmul(bank[:, 4 + l % 2, c * 64:(c + 1) * 64].rearrange(
                            "p (b r) -> p b r", r=1 << l), k_dec[:, at_], second(q_dec[:, at_], l),
                            start=True, stop=True)
                    ins.then_inc(pe_lvl, 1)
                elif step == LEVELS + 1:
                    pe.wait_ge(kd_r, LEVELS * h + LEVELS)
                    pe.wait_ge(vrow_r, h + 1)
                    for c in range(3):
                        ins = pe.transpose(bank[:, 6, c * P:(c + 1) * P], k_dec[:, c * P:(c + 1) * P], ident[:, :])
                    ins.then_inc(pe_kt, 1)
                elif step == LEVELS + 3:
                    pe.wait_ge(kt_r, h + 1)
                    pe.wait_ge(a_r, (LEVELS + 1) * h + 2)
                    for c in range(3):
                        ins = pe.matmul(bank[:, 7, c * P:(c + 1) * P], kd_row[:, c, :], v_row[:, c, :],
                                        start=True, stop=True)
                    ins.then_inc(pe_ds, 1)
                elif step == LEVELS + 5:
                    pe.wait_ge(a_r, (LEVELS + 1) * (h + 1) + 1)
                    pe.wait_ge(qd_r, (LEVELS + 1) * (h + 1))
                    pe.wait_ge(st_r, 3 * h + 3)
                    for c in range(TT):
                        at_ = slice(c * P, (c + 1) * P)
                        ins = pe.matmul(bank[:, 6, at_], v_row[:, c, :], a_mat[:, at_], start=True, stop=c == 0)
                        if c:
                            ins = pe.matmul(bank[:, 6, at_], state[:, c - 1, :], q_dec[:, at_],
                                            start=False, stop=True)
                    ins.then_inc(pe_o, 1)
                elif step == LEVELS + 7:
                    pe.wait_ge(osq_r, h + 1)
                    pe.matmul(bank[:, 7, :], ones_v[:, :], o_sq, start=True, stop=True).then_inc(pe_ms, 1)

            STEPS = LEVELS + 8
            pair(0, 0, NT, x_hi, x_lo, x_ready, 0)
            pair(0, 1, NT, x_hi, x_lo, x_ready, 0)
            with pe.Fori(1, HEADS) as i:
                h = i - 1
                pair(i, 0, NT, x_hi, x_lo, x_ready, 0, lambda k: recur(h, k), k_r)
                pair(i, 1, NT, x_hi, x_lo, x_ready, 0, lambda k: recur(h, NT + k), g_r)
            for step in range(STEPS):
                recur(HEADS - 1, step)

            def statistics(n):
                pe.wait_ge(sumy_r, 7 * n + 7)
                pe.matmul(bank[:, 6, :], ones_d[:, :], sum_y, start=True, stop=True).then_inc(stat_mm, 1)
                pe.wait_ge(sumsq_r, 7 * n + 7)
                pe.matmul(bank[:, 7, :], ones_d[:, :], sum_sq, start=True, stop=True).then_inc(stat_mm, 1)

            def rounds(r0, n, kt, hi, lo, ready, base):
                with pe.Fori(r0, r0 + n) as r:
                    pair(r, 0, kt, hi, lo, ready, base)
                    pair(r, 1, kt, hi, lo, ready, base)

            rounds(R_WO, 2, NT, mid_hi, mid_lo, mid_ready, M_HG)
            statistics(0)
            for layer in range(LAYERS):
                X = NT * (3 * layer + 1)
                if layer == 1:
                    pair(R_KV, 0, NT, x_hi, x_lo, x_ready, NT * 3)
                    pair(R_KV, 1, NT, x_hi, x_lo, x_ready, NT * 3)
                    pe.wait_ge(v_w, 1)
                    pe.wait_ge(bank_free[1], freed(R_KV + 1))
                    for blk in range(TT):
                        for u in range(2):
                            at_ = (blk % 2) * KVD + u * P
                            ins = pe.transpose(bank[:, 4 + blk // 2, at_:at_ + P],
                                               v_cols[:, u, blk * P:(blk + 1) * P], ident[:, :])
                    ins.then_inc(v_turn, 1)
                    for n in range(QH + 2):
                        if n % G == 0 and n < QH:
                            g = n // G
                            if n:
                                pe.wait_ge(sc_r, n)
                            pair(R_Q + g // 2, g % 2, NT, x_hi, x_lo, x_ready, NT * 3)
                        if n < QH:
                            b, g = n % 2, n // G
                            rows = slice(HD * (n % 2), HD * (n % 2) + HD)
                            pe.wait_ge(bank_free[g % 2], freed(R_Q + g // 2 + 1))
                            pe.wait_ge(k_ok, KVH)
                            if n >= 2:
                                pe.wait_ge(sc_r, n - 1)
                            for blk in range(TT):
                                ins = pe.matmul(bank[:, 2 * b + blk // 2, (blk % 2) * 2 * WIN:(blk % 2 + 1) * 2 * WIN],
                                                q_s[g % 2][rows, (n % G) // 2, blk * P:(blk + 1) * P],
                                                k_pad[rows, g, blk * WIN:(blk + 2) * WIN], start=True, stop=True)
                            ins.then_inc(s_done, 1)
                        if 1 <= n <= QH:
                            m, c = n - 1, (n - 1) % 2
                            pe.wait_ge(p_r, m + 1)
                            if m == 0:
                                pe.wait_ge(v_ok, 2)
                            else:
                                pe.wait_ge(pta_r, m)
                                pe.wait_ge(ptb_r, m)
                            for blk in range(TT):
                                for half in range(2):
                                    at_ = (blk % 2) * 2 * P + half * P
                                    ins = pe.transpose(bank[:, 4 + blk // 2, at_:at_ + P],
                                                       scores[c][:, blk, half * P:(half + 1) * P], ident[:, :])
                            ins.then_inc(t_done, 1)
                        if 2 <= n:
                            m = n - 2
                            kvh, t = m // G, m // 2
                            rows = slice(HD * (m % 2), HD * (m % 2) + HD)
                            vs = slice(HD * kvh, HD * kvh + HD)
                            pe.wait_ge(pta_r, m + 1)
                            pe.wait_ge(ptb_r, m + 1)
                            if t >= 2:
                                pe.wait_ge(mid_ready, M_AT + t - 1)
                            for blk in range(TT):
                                to = bank[rows, 6 + t % 2, blk * P:(blk + 1) * P]
                                if blk:
                                    pe.matmul(to, v_all[:, blk - 1, vs], p_t[:, blk, 0, :], start=True, stop=False)
                                ins = pe.matmul(to, v_all[:, blk, vs], p_t[:, blk, 1, :], start=blk == 0, stop=True)
                            ins.then_inc(pv_done, 1)
                    rounds(R_AO, 2, NT, mid_hi, mid_lo, mid_ready, M_AT)
                    statistics(3)
                    pe.wait_ge(mid_ready, M_AT + NT)
                    turn_embedding(1)
                for part, n in enumerate(PARTS):
                    rounds(R_GU[layer][part], n // 2, NT, x_hi, x_lo, x_ready, X)
                    rounds(R_DN[layer][part], 2, n, mid_hi, mid_lo, mid_ready, M_GU[layer][part])
                statistics(3 * layer + 1)
                for i in range(2):
                    for par in range(2):
                        r = R_PLE[layer] + i
                        def with_up(k):
                            if k != NT - 1:
                                return
                            if i or par:
                                pe.wait_ge(bank_free[1 - par], freed(r + par))
                            for kk in range(PT):
                                for u in range(2):
                                    ins = product(bank[:, 4 + u, :], 2 * par + u, NT + kk, pe_hi[:, kk, :],
                                                  pe_lo[:, kk, :], kk == 0, kk == PT - 1)
                                    if kk == PT - 1:
                                        ins.then_inc(unit_done, 1)
                        pe.wait_ge(bank_free[par], freed(r))
                        for k in range(NT):
                            pe.wait_ge(x_ready, X + NT + k + 1)
                            for u in range(2):
                                s = 2 * par + u
                                if k == 0:
                                    pe.wait_ge(w_lo_ready, 4 * r + s + 1)
                                product(bank[:, s, :], s, k, x_hi[:, k, :], x_lo[:, k, :], k == 0, k == NT - 1)
                        if layer == 1 and not i and not par:
                            pe.wait_ge(p_lo_ready, 2 * PT)
                        with_up(NT - 1)
                statistics(3 * layer + 2)
            for k in range(NT):
                pe.wait_ge(x_f32, NT * (3 * LAYERS) + k + 1)
                for t in range(TT):
                    ins = pe.transpose(bank[:, 4 * (k // 4) + t, (k % 4) * P:(k % 4 + 1) * P],
                                       x[:, k, t * P:(t + 1) * P], ident[:, :])
                if k % 4 == 3:
                    ins.then_inc(fin_t, 1)


_INS = ['x', 'p', 'a_w_in', 'a_lower_bound', 'a_norm_gain', 'a_w_out', 'kv_w', 'kv_b', 'b_w_q', 'b_b_q', 'b_sinks',
        'b_w_out', 'b_b_out', 'ffn_w_gate_up', 'ffn_w_down', 'ple_w_up', 'ple_w_gate', 'ple_b_gate', 'ln_gain',
        'ln_bias']


def kernel(**inputs):
    import numpy as _np
    import concourse.bacc as _bacc
    from concourse import mybir as _mybir
    from concourse.bass_utils import run_bass_kernel_spmd as _run

    nc = _bacc.Bacc("TRN2", target_bir_lowering=False, num_devices=1)
    arrays, args = {}, []
    for name in _INS:
        a = _np.ascontiguousarray(inputs[name])
        arrays[f"in_{name}_dram"] = a
        args.append(nc.dram_tensor(f"in_{name}_dram", a.shape, _mybir.dt.from_np(a.dtype), kind="ExternalInput").ap())
    shape = inputs['x'].shape
    args.append(nc.dram_tensor("out_0_dram", shape, _mybir.dt.float32, kind="ExternalOutput").ap())
    yoco_trunk(nc, *args)
    r = _run(nc, [arrays], core_ids=[0])
    return r.results[0]["out_0_dram"]
```

```python
from contextlib import ExitStack

import concourse.bass as bass
from concourse import mybir

F32 = mybir.dt.float32
F32R = mybir.dt.float32r
BF16 = mybir.dt.bfloat16
U16 = mybir.dt.uint16
ALU = mybir.AluOpType
ACT = mybir.ActivationFunctionType
AX_X = mybir.AxisListType.X

P = 128


def yoco_trunk(nc, x_in, p_in, a_w_in, a_lb, a_gain, a_w_out, kv_w, kv_b, w_q, b_q, sinks, w_o, b_o,
               w_gu, w_dn, w_up, w_gate, b_gate, ln_g, ln_b, out):
    S, D = x_in.shape[1:]
    NT = D // P
    TT = S // P
    HEADS = NT
    KVD = kv_w.shape[1] // 2
    KVH, HD = 4, 64
    G = D // HD // KVH
    QH = KVH * G
    WIN = P
    F = w_dn.shape[1]
    PT = w_up.shape[1] // P
    LAYERS = w_gu.shape[0]
    ALPHA = (2.0 * LAYERS) ** 0.25
    QSCALE = float(P) ** -0.5
    ASCALE = float(HD) ** -0.5
    LEVELS = P.bit_length() - 1
    FT = F // P
    PARTS = [8, 8, FT - 16]
    KMAX = NT + PT
    HALF = S // 2
    FAR = 1e30
    assert S == 512 and TT == 4 and NT == 8 and PARTS[2] % 2 == 0

    SPLIT_AT = {1: 4, 3: 5, 5: 6, 7: 7, 9: 8, 11: 9, 12: 10, 13: 11}
    OUT_AT = {13: [(0, [0, 1, 2])], 14: [(0, [3, 4])], 15: [(1, [0, 1, 2, 3, 4])],
              16: [(0, [5]), (1, [5]), (2, [0, 1, 2])], 17: [(2, [3, 4, 5]), (3, [0, 1, 2])], 18: [(3, [3])],
              19: [(3, [4]), (0, [6]), (1, [6]), (0, [7]), (1, [7]), (3, [5]), (2, [6]), (3, [6]), (2, [7]), (3, [7])]}
    RESULT = [(2 * hf + t, side) for hf in range(2) for side in range(2) for t in range(2)]

    R_HG = 0
    R_WO = R_HG + HEADS
    at = R_WO + NT // 4
    R_GU, R_DN, R_PLE = [], [], []
    for layer in range(LAYERS):
        if layer == 1:
            R_KV = at
            R_Q = R_KV + 1
            R_AO = R_Q + 2
            at = R_AO + 2
        R_GU.append([])
        R_DN.append([])
        for n in PARTS:
            R_GU[layer].append(at)
            R_DN[layer].append(at + n // 2)
            at += n // 2 + 2
        R_PLE.append(at)
        at += 2
    ROUNDS = at
    M_HG, M_GU, M_AT = 0, [[8, 16, 24], [38, 46, 54]], 30

    with ExitStack() as ctx:
        def sb(name, shape, dt=F32):
            return ctx.enter_context(nc.sbuf_tensor(name, shape, dt))

        def sem(name):
            return ctx.enter_context(nc.semaphore(name))

        bank = ctx.enter_context(nc.psum_tensor("bank", [P, 8, S], F32))

        x = sb("x", [P, NT, S])
        x_hi = sb("x_hi", [P, NT, S], F32R)
        x_lo = sb("x_lo", [P, NT, S], F32R)
        mid_hi = sb("mid_hi", [P, NT, S], F32R)
        mid_lo = sb("mid_lo", [P, NT, S], F32R)
        w_raw = sb("w_raw", [P, 4, KMAX * P])
        w_hi = sb("w_hi", [P, 4, KMAX * P], F32R)
        w_lo = sb("w_lo", [P, 4, KMAX * P], F32R)
        p_rows = sb("p_rows", [P, TT, PT * P])
        pe_hi = sb("pe_hi", [P, PT, S], F32R)
        pe_lo = sb("pe_lo", [P, PT, S], F32R)
        ident = sb("ident", [P, P])
        ones_d = sb("ones_d", [P, P])
        ones_v = sb("ones_v", [P, P])
        vec = sb("vec", [P, 160])
        lbs = sb("lbs", [P, 3, HEADS])
        sink = sb("sink", [P, QH])
        stat = sb("stat", [P, 2, 5, TT])
        arena = sb("arena", [P, 12288])

        taken = [0]

        def carve(words):
            taken[0] += words
            assert taken[0] <= 12288
            return arena[:, taken[0] - words:taken[0]]

        q_t, f_t, k_raw, k_dec, q_dec, g_t = (carve(S) for _ in range(6))
        s_q, s_f, s_n, v_t, s_g = (carve(S) for _ in range(5))
        v_row = carve(S).rearrange("p (c v) -> p c v", c=TT)
        a_mat = carve(S)
        kd_row = carve(3 * P).rearrange("p (c k) -> p c k", c=3)
        state = carve(3 * P).rearrange("p (c v) -> p c v", c=3)
        tot = [f_t] + [carve(S >> l) for l in range(1, LEVELS + 1)]
        o_sq, o_row, o_rms, o_inv, o_n, o_g = (carve(S) for _ in range(6))
        eye_m = carve(S // 2).bitcast(BF16)
        lvl_m = [carve(S // 4).bitcast(BF16) for _ in range(LEVELS)]
        x_rows = arena[:, 0:TT * D].rearrange("p (t d) -> p t d", t=TT)
        vec_rows = arena[:, TT * D:TT * D + 2 * P].rearrange("p (a c) -> p a c", a=2)
        taken[0] = 0
        k_pad = carve(KVH * (WIN + S)).rearrange("p (h s) -> p h s", h=KVH)
        v_all = carve(TT * KVD).rearrange("p (b v) -> p b v", b=TT)
        dist = carve(TT * 2 * WIN)
        shared = taken[0]
        scores = [carve(TT * 2 * WIN).rearrange("p (b s) -> p b s", b=TT) for _ in range(3)]
        p_t = [carve(TT * 2 * WIN).rearrange("p (b h t) -> p b h t", b=TT, h=2) for _ in range(2)]
        q_s = [carve(S) for _ in range(2)]
        v_cols = p_t[0].rearrange("p b h t -> p (b h t)").rearrange("p (u t) -> p u t", u=2)
        taken[0] = shared
        sq = [carve(S) for _ in range(2)]
        act_t = [carve(S) for _ in range(2)]
        hid = [carve(S) for _ in range(2)]
        sum_y, sum_sq, mean, mean_sq, var, rstd = (carve(S) for _ in range(6))
        out_rows = arena[:, 0:TT * D].rearrange("p (t d) -> p t d", t=TT)

        C_G, C_B = 0, LAYERS * 3 * NT
        C_KV = 2 * LAYERS * 3 * NT
        C_BQ = C_KV + 2 * KVD // P
        C_BO = C_BQ + NT
        N_A = C_BO + NT
        C_PG = N_A
        C_LB = C_PG + LAYERS * NT
        C_NG = C_LB + 2 * NT
        N_ALL = C_NG + 1

        w_landed = [sem(f"w_landed{s}") for s in range(4)]
        up_landed = [sem(f"up_landed{s}") for s in range(4)]
        w_hi_ready, w_lo_ready = sem("w_hi_ready"), sem("w_lo_ready")
        unit_done = sem("unit_done")
        bank_free = [sem("bank_free0"), sem("bank_free1")]
        rows_landed = [sem("rows_landed0"), sem("rows_landed1")]
        vecs_landed, sink_landed = sem("vecs_landed"), sem("sink_landed")
        p_landed = [sem("p_landed0"), sem("p_landed1")]
        consts, masks, far_ready = sem("consts"), sem("masks"), sem("far_ready")
        turned, turn_read = sem("turned"), sem("turn_read")
        lb_ready = sem("lb_ready")
        p_hi_ready, p_lo_ready = sem("p_hi_ready"), sem("p_lo_ready")
        x_f32, x_hi_ready, x_ready = sem("x_f32"), sem("x_hi_ready"), sem("x_ready")
        mid_ready = sem("mid_ready")
        sq_r, sf_r, sn_r, sg_r, vt_r = (sem(n) for n in ("sig_q", "sig_f", "sig_n", "sig_g", "v_copied"))
        q_r, f_r, k_r, g_r = (sem(n) for n in ("q_ready", "forget_ready", "k_ready", "gate_ready"))
        kd0_r, kd_r, qd_r, tot_r = (sem(n) for n in ("kdec_begun", "kdec_ready", "qdec_ready", "totals"))
        pe_vtr, vrow_r, pe_diag, pe_lvl, a_r = (sem(n) for n in
                                                ("v_turned", "v_rows", "diag_done", "level_done", "a_ready"))
        pe_kt, kt_r, pe_ds, st_r, pe_o = (sem(n) for n in
                                          ("k_turned", "k_rows", "state_terms", "states", "o_done"))
        osq_r, orow_r, pe_ms, rms_r, oinv_r, on_r, og_r, oh_r = (
            sem(n) for n in ("o_squared", "o_copied", "o_mean_sq", "o_rms_r", "o_inv_r", "o_normed", "o_gated", "o_hi"))
        silu_r = [sem(f"silu{i}") for i in range(LAYERS)]
        hhi_r = [sem(f"hidden_hi{i}") for i in range(LAYERS)]
        gate_r = sem("ple_gate")
        biased = sem("ao_biased")
        y_r, sq_done, sumy_r, sumsq_r = (sem(n) for n in ("y_ready", "y_squared", "sum_y_r", "sum_sq_r"))
        stat_mm, mean_r, msq_r, var_r, std_r, rstd_r = (
            sem(n) for n in ("stat_mm", "mean_r", "mean_sq_r", "var_r", "std_r", "rstd_r"))
        cen_r, nrm_r = sem("centred"), sem("normed")
        half_done = sem("half_done")
        q_ok = sem("query_tile")
        up_r = sem("ple_last_product")
        k_w, k_ok, v_w, v_turn, v_ok = (sem(n) for n in ("k_biased", "k_both", "v_biased", "v_turned_b", "v_ok"))
        s_done, sc_r, mx_r, nmx_r, exp_r, den_r, rden_r, p_r = (
            sem(n) for n in ("scores_done", "scores_r", "max_r", "neg_max_r", "exp_r", "den_r", "rden_r", "p_r"))
        t_done, pta_r, ptb_r, pv_done, ohi_r = (sem(n) for n in ("p_turned", "pt_a", "pt_b", "pv_done", "att_hi"))
        fin_t, fin_c, stored = sem("out_turned"), sem("out_copied"), sem("stored")

        block = ctx.enter_context(nc.Block())

        def freed(r):
            return r - (HEADS - 1)

        def x_before(n):
            return NT + 2 * NT * n

        def half(hf):
            return slice(hf * HALF, (hf + 1) * HALF)

        def f32(ap):
            return ap.bitcast(F32)

        def second(ap, l):
            return ap.rearrange("p (b two r) -> p b two r", two=2, r=1 << l)[:, :, 1, :]

        def first(ap, l):
            return ap.rearrange("p (b two r) -> p b two r", two=2, r=1 << l)[:, :, 0, :]

        def totals(l, which):
            t = tot[l].rearrange("p (b two) -> p b two", two=2)[:, :, which:which + 1]
            return t.to_broadcast([P, S >> (l + 1), 1 << l])

        @block.sync
        def _(sp):

            def load(r, par, u, src, kt):
                s = 2 * par + u
                if not (isinstance(r, int) and r == 0):
                    sp.wait_ge(w_lo_ready, 4 * r + s - 3)
                sp.dma_start(w_raw[:, s, 0:kt * P].rearrange("p (k n) -> p k n", k=kt), src
                             ).then_inc(w_landed[s], 16)

            def tile_of(w, n, k0, kt):
                return w[k0 * P:(k0 + kt) * P, bass.ds(n, P)].rearrange("(k p) n -> p k n", p=P)

            def square(r, w):
                for i in range(2):
                    for s in range(4):
                        load(r + i, s // 2, s % 2, tile_of(w, (4 * i + s) * P, 0, NT), NT)

            def head_units(h):
                for s in range(4):
                    load(h, s // 2, s % 2, tile_of(a_w_in[0], s * D + h * P, 0, NT), NT)

            def rows(side):
                at_ = slice(side * S, (side + 1) * S)
                sp.dma_start(x_rows[:, :, at_], x_in[:, :, at_].rearrange("b (t p) d -> p (b t) d", p=P)
                             ).then_inc(rows_landed[side], 16)

            rows(0)
            for s in range(4):
                if s == 2:
                    rows(1)
                load(0, s // 2, s % 2, tile_of(a_w_in[0], s * D, 0, NT), NT)
            sp.dma_start(p_rows[:, :, :], p_in[0].rearrange("b (t p) d -> p (b t) d", p=P)).then_inc(p_landed[0], 16)
            sp.dma_start(sink[:, :], sinks[0:1, :].to_broadcast([P, QH])).then_inc(sink_landed, 16)
            with sp.Fori(1, HEADS) as h:
                head_units(h)
            square(R_WO, a_w_out[0])
            for layer in range(LAYERS):
                if layer == 1:
                    for s in range(4):
                        load(R_KV, s // 2, s % 2, tile_of(kv_w, s * P, 0, NT), NT)
                    square(R_Q, w_q[0])
                    square(R_AO, w_o[0])
                    sp.wait_ge(p_lo_ready, PT)
                    sp.dma_start(p_rows[:, :, :], p_in[1].rearrange("b (t p) d -> p (b t) d", p=P)
                                 ).then_inc(p_landed[1], 16)
                j0 = 0
                for part, n in enumerate(PARTS):
                    with sp.Fori(0, n // 2) as i:
                        for s in range(4):
                            col = (s % 2) * F + (j0 + s // 2) * P
                            load(R_GU[layer][part] + i, s // 2, s % 2,
                                 tile_of(w_gu[layer], i * (2 * P) + col, 0, NT), NT)
                    for i in range(2):
                        for s in range(4):
                            load(R_DN[layer][part] + i, s // 2, s % 2,
                                 tile_of(w_dn[layer], (4 * i + s) * P, j0, n), n)
                    j0 += n
                for i in range(2):
                    for s in range(4):
                        n0 = (4 * i + s) * P
                        load(R_PLE[layer] + i, s // 2, s % 2, tile_of(w_gate[layer], n0, 0, NT), NT)
                        sp.dma_start(w_raw[:, s, NT * P:KMAX * P].rearrange("p (k n) -> p k n", k=PT),
                                     tile_of(w_up[layer], n0, 0, PT)).then_inc(up_landed[s], 16)
            for n, (t, side) in enumerate(RESULT):
                sp.wait_ge(fin_c, n + 1)
                sp.dma_start(out[0, t * P:(t + 1) * P, side * S:(side + 1) * S],
                             out_rows[:, t, side * S:(side + 1) * S]).then_inc(stored, 16)
            sp.wait_ge(stored, 16 * 2 * TT)

        @block.gpsimd
        def _(pool):
            pool.memset(ident[:, :], 0.0).then_inc(consts, 1)
            pool.memset(ones_d[:, :], 1.0 / D).then_inc(consts, 1)
            pool.memset(ones_v[:, :], 1.0 / P).then_inc(consts, 1)
            pool.wait_ge(consts, 3)
            pool.affine_select(out=ident[:, :], in_=ident[:, :], compare_op=ALU.not_equal, fill=1.0, base=0,
                               pattern=[[-1, P]], channel_multiplier=1).then_inc(consts, 1)
            pool.memset(eye_m, 0.0).then_inc(masks, 1)
            for l in range(LEVELS):
                pool.memset(lvl_m[l], 1.0).then_inc(masks, 1)
            pool.wait_ge(masks, 1 + LEVELS)
            pool.affine_select(out=eye_m, in_=eye_m, compare_op=ALU.not_equal, fill=1.0, base=0,
                               pattern=[[0, TT], [-1, P]], channel_multiplier=1).then_inc(masks, 1)
            for l in range(LEVELS):
                pool.affine_select(out=lvl_m[l], in_=lvl_m[l], compare_op=ALU.is_ge, fill=0.0, base=0,
                                   pattern=[[0, TT], [-(2 << l), 64 >> l], [0, 1 << l]],
                                   channel_multiplier=1).then_inc(masks, 1)
            pool.wait_ge(masks, 2 + 2 * LEVELS)
            for l in range(LEVELS):
                pool.affine_select(out=lvl_m[l], in_=lvl_m[l], compare_op=ALU.is_ge, fill=0.0,
                                   base=(1 << l) - 1, pattern=[[0, TT], [2 << l, 64 >> l], [0, 1 << l]],
                                   channel_multiplier=-1).then_inc(masks, 1)

            def head(h):
                pool.wait_ge(k_r, h + 1)
                if not isinstance(h, int):
                    pool.wait_ge(pe_kt, h)
                    pool.wait_ge(st_r, 3 * h)
                for l in range(LEVELS):
                    if l == 0:
                        pool.wait_ge(f_r, h + 1)
                    else:
                        pool.wait_ge(tot_r, LEVELS * h + l)
                    pair = tot[l].rearrange("p (b two) -> p b two", two=2)
                    pool.tensor_tensor(tot[l + 1], pair[:, :, 0], pair[:, :, 1], ALU.mult).then_inc(tot_r, 1)
                    if l == 0:
                        pool.tensor_copy(k_dec, k_raw).then_inc(kd0_r, 1)

            head(0)
            with pool.Fori(1, HEADS) as h:
                head(h)

            def centre(n):
                for hf in range(2):
                    pool.wait_ge(mean_r, 2 * n + hf + 1)
                    for k in range(NT):
                        pool.tensor_tensor(x[:, k, half(hf)], x[:, k, half(hf)], mean[:, half(hf)], ALU.subtract
                                           ).then_inc(cen_r, 1)

            for n in range(3 * LAYERS):
                centre(n)
                if n == 0:
                    pool.wait_ge(x_ready, x_before(1))
                    pool.memset(k_pad[:, :, 0:WIN], 0.0).then_inc(far_ready, 1)
                    d = dist.rearrange("p (b s) -> p b s", b=TT)
                    pool.iota(dist, pattern=[[0, TT], [-1, 2 * WIN]], base=WIN, channel_multiplier=1,
                              allow_small_or_imprecise_dtypes=True).then_inc(far_ready, 1)
                    pool.wait_ge(far_ready, 2)
                    pool.affine_select(out=dist, in_=dist, compare_op=ALU.is_ge, fill=FAR, base=WIN,
                                       pattern=[[0, TT], [-1, 2 * WIN]], channel_multiplier=1
                                       ).then_inc(far_ready, 1)
                    pool.wait_ge(far_ready, 3)
                    pool.affine_select(out=dist, in_=dist, compare_op=ALU.is_ge, fill=FAR, base=-1,
                                       pattern=[[0, TT], [1, 2 * WIN]], channel_multiplier=-1
                                       ).then_inc(far_ready, 1)
                    pool.wait_ge(far_ready, 4)
                    pool.memset(d[:, 0, 0:WIN], FAR).then_inc(far_ready, 1)

        @block.scalar
        def _(act):
            def split_unit_hi(r, s, kt):
                act.wait_ge(w_landed[s], 16 * (r + 1))
                act.activation(w_hi[:, s, 0:kt * P], w_raw[:, s, 0:kt * P], ACT.Copy).then_inc(w_hi_ready, 1)

            def split_hi(r, par, kt):
                for u in range(2):
                    s = 2 * par + u
                    act.wait_ge(w_landed[s], 16 * (r + 1))
                    if kt > NT:
                        layer = R_PLE.index(r if r in R_PLE else r - 1)
                        act.wait_ge(up_landed[s], 16 * (2 * layer + r - R_PLE[layer] + 1))
                    if not (isinstance(r, int) and r == 0):
                        act.wait_ge(unit_done, 4 * r + 2 * par - 2)
                    act.activation(w_hi[:, s, 0:kt * P], w_raw[:, s, 0:kt * P], ACT.Copy).then_inc(w_hi_ready, 1)

            act.dma_start(vec_rows[0:C_B, 0, :], ln_g.rearrange("l c (t p) -> (l c t) p", p=P)
                         ).then_inc(vecs_landed, 16)
            act.dma_start(vec_rows[C_B:C_KV, 0, :], ln_b.rearrange("l c (t p) -> (l c t) p", p=P)
                         ).then_inc(vecs_landed, 16)
            act.dma_start(vec_rows[C_KV:C_BQ, 0, :], kv_b.rearrange("(t p) -> t p", p=P)).then_inc(vecs_landed, 16)
            act.dma_start(vec_rows[C_BQ:C_BO, 0, :], b_q.rearrange("l (t p) -> (l t) p", p=P)
                         ).then_inc(vecs_landed, 16)
            act.dma_start(vec_rows[C_BO:N_A, 0, :], b_o.rearrange("l (t p) -> (l t) p", p=P)
                         ).then_inc(vecs_landed, 16)
            act.dma_start(vec_rows[0:C_LB - N_A, 1, :], b_gate.rearrange("l (t p) -> (l t) p", p=P)
                         ).then_inc(vecs_landed, 16)
            act.dma_start(vec_rows[C_LB - N_A:C_NG - N_A, 1, :], a_lb.rearrange("l (t p) -> (l t) p", p=P)
                         ).then_inc(vecs_landed, 16)
            act.dma_start(vec_rows[C_NG - N_A:N_ALL - N_A, 1, :], a_gain).then_inc(vecs_landed, 16)
            for k in range(NT):
                act.wait_ge(turned, k + 1)
                act.activation(x[:, k, :], bank[:, 4 + k % 4, :], ACT.Copy).then_inc(x_f32, 1)
                act.activation(x_hi[:, k, :], bank[:, 4 + k % 4, :], ACT.Copy).then_inc(x_hi_ready, 1)
                if k == 0:
                    split_hi(0, 0, NT)
            act.wait_ge(lb_ready, 1)
            act.activation(lbs[:, 0, :], lbs[:, 2, :], ACT.Sigmoid).then_inc(lb_ready, 1)

            def embedding_hi(layer):
                for k in range(PT):
                    act.wait_ge(turned, 1 + NT + PT * layer + k + 1)
                    act.activation(pe_hi[:, k, :], bank[:, 4 + k, :], ACT.Copy).then_inc(p_hi_ready, 1)

            def project(i):
                act.wait_ge(unit_done, 4 * i + 2)
                act.activation(s_q, bank[:, 0, :], ACT.Sigmoid).then_inc(sq_r, 1)
                act.activation(s_f, bank[:, 1, :], ACT.Sigmoid).then_inc(sf_r, 1)
                act.activation(s_n, bank[:, 1, :], ACT.Sigmoid, scale=-1.0).then_inc(sn_r, 1)

            def project_vg(i):
                act.wait_ge(unit_done, 4 * i + 4)
                act.activation(v_t, bank[:, 2, :], ACT.Copy).then_inc(vt_r, 1)
                act.activation(s_g, bank[:, 3, :], ACT.Sigmoid).then_inc(sg_r, 1)

            def keys(h):
                act.wait_ge(pe_kt, h + 1)
                act.activation(kd_row[:, :, :], bank[:, 6, 0:3 * P].rearrange("p (c k) -> p c k", c=3), ACT.Copy
                               ).then_inc(kt_r, 1)

            def readout(h):
                act.wait_ge(pe_o, h + 1)
                act.activation(o_sq, bank[:, 6, :], ACT.Square).then_inc(osq_r, 1)
                act.activation(o_row, bank[:, 6, :], ACT.Copy).then_inc(orow_r, 1)
                act.wait_ge(pe_ms, h + 1)
                act.activation(o_rms, bank[:, 7, :], ACT.Sqrt, bias=eps_rms).then_inc(rms_r, 1)

            def mixed(h):
                act.wait_ge(og_r, h + 1)
                act.activation(mid_hi[:, bass.ds(h, 1), :].rearrange("p a s -> p (a s)"), o_g, ACT.Copy
                               ).then_inc(oh_r, 1)

            eps_rms = vec[:, N_ALL:N_ALL + 1]

            split_hi(0, 1, NT)
            project(0)
            split_hi(1, 0, NT)
            project_vg(0)
            embedding_hi(0)

            def head(i):
                split_hi(i, 1, NT)
                if not (isinstance(i, int) and i == 1):
                    mixed(i - 2)
                split_hi(i + 1, 0, NT)
                act.wait_ge(q_r, i)
                act.wait_ge(k_r, i)
                project(i)
                keys(i - 1)
                readout(i - 1)
                act.wait_ge(pe_vtr, i)
                act.wait_ge(g_r, i)
                project_vg(i)

            head(1)
            with act.Fori(2, HEADS) as i:
                head(i)
            split_hi(R_WO, 1, NT)
            mixed(HEADS - 2)
            keys(HEADS - 1)
            readout(HEADS - 1)
            mixed(HEADS - 1)

            def squares(n, r, par):
                pp = 2 * r + par
                if pp == NT // 2 - 1:
                    act.activation(vec[0:1, N_ALL + 1 + n:N_ALL + 2 + n], eps_rms[0:1, :], ACT.Sqrt)
                for u in range(2 if pp < NT // 2 - 1 else 1):
                    j = 2 * pp + u
                    act.wait_ge(y_r, (NT + 1) * n + j + 1)
                    if pp == 1:
                        act.wait_ge(sumsq_r, 6 * n + 1)
                    elif pp > 1:
                        act.wait_ge(sumsq_r, 6 * n + 2 * pp - 2 + u)
                    act.activation(sq[u], x[:, j, :], ACT.Square).then_inc(sq_done, 1)

            def norm(n, take_half=None):
                def last_square(hf):
                    if take_half is not None:
                        take_half(hf)
                    act.wait_ge(y_r, (NT + 1) * n + NT + hf)
                    if hf == 0:
                        act.wait_ge(sumsq_r, 6 * n + 5)
                    act.activation(sq[1][:, half(hf)], x[:, NT - 1, half(hf)], ACT.Square).then_inc(sq_done, 1)

                def deviation(hf):
                    act.wait_ge(mean_r, 2 * n + hf + 1)
                    act.activation(mean_sq[:, half(hf)], mean[:, half(hf)], ACT.Square).then_inc(msq_r, 1)
                    act.wait_ge(var_r, 4 * n + 2 * hf + 2)
                    act.activation(rstd[:, half(hf)], var[:, half(hf)], ACT.Sqrt).then_inc(std_r, 1)

                def apply(hf, ks):
                    for k in ks:
                        c = NT * n + k
                        done = x_before(n) + NT * hf + k + 1
                        act.wait_ge(nrm_r, 2 * NT * n + NT * hf + k + 1)
                        act.activation(x[:, k, half(hf)], x[:, k, half(hf)], ACT.Identity,
                                       scale=vec[:, C_G + c:C_G + c + 1], bias=vec[:, C_B + c:C_B + c + 1]
                                       ).then_inc(x_f32, 1)
                        if n < 3 * LAYERS - 1:
                            act.wait_ge(x_f32, done)
                            act.activation(x_hi[:, k, half(hf)], x[:, k, half(hf)], ACT.Copy
                                           ).then_inc(x_hi_ready, 1)

                last_square(0)
                deviation(0)
                last_square(1)
                apply(0, range(3))
                deviation(1)
                apply(0, range(3, NT))
                apply(1, range(NT))

            def rounds(r0, n, kt, next_kt, take, begun=False):
                for i in range(n):
                    if i or not begun:
                        split_hi(r0 + i, 1, kt)
                    take(i, 0)
                    if next_kt is not None or i < n - 1:
                        split_hi(r0 + i + 1, 0, kt if i < n - 1 else next_kt)
                    take(i, 1)

            def hidden(layer, part, i, par):
                r = R_GU[layer][part] + i
                n = sum(PARTS[:part]) + 2 * i + par
                act.wait_ge(unit_done, 4 * r + 2 * par + 2)
                act.activation(act_t[par], bank[:, 2 * par, :], ACT.Silu).then_inc(silu_r[layer], 1)
                act.wait_ge(bank_free[par], freed(r + 1))
                act.activation(mid_hi[:, bass.ds(2 * i + par, 1), :].rearrange("p a s -> p (a s)"), hid[par],
                               ACT.Copy).then_inc(hhi_r[layer], 1)

            def last_tile(to, hf, r, n, func, bias):
                if hf == 0:
                    act.wait_ge(half_done, n + 1)
                else:
                    act.wait_ge(unit_done, 4 * r + 4)
                return act.activation(to[:, half(hf)], bank[:, 3 if hf == 0 else 0, 0:HALF], func, bias=bias)

            def gate(layer, i, par):
                r = R_PLE[layer] + i
                if i or par:
                    act.wait_ge(bank_free[1 - par], freed(r + par))
                for u in range(2):
                    j = 4 * i + 2 * par + u
                    if j == NT - 1:
                        break
                    act.wait_ge(unit_done, 4 * r + 2 * par + (2 if j < NT - 2 else 1))
                    c = C_PG + NT * layer + j
                    act.activation(act_t[u], bank[:, 2 * par + u, :], ACT.Sigmoid, bias=vec[:, c:c + 1]
                                   ).then_inc(gate_r, 1)

            rounds(R_WO, 2, NT, NT, lambda i, par: squares(0, i, par), begun=True)
            norm(0)
            for layer in range(LAYERS):
                if layer == 1:
                    split_hi(R_KV, 1, NT)
                    act.wait_ge(unit_done, 4 * R_KV + 2)
                    act.wait_ge(far_ready, 1)
                    for u in range(2):
                        for side in range(2):
                            at_ = slice(HD * side, HD * side + HD)
                            ins = act.activation(k_pad[at_, 2 * u + side, WIN:], bank[at_, u, :], ACT.Identity,
                                                 bias=vec[at_, C_KV + u:C_KV + u + 1])
                            ins.then_inc(bank_free[0] if u and side else k_w, 1)
                    split_hi(R_Q, 0, NT)
                    act.wait_ge(unit_done, 4 * R_KV + 4)
                    for u in range(2):
                        act.activation(v_cols[:, u, :], bank[:, 2 + u, :], ACT.Identity,
                                       bias=vec[:, C_KV + 2 + u:C_KV + 3 + u]
                                       ).then_inc(bank_free[1] if u else v_w, 1)
                    split_hi(R_Q, 1, NT)
                    for n in range(QH + 4):
                        if n >= 5 and n % 2:
                            t = (n - 5) // 2
                            act.wait_ge(pv_done, 2 * t + 2)
                            act.activation(mid_hi[:, t, :], bank[:, 6, :], ACT.Copy).then_inc(ohi_r, 1)
                        if 3 <= n < QH + 3:
                            act.wait_ge(t_done, n - 2)
                            if n > 4:
                                act.wait_ge(pv_done, n - 4)
                            turned_to = p_t[(n - 3) % 2][:, 0:2, :, :].rearrange("p b h t -> p (b h t)")
                            act.activation(turned_to, bank[:, 4, :], ACT.Copy).then_inc(pta_r, 1)
                        if n < QH:
                            b, at_ = n % 2, scores[n % 3]
                            act.wait_ge(nmx_r, n + 1)
                            act.activation(stat[:, b, 3, :], stat[:, b, 1, :], ACT.Exp, bias=sink[:, n:n + 1])
                            for blk in range(TT):
                                ins = act.activation(at_[:, blk, :], at_[:, blk, :], ACT.Exp,
                                                     bias=stat[:, b, 1, blk:blk + 1],
                                                     accum_out=stat[:, b, 2, blk:blk + 1])
                            ins.then_inc(exp_r, 1)
                        if 1 <= n <= QH:
                            c, at_ = (n - 1) % 2, scores[(n - 1) % 3]
                            act.wait_ge(exp_r, n)
                            act.wait_ge(rden_r, n)
                            for blk in range(TT):
                                ins = act.activation(at_[:, blk, :], at_[:, blk, :], ACT.Copy,
                                                     scale=stat[:, c, 4, blk:blk + 1])
                            ins.then_inc(p_r, 1)
                        if n in SPLIT_AT:
                            j = SPLIT_AT[n]
                            act.wait_ge(unit_done, 4 * R_Q + j - 3)
                            split_unit_hi(R_Q + j // 4, j % 4, NT)

                    def bias_out(i, par):
                        r = R_AO + i
                        for u in range(2):
                            j = 4 * i + 2 * par + u
                            if j == NT - 1:
                                break
                            act.wait_ge(unit_done, 4 * r + 2 * par + (2 if j < NT - 2 else 1))
                            if i or par:
                                act.wait_ge(y_r, (NT + 1) * 3 + j - 1)
                            act.activation(act_t[u], bank[:, 2 * par + u if j else 7, :], ACT.Identity,
                                           bias=vec[:, C_BO + j:C_BO + j + 1]).then_inc(biased, 1)

                    def project_last(hf):
                        if hf == 0:
                            act.wait_ge(y_r, (NT + 1) * 3 + NT - 2)
                        last_tile(act_t[1], hf, R_AO + 1, 3, ACT.Identity, vec[:, C_BO + NT - 1:C_BO + NT]
                                  ).then_inc(biased, 1)
                    bias_out(0, 0)
                    split_hi(R_AO + 1, 0, NT)
                    squares(3, 0, 0)
                    bias_out(0, 1)
                    squares(3, 0, 1)
                    split_hi(R_AO + 1, 1, NT)
                    bias_out(1, 0)
                    squares(3, 1, 0)
                    split_hi(R_AO + 2, 0, NT)
                    bias_out(1, 1)
                    squares(3, 1, 1)
                    norm(3, project_last)
                    embedding_hi(1)
                for part, n in enumerate(PARTS):
                    r = R_GU[layer][part]

                    def gate_up(i, next_kt):
                        split_hi(r + i, 1, NT)
                        hidden(layer, part, i, 0)
                        split_hi(r + i + 1, 0, next_kt)
                        hidden(layer, part, i, 1)
                    with act.Fori(0, n // 2 - 1) as i:
                        gate_up(i, NT)
                    gate_up(n // 2 - 1, n)
                    last = part == len(PARTS) - 1
                    rounds(R_DN[layer][part], 2, n, KMAX if last else NT,
                           lambda i, par: squares(3 * layer + 1, i, par) if last else None)
                norm(3 * layer + 1)
                def embed(i, par):
                    gate(layer, i, par)
                    squares(3 * layer + 2, i, par)

                def gate_last(hf):
                    c = C_PG + NT * layer + NT - 1
                    last_tile(act_t[1], hf, R_PLE[layer] + 1, 3 * layer + 2, ACT.Sigmoid, vec[:, c:c + 1]
                              ).then_inc(gate_r, 1)
                rounds(R_PLE[layer], 2, KMAX, NT if layer == 0 else None, embed)
                norm(3 * layer + 2, gate_last)

        @block.vector
        def _(dve):
            def split_unit_lo(r, s, kt):
                dve.wait_ge(w_hi_ready, 4 * r + s + 1)
                dve.tensor_tensor(w_lo[:, s, 0:kt * P], w_raw[:, s, 0:kt * P], f32(w_hi[:, s, 0:kt * P]),
                                  ALU.subtract).then_inc(w_lo_ready, 1)

            def split_lo(r, par, kt):
                for u in range(2):
                    split_unit_lo(r, 2 * par + u, kt)

            dve.memset(vec[:, N_ALL:N_ALL + 1], 1e-6)
            for k in range(NT):
                dve.wait_ge(x_f32, k + 1)
                dve.wait_ge(x_hi_ready, k + 1)
                dve.tensor_tensor(x_lo[:, k, :], x[:, k, :], f32(x_hi[:, k, :]), ALU.subtract).then_inc(x_ready, 1)
                if k == 0:
                    split_lo(0, 0, NT)
            dve.wait_ge(turned, NT + 1)
            dve.tensor_copy(vec[:, 0:N_A], bank[:, 4, 0:N_A])
            dve.tensor_copy(vec[:, N_A:N_ALL], bank[:, 4, P:P + N_ALL - N_A]).then_inc(turn_read, 1)
            dve.wait_ge(turn_read, 1)
            dve.tensor_tensor(lbs[:, 2, :], vec[:, C_LB:C_LB + NT], vec[:, C_LB + NT:C_LB + 2 * NT], ALU.subtract
                              ).then_inc(lb_ready, 1)
            dve.wait_ge(lb_ready, 2)
            dve.tensor_scalar(lbs[:, 1, :], lbs[:, 0, :], -1.0, 1.0, ALU.mult, ALU.add).then_inc(lb_ready, 1)

            def embedding_lo(layer):
                for k in range(PT):
                    dve.wait_ge(p_hi_ready, PT * layer + k + 1)
                    dve.tensor_tensor(pe_lo[:, k, :], bank[:, 4 + k, :], f32(pe_hi[:, k, :]), ALU.subtract
                                      ).then_inc(p_lo_ready, 1)

            dve.memset(a_mat, 0.0).then_inc(a_r, 1)

            def project(i):
                dve.wait_ge(sq_r, i + 1)
                dve.scalar_tensor_tensor(q_t, bank[:, 0, :], QSCALE, s_q, ALU.mult, ALU.mult).then_inc(q_r, 1)
                dve.wait_ge(sf_r, i + 1)
                dve.tensor_scalar(f_t, s_f, lbs[:, 1, bass.ds(i, 1)], lbs[:, 0, bass.ds(i, 1)], ALU.mult, ALU.add
                                  ).then_inc(f_r, 1)
                dve.wait_ge(sn_r, i + 1)
                dve.tensor_scalar(k_raw, s_n, lbs[:, 1, bass.ds(i, 1)], None, ALU.mult).then_inc(k_r, 1)

            def gate_of(i):
                dve.wait_ge(sg_r, i + 1)
                dve.tensor_tensor(g_t, bank[:, 3, :], s_g, ALU.mult).then_inc(g_r, 1)

            def query(i):
                dve.wait_ge(q_r, i + 1)
                dve.wait_ge(f_r, i + 1)
                dve.tensor_tensor(q_dec, q_t, f_t, ALU.mult).then_inc(qd_r, 1)

            def scores_of(h, read_before):
                dve.wait_ge(pe_diag, h + 1)
                dve.tensor_copy(v_row[:, :, :].rearrange("p c v -> p (c v)"), bank[:, 6, :]).then_inc(vrow_r, 1)
                dve.copy_predicated(a_mat, eye_m.bitcast(U16), bank[:, 7, :]).then_inc(a_r, 1)
                dve.wait_ge(kd0_r, h + 1)
                for l in range(LEVELS):
                    dve.wait_ge(pe_lvl, LEVELS * h + l + 1)
                    dve.wait_ge(a_r, (LEVELS + 1) * h + l + 2)
                    if l:
                        dve.wait_ge(tot_r, LEVELS * h + l)
                        dve.wait_ge(kd_r, LEVELS * h + l)
                    dve.wait_ge(qd_r, (LEVELS + 1) * h + l + 1)
                    dve.tensor_tensor(second(q_dec, l), second(q_dec, l), totals(l, 0), ALU.mult).then_inc(qd_r, 1)
                    dve.tensor_tensor(first(k_dec, l), first(k_dec, l), totals(l, 1), ALU.mult).then_inc(kd_r, 1)
                    shape = "p (b r) -> p b r"
                    dve.copy_predicated(second(a_mat, l), lvl_m[l].bitcast(U16).rearrange(shape, r=1 << l),
                                        bank[:, 4 + l % 2, 0:S // 2].rearrange(shape, r=1 << l)).then_inc(a_r, 1)
                    if read_before:
                        readout(h - 1, l)
                    if l == 0:
                        gate_of(h)

            def states(h):
                dve.wait_ge(pe_ds, h + 1)
                dve.wait_ge(tot_r, LEVELS * h + LEVELS)
                term = bank[:, 7, 0:3 * P].rearrange("p (c v) -> p c v", c=3)
                dve.tensor_copy(state[:, 0, :], term[:, 0, :]).then_inc(st_r, 1)
                for c in (1, 2):
                    dve.wait_ge(st_r, 3 * h + c)
                    dve.scalar_tensor_tensor(state[:, c, :], state[:, c - 1, :], tot[LEVELS][:, c:c + 1],
                                             term[:, c, :], ALU.mult, ALU.add).then_inc(st_r, 1)

            def gated(h):
                dve.wait_ge(orow_r, h + 1)
                dve.wait_ge(g_r, h + 1)
                dve.scalar_tensor_tensor(o_n, o_row, vec[:, C_NG:C_NG + 1], g_t, ALU.mult, ALU.mult
                                         ).then_inc(on_r, 1)

            def readout(h, piece):
                if 1 <= piece <= 4:
                    if piece == 1:
                        dve.wait_ge(rms_r, h + 1)
                    at_ = slice((piece - 1) * P, piece * P)
                    dve.reciprocal(o_inv[:, at_], o_rms[:, at_]).then_inc(oinv_r, 1)
                elif piece == 5:
                    dve.wait_ge(oinv_r, 4 * h + 4)
                    dve.wait_ge(on_r, h + 1)
                    dve.tensor_tensor(o_g, o_n, o_inv, ALU.mult).then_inc(og_r, 1)
                elif piece == 6:
                    dve.wait_ge(oh_r, h + 1)
                    at_ = bass.ds(h, 1)
                    dve.tensor_tensor(mid_lo[:, at_, :].rearrange("p a s -> p (a s)"), o_g,
                                      f32(mid_hi[:, at_, :]).rearrange("p a s -> p (a s)"), ALU.subtract
                                      ).then_inc(mid_ready, 1)

            split_lo(0, 1, NT)
            dve.wait_ge(masks, 2 + 3 * LEVELS)
            dve.wait_ge(lb_ready, 3)
            project(0)
            split_lo(1, 0, NT)
            query(0)
            embedding_lo(0)

            def head(i):
                split_lo(i, 1, NT)
                scores_of(i - 1, not (isinstance(i, int) and i == 1))
                split_lo(i + 1, 0, NT)
                project(i)
                states(i - 1)
                dve.wait_ge(pe_o, i)
                query(i)
                gated(i - 1)

            head(1)
            with dve.Fori(2, HEADS) as i:
                head(i)
            dve.wait_ge(k_r, HEADS)
            dve.engine_nop().then_inc(bank_free[0], 1)
            split_lo(R_WO, 1, NT)
            scores_of(HEADS - 1, True)
            dve.wait_ge(g_r, HEADS)
            dve.engine_nop().then_inc(bank_free[1], 1)
            states(HEADS - 1)
            gated(HEADS - 1)
            for piece in range(LEVELS):
                readout(HEADS - 1, piece)

            def sums(n, i, par):
                pp = 2 * i + par
                j = 2 * pp
                us = range(2 if pp < NT // 2 - 1 else 1)
                dve.wait_ge(y_r, (NT + 1) * n + j + len(us))
                if pp == 0:
                    dve.tensor_tensor(sum_y, x[:, 0, :], x[:, 1, :], ALU.add).then_inc(sumy_r, 1)
                    dve.wait_ge(sq_done, (NT + 1) * n + 2)
                    dve.tensor_tensor(sum_sq, sq[0], sq[1], ALU.add).then_inc(sumsq_r, 1)
                else:
                    for u in us:
                        dve.wait_ge(sumy_r, 6 * n + 2 * pp - 1 + u)
                        dve.tensor_tensor(sum_y, sum_y, x[:, j + u, :], ALU.add).then_inc(sumy_r, 1)
                    for u in us:
                        dve.wait_ge(sq_done, (NT + 1) * n + j + u + 1)
                        dve.wait_ge(sumsq_r, 6 * n + 2 * pp - 1 + u)
                        dve.tensor_tensor(sum_sq, sum_sq, sq[u], ALU.add).then_inc(sumsq_r, 1)

            def free_bank(par):
                dve.engine_nop().then_inc(bank_free[par], 1)

            def norm(n, take_half):
                def moments(hf):
                    at_ = half(hf)
                    dve.wait_ge(stat_mm, 2 * n + hf + 1)
                    dve.tensor_copy(mean[:, at_], bank[:, 6 + hf, 0:HALF]).then_inc(mean_r, 1)
                    dve.wait_ge(msq_r, 2 * n + hf + 1)
                    dve.tensor_tensor(var[:, at_], bank[:, 6 + hf, HALF:S], mean_sq[:, at_], ALU.subtract
                                      ).then_inc(var_r, 1)
                    dve.wait_ge(var_r, 4 * n + 2 * hf + 1)
                    dve.tensor_scalar(var[:, at_], var[:, at_], 0.0, 1e-5, ALU.max, ALU.add).then_inc(var_r, 1)

                def invert(hf):
                    dve.wait_ge(std_r, 2 * n + hf + 1)
                    dve.reciprocal(rstd[:, half(hf)], rstd[:, half(hf)]).then_inc(rstd_r, 1)
                    dve.wait_ge(rstd_r, 2 * n + hf + 1)

                def low(hf, k):
                    if n < 3 * LAYERS - 1:
                        dve.wait_ge(x_hi_ready, x_before(n) + NT * hf + k + 1)
                        dve.tensor_tensor(x_lo[:, k, half(hf)], x[:, k, half(hf)], f32(x_hi[:, k, half(hf)]),
                                          ALU.subtract).then_inc(x_ready, 1)

                def scale(hf, k):
                    dve.wait_ge(cen_r, 2 * NT * n + NT * hf + k + 1)
                    dve.tensor_tensor(x[:, k, half(hf)], x[:, k, half(hf)], rstd[:, half(hf)], ALU.mult
                                      ).then_inc(nrm_r, 1)

                take_half(0)
                moments(0)
                take_half(1)
                free_bank(1)
                invert(0)
                scale(0, 0)
                for k in range(1, NT):
                    scale(0, k)
                    low(0, k - 1)
                    if k == 3:
                        moments(1)
                    if k == 4:
                        invert(1)
                low(0, NT - 1)
                scale(1, 0)
                for k in range(1, NT):
                    scale(1, k)
                    low(1, k - 1)
                low(1, NT - 1)

            def rounds(r0, n, kt, next_kt, take, begun=False):
                for i in range(n):
                    if i or not begun:
                        split_lo(r0 + i, 1, kt)
                    take(i, 0)
                    if next_kt is not None or i < n - 1:
                        split_lo(r0 + i + 1, 0, kt if i < n - 1 else next_kt)
                    take(i, 1)

            def add_to_stream(n, r0, scale, final):
                def take(i, par):
                    r = r0 + i
                    for u in range(2):
                        j = 4 * i + 2 * par + u
                        if final and j == NT - 1:
                            break
                        dve.wait_ge(unit_done, 4 * r + 2 * par + u + 1)
                        ins = dve.scalar_tensor_tensor(x[:, j, :], x[:, j, :], scale, bank[:, 2 * par + u, :],
                                                       ALU.mult, ALU.add)
                        if final:
                            ins.then_inc(y_r, 1)
                    if not final:
                        ins.then_inc(bank_free[par], 1)
                    else:
                        sums(n, i, par)
                        if j < NT - 1:
                            free_bank(par)
                return take

            def add_half(n, r, scale):
                def take(hf):
                    if hf == 0:
                        dve.wait_ge(half_done, n + 1)
                    else:
                        dve.wait_ge(unit_done, 4 * r + 4)
                    at_ = x[:, NT - 1, half(hf)]
                    dve.scalar_tensor_tensor(at_, at_, scale, bank[:, 3 if hf == 0 else 0, 0:HALF],
                                             ALU.mult, ALU.add).then_inc(y_r, 1)
                return take

            def hidden(layer, part, i, par):
                r = R_GU[layer][part] + i
                n = sum(PARTS[:part]) + 2 * i + par
                dve.wait_ge(silu_r[layer], n + 1)
                dve.tensor_tensor(hid[par], bank[:, 2 * par + 1, :], act_t[par], ALU.mult
                                  ).then_inc(bank_free[par], 1)
                dve.wait_ge(hhi_r[layer], n + 1)
                at_ = bass.ds(2 * i + par, 1)
                dve.tensor_tensor(mid_lo[:, at_, :].rearrange("p a s -> p (a s)"), hid[par],
                                  f32(mid_hi[:, at_, :]).rearrange("p a s -> p (a s)"), ALU.subtract
                                  ).then_inc(mid_ready, 1)

            rounds(R_WO, 2, NT, NT, add_to_stream(0, R_WO, ALPHA, True), begun=True)
            norm(0, add_half(0, R_WO + 1, ALPHA))
            for layer in range(LAYERS):
                if layer == 1:
                    split_lo(R_KV, 1, NT)
                    dve.wait_ge(k_w, 3)
                    dve.wait_ge(bank_free[0], freed(R_KV + 1))
                    for kvh in range(KVH):
                        own, other = HD * (kvh % 2), HD * (1 - kvh % 2)
                        dve.tensor_copy(k_pad[other:other + HD, kvh, WIN:], k_pad[own:own + HD, kvh, WIN:]
                                        ).then_inc(k_ok, 1)
                    split_lo(R_Q, 0, NT)
                    dve.wait_ge(far_ready, 5)
                    dve.wait_ge(sink_landed, 16)
                    def query_tile(j):
                        dve.wait_ge(unit_done, 4 * R_Q + j + 1)
                        dve.tensor_scalar(q_s[j % 2], bank[:, 7, :], vec[:, C_BQ + j:C_BQ + j + 1], ASCALE,
                                          ALU.add, ALU.mult).then_inc(q_ok, 1)
                        if j % 2:
                            free_bank(j // 2 % 2)

                    query_tile(0)
                    dve.wait_ge(v_turn, 1)
                    for u in range(2):
                        dve.tensor_copy(v_all[:, 2 * u:2 * u + 2, :].rearrange("p b v -> p (b v)"),
                                        bank[:, 4 + u, :]).then_inc(v_ok, 1)
                    query_tile(1)
                    split_lo(R_Q, 1, NT)
                    for n in range(QH + 4):
                        b = n % 2
                        if 3 <= n < QH + 3:
                            dve.wait_ge(t_done, n - 2)
                            if n > 4:
                                dve.wait_ge(pv_done, n - 4)
                            turned_to = p_t[(n - 3) % 2][:, 2:4, :, :].rearrange("p b h t -> p (b h t)")
                            dve.tensor_copy(turned_to, bank[:, 5, :]).then_inc(ptb_r, 1)
                        if n < QH:
                            slope = 2.0 ** (-8.0 * (n + 1) / QH)
                            dve.wait_ge(s_done, n + 1)
                            if n >= 3:
                                dve.wait_ge(t_done, n - 2)
                            dve.scalar_tensor_tensor(scores[n % 3].rearrange("p b s -> p (b s)"), dist, -slope,
                                                     bank[:, 2 * b:2 * b + 2, :].rearrange("p a s -> p (a s)"),
                                                     ALU.mult, ALU.add).then_inc(sc_r, 1)
                            dve.wait_ge(sc_r, n + 1)
                            dve.tensor_reduce(stat[:, b, 0, :], scores[n % 3], AX_X, ALU.max).then_inc(mx_r, 1)
                            dve.wait_ge(mx_r, n + 1)
                            dve.tensor_scalar(stat[:, b, 1, :], stat[:, b, 0, :], sink[:, n:n + 1], -1.0,
                                              ALU.max, ALU.mult).then_inc(nmx_r, 1)
                        if 1 <= n <= QH:
                            m, c = n - 1, (n - 1) % 2
                            dve.wait_ge(exp_r, m + 1)
                            dve.tensor_tensor(stat[:, c, 3, :], stat[:, c, 3, :], stat[:, c, 2, :], ALU.add
                                              ).then_inc(den_r, 1)
                            dve.wait_ge(den_r, m + 1)
                            dve.reciprocal(stat[:, c, 4, :], stat[:, c, 3, :]).then_inc(rden_r, 1)
                        if n - 1 in SPLIT_AT:
                            split_unit_lo(R_Q + SPLIT_AT[n - 1] // 4, SPLIT_AT[n - 1] % 4, NT)
                        if n >= 5 and n % 2:
                            t = (n - 5) // 2
                            dve.wait_ge(ohi_r, t + 1)
                            dve.tensor_tensor(mid_lo[:, t, :], bank[:, 6, :], f32(mid_hi[:, t, :]),
                                              ALU.subtract).then_inc(mid_ready, 1)
                        if n % 2 and (n + 3) // 2 < NT:
                            query_tile((n + 3) // 2)

                    def project_out(i, par):
                        for u in range(2):
                            j = 4 * i + 2 * par + u
                            if j == NT - 1:
                                break
                            dve.wait_ge(biased, j + 1)
                            dve.scalar_tensor_tensor(x[:, j, :], x[:, j, :], ALPHA, act_t[u], ALU.mult, ALU.add
                                                     ).then_inc(y_r, 1)
                        if j < NT - 1:
                            free_bank(par)
                        sums(3, i, par)

                    def project_last(hf):
                        dve.wait_ge(biased, NT + hf)
                        at_ = x[:, NT - 1, half(hf)]
                        dve.scalar_tensor_tensor(at_, at_, ALPHA, act_t[1][:, half(hf)], ALU.mult, ALU.add
                                                 ).then_inc(y_r, 1)
                    split_lo(R_AO + 1, 0, NT)
                    project_out(0, 0)
                    project_out(0, 1)
                    split_lo(R_AO + 1, 1, NT)
                    project_out(1, 0)
                    split_lo(R_AO + 2, 0, NT)
                    project_out(1, 1)
                    norm(3, project_last)
                    embedding_lo(1)
                for part, n in enumerate(PARTS):
                    r = R_GU[layer][part]

                    def gate_up(i, next_kt):
                        split_lo(r + i, 1, NT)
                        hidden(layer, part, i, 0)
                        split_lo(r + i + 1, 0, next_kt)
                        hidden(layer, part, i, 1)
                    with dve.Fori(0, n // 2 - 1) as i:
                        gate_up(i, NT)
                    gate_up(n // 2 - 1, n)
                    last = part == len(PARTS) - 1
                    rounds(R_DN[layer][part], 2, n, KMAX if last else NT,
                           add_to_stream(3 * layer + 1, R_DN[layer][part], ALPHA if part == 0 else 1.0, last))
                norm(3 * layer + 1, add_half(3 * layer + 1, R_DN[layer][-1] + 1, 1.0))

                def embed(i, par):
                    for u in range(2):
                        j = 4 * i + 2 * par + u
                        if j == NT - 1:
                            break
                        dve.wait_ge(gate_r, (NT + 1) * layer + j + 1)
                        ins = dve.tensor_tensor(hid[u], bank[:, 4 + u, :], act_t[u], ALU.mult)
                    if j < NT - 1:
                        ins.then_inc(bank_free[par], 1)
                        dve.wait_ge(bank_free[par], freed(R_PLE[layer] + i + 1))
                    else:
                        ins.then_inc(up_r, 1)
                        dve.wait_ge(up_r, 3 * layer + 1)
                    for u in range(2):
                        j = 4 * i + 2 * par + u
                        if j == NT - 1:
                            break
                        dve.scalar_tensor_tensor(x[:, j, :], x[:, j, :], ALPHA, hid[u], ALU.mult, ALU.add
                                                 ).then_inc(y_r, 1)
                    sums(3 * layer + 2, i, par)

                def embed_last(hf):
                    dve.wait_ge(gate_r, (NT + 1) * layer + NT + hf)
                    dve.tensor_tensor(hid[1][:, half(hf)], bank[:, 5 if hf == 0 else 1, 0:HALF],
                                      act_t[1][:, half(hf)], ALU.mult).then_inc(up_r, 1)
                    dve.wait_ge(up_r, 3 * layer + 2 + hf)
                    at_ = x[:, NT - 1, half(hf)]
                    dve.scalar_tensor_tensor(at_, at_, ALPHA, hid[1][:, half(hf)], ALU.mult, ALU.add
                                             ).then_inc(y_r, 1)
                rounds(R_PLE[layer], 2, KMAX, NT if layer == 0 else None, embed)
                norm(3 * layer + 2, embed_last)
            for n, (t, side) in enumerate(RESULT):
                dve.wait_ge(fin_t, n // 2 + 1)
                dve.tensor_copy(out_rows[:, t, side * S:(side + 1) * S], bank[:, 2 * t + side, :]
                                ).then_inc(fin_c, 1)

        @block.tensor
        def _(pe):
            def product(to, s, k, hi, lo, start, stop):
                cols = slice(k * P, (k + 1) * P)
                pe.matmul(to, w_hi[:, s, cols], hi, start=start, stop=False)
                pe.matmul(to, w_hi[:, s, cols], lo, start=False, stop=False)
                return pe.matmul(to, w_lo[:, s, cols], hi, start=False, stop=stop)

            def free(r, par, taken=None):
                if isinstance(taken, tuple):
                    pe.wait_ge(*taken)
                elif taken is not None:
                    pe.wait_ge(taken, r)
                elif not isinstance(r, int) or r > 0:
                    pe.wait_ge(bank_free[par], freed(r))

            def pair(r, par, kt, hi, lo, ready, base, also=None, taken=None, ks=None):
                for k in range(kt) if ks is None else ks:
                    if k == 0:
                        free(r, par, taken)
                    if ready is not None:
                        pe.wait_ge(ready, base + k + 1)
                    for u in range(2):
                        s = 2 * par + u
                        if k == 0:
                            pe.wait_ge(w_lo_ready, 4 * r + s + 1)
                        ins = product(bank[:, s, :], s, k, hi[:, k, :], lo[:, k, :], k == 0, k == kt - 1)
                        if k == kt - 1:
                            ins.then_inc(unit_done, 1)
                    if also is not None:
                        also(k)

            def opening(r, n, up=None):
                free(r, 0)
                for hf in range(2):
                    for k in range(NT):
                        pe.wait_ge(x_ready, x_before(n) + NT * hf + k + 1)
                        for s in range(2):
                            if k == 0 and hf == 0:
                                pe.wait_ge(w_lo_ready, 4 * r + s + 1)
                            ins = product(bank[:, s, half(hf)], s, k, x_hi[:, k, half(hf)], x_lo[:, k, half(hf)],
                                          k == 0, k == NT - 1)
                            if up is None and hf and k == NT - 1:
                                ins.then_inc(unit_done, 1)

            def up_product(to, s, cols):
                for k in range(PT):
                    ins = product(to, s, NT + k, pe_hi[:, k, cols], pe_lo[:, k, cols], k == 0, k == PT - 1)
                return ins

            def statistics(n, hf):
                at_, to = half(hf), bank[:, 6 + hf, :]
                pe.wait_ge(sumy_r, 6 * n + 6)
                pe.matmul(to[:, 0:HALF], ones_d[:, :], sum_y[:, at_], start=True, stop=False)
                pe.wait_ge(y_r, (NT + 1) * n + NT + hf)
                pe.matmul(to[:, 0:HALF], ones_d[:, :], x[:, NT - 1, at_], start=False, stop=True)
                pe.wait_ge(sumsq_r, 6 * n + 6)
                pe.matmul(to[:, HALF:S], ones_d[:, :], sum_sq[:, at_], start=True, stop=False)
                pe.wait_ge(sq_done, (NT + 1) * n + NT + hf)
                pe.matmul(to[:, HALF:S], ones_d[:, :], sq[1][:, at_], start=False, stop=True
                          ).then_inc(stat_mm, 1)

            def closing(r, kt, hi, lo, ready, base, n, up=False):
                whole = slice(0, S)
                free(r, 1)
                pe.wait_ge(w_lo_ready, 4 * r + 3)
                for k in range(kt):
                    if ready is not None:
                        pe.wait_ge(ready, base + k + 1)
                    ins = product(bank[:, 2, :], 2, k, hi[:, k, :], lo[:, k, :], k == 0, k == kt - 1)
                if up:
                    pe.wait_ge(bank_free[0], freed(r + 1))
                    ins = up_product(bank[:, 4, :], 2, whole)
                ins.then_inc(unit_done, 1)
                pe.wait_ge(w_lo_ready, 4 * r + 4)
                for k in range(kt):
                    ins = product(bank[:, 3, 0:HALF], 3, k, hi[:, k, half(0)], lo[:, k, half(0)],
                                  k == 0, k == kt - 1)
                if up:
                    ins = up_product(bank[:, 5, 0:HALF], 3, half(0))
                ins.then_inc(half_done, 1)
                pe.wait_ge(bank_free[0], freed(r + 1))
                for k in range(kt):
                    ins = product(bank[:, 0, 0:HALF], 3, k, hi[:, k, half(1)], lo[:, k, half(1)],
                                  k == 0, k == kt - 1)
                    if k == 3:
                        statistics(n, 0)
                if up:
                    ins = up_product(bank[:, 1, 0:HALF], 3, half(1))
                ins.then_inc(unit_done, 1)
                statistics(n, 1)

            def turn_stream(ks):
                for k in ks:
                    if k >= 4:
                        pe.wait_ge(x_hi_ready, k - 3)
                    for t in range(TT):
                        ins = pe.transpose(bank[:, 4 + k % 4, t * P:(t + 1) * P],
                                           x_rows[:, t, k * P:(k + 1) * P], ident[:, :])
                    ins.then_inc(turned, 1)

            pe.wait_ge(consts, 4)
            pe.wait_ge(rows_landed[0], 16)
            turn_stream(range(4))
            pair(0, 0, NT, x_hi, x_lo, x_ready, 0, ks=range(4))
            pe.wait_ge(rows_landed[1], 16)
            turn_stream(range(4, NT))
            pe.wait_ge(vecs_landed, 16 * 8)
            pe.wait_ge(x_hi_ready, 5)
            pe.transpose(bank[:, 4, 0:N_A], vec_rows[0:N_A, 0, :], ident[0:N_A, 0:N_A])
            pe.transpose(bank[:, 4, P:P + N_ALL - N_A], vec_rows[0:N_ALL - N_A, 1, :],
                         ident[0:N_ALL - N_A, 0:N_ALL - N_A]).then_inc(turned, 1)

            def turn_embedding(layer):
                pe.wait_ge(p_landed[layer], 16)
                for k in range(PT):
                    for t in range(TT):
                        ins = pe.transpose(bank[:, 4 + k, t * P:(t + 1) * P], p_rows[:, t, k * P:(k + 1) * P],
                                           ident[:, :])
                    ins.then_inc(turned, 1)

            def recur(h, step):
                if step == 1:
                    pe.wait_ge(vt_r, h + 1)
                    for c in range(TT):
                        ins = pe.transpose(bank[:, 6, c * P:(c + 1) * P], v_t[:, c * P:(c + 1) * P], ident[:, :])
                    ins.then_inc(pe_vtr, 1)
                    pe.wait_ge(k_r, h + 1)
                    pe.wait_ge(q_r, h + 1)
                    for c in range(TT):
                        at_ = slice(c * P, (c + 1) * P)
                        ins = pe.matmul(bank[:, 7, at_], k_raw[:, at_], q_t[:, at_], start=True, stop=True)
                    ins.then_inc(pe_diag, 1)
                elif 2 <= step <= LEVELS + 1:
                    l = step - 2
                    pe.wait_ge(qd_r, (LEVELS + 1) * h + l + 1)
                    if l == 0:
                        pe.wait_ge(kd0_r, h + 1)
                    else:
                        pe.wait_ge(kd_r, LEVELS * h + l)
                    pe.wait_ge(a_r, (LEVELS + 1) * h + (l + 1 if l >= 2 else 1))
                    for c in range(TT):
                        at_ = slice(c * P, (c + 1) * P)
                        ins = pe.matmul(bank[:, 4 + l % 2, c * 64:(c + 1) * 64].rearrange(
                            "p (b r) -> p b r", r=1 << l), k_dec[:, at_], second(q_dec[:, at_], l),
                            start=True, stop=True)
                    ins.then_inc(pe_lvl, 1)
                elif step == LEVELS + 2:
                    pe.wait_ge(kd_r, LEVELS * h + LEVELS)
                    pe.wait_ge(vrow_r, h + 1)
                    for c in range(3):
                        ins = pe.transpose(bank[:, 6, c * P:(c + 1) * P], k_dec[:, c * P:(c + 1) * P], ident[:, :])
                    ins.then_inc(pe_kt, 1)
                elif step == LEVELS + 4:
                    pe.wait_ge(kt_r, h + 1)
                    pe.wait_ge(a_r, (LEVELS + 1) * h + 2)
                    for c in range(3):
                        ins = pe.matmul(bank[:, 7, c * P:(c + 1) * P], kd_row[:, c, :], v_row[:, c, :],
                                        start=True, stop=True)
                    ins.then_inc(pe_ds, 1)
                elif step == LEVELS + 6:
                    pe.wait_ge(a_r, (LEVELS + 1) * (h + 1) + 1)
                    pe.wait_ge(qd_r, (LEVELS + 1) * (h + 1))
                    pe.wait_ge(st_r, 3 * h + 3)
                    for c in range(TT):
                        at_ = slice(c * P, (c + 1) * P)
                        ins = pe.matmul(bank[:, 6, at_], v_row[:, c, :], a_mat[:, at_], start=True, stop=c == 0)
                        if c:
                            ins = pe.matmul(bank[:, 6, at_], state[:, c - 1, :], q_dec[:, at_],
                                            start=False, stop=True)
                    ins.then_inc(pe_o, 1)
                elif step == LEVELS + 7:
                    pe.wait_ge(osq_r, h + 1)
                    pe.matmul(bank[:, 7, :], ones_v[:, :], o_sq, start=True, stop=True).then_inc(pe_ms, 1)

            pair(0, 0, NT, x_hi, x_lo, x_ready, 0, ks=range(4, NT))
            pair(0, 1, NT, x_hi, x_lo, x_ready, 0)
            pe.wait_ge(turn_read, 1)
            pe.wait_ge(x_hi_ready, 6)
            turn_embedding(0)
            pe.wait_ge(p_lo_ready, PT)
            with pe.Fori(1, HEADS) as i:
                h = i - 1
                pair(i, 0, NT, x_hi, x_lo, None, 0, lambda k: recur(h, k), k_r)
                pair(i, 1, NT, x_hi, x_lo, None, 0, lambda k: recur(h, NT + k), g_r)
            last = HEADS - 1
            steps = [(0, range(last - 1), 0), (1, range(last - 1), last - 1), (0, [last - 1], last - 1),
                     (1, [last - 1], last)]
            for par, ks, first_step in steps:
                pair(R_WO, par, NT, mid_hi, mid_lo, mid_ready, M_HG, lambda k: recur(last, first_step + k),
                     (k_r, g_r)[par], ks)
            recur(last, 2 * last)
            pair(R_WO, 0, NT, mid_hi, mid_lo, mid_ready, M_HG, ks=[last])
            pair(R_WO, 1, NT, mid_hi, mid_lo, mid_ready, M_HG, ks=[last])

            def rounds(r0, n, kt, hi, lo, ready, base):
                if n:
                    with pe.Fori(r0, r0 + n) as r:
                        pair(r, 0, kt, hi, lo, ready, base)
                        pair(r, 1, kt, hi, lo, ready, base)

            pair(R_WO + 1, 0, NT, mid_hi, mid_lo, None, 0)
            closing(R_WO + 1, NT, mid_hi, mid_lo, None, 0, 0)
            for layer in range(LAYERS):
                if layer == 1:
                    opening(R_KV, 2)
                    pair(R_KV, 1, NT, x_hi, x_lo, None, 0)
                    def query_tile(j, ks):
                        for k in ks:
                            if k == 0:
                                pe.wait_ge(w_lo_ready, 4 * R_Q + j + 1)
                                if j:
                                    pe.wait_ge(q_ok, j)
                            ins = product(bank[:, 7, :], j % 4, k, x_hi[:, k, :], x_lo[:, k, :],
                                          k == 0, k == NT - 1)
                        if NT - 1 in ks:
                            ins.then_inc(unit_done, 1)

                    def scores_of(n):
                        b, g = n % 2, n // G
                        rows = slice(HD * (n % 2), HD * (n % 2) + HD)
                        pe.wait_ge(q_ok, n // 2 + 1)
                        if n == 0:
                            pe.wait_ge(k_ok, KVH)
                        if n >= 2:
                            pe.wait_ge(sc_r, n - 1)
                        for blk in range(TT):
                            ins = pe.matmul(bank[:, 2 * b + blk // 2, (blk % 2) * 2 * WIN:(blk % 2 + 1) * 2 * WIN],
                                            q_s[n // 2 % 2][rows, blk * P:(blk + 1) * P],
                                            k_pad[rows, g, blk * WIN:(blk + 2) * WIN], start=True, stop=True)
                        ins.then_inc(s_done, 1)

                    query_tile(0, range(NT))
                    pe.wait_ge(v_w, 1)
                    pe.wait_ge(bank_free[1], freed(R_KV + 1))
                    for blk in range(TT):
                        for u in range(2):
                            at_ = (blk % 2) * KVD + u * P
                            ins = pe.transpose(bank[:, 4 + blk // 2, at_:at_ + P],
                                               v_cols[:, u, blk * P:(blk + 1) * P], ident[:, :])
                    ins.then_inc(v_turn, 1)
                    query_tile(1, range(NT))
                    pe.wait_ge(bank_free[1], freed(R_KV + 1))
                    scores_of(0)
                    def out_unit(u, ks):
                        for k in ks:
                            if k == 0:
                                pe.wait_ge(w_lo_ready, 4 * R_AO + u + 1)
                                pe.wait_ge(bank_free[u // 2], freed(R_AO))
                                if u == 0:
                                    pe.wait_ge(q_ok, NT)
                                else:
                                    pe.wait_ge(sc_r, QH - 1 + u // 2)
                            pe.wait_ge(mid_ready, M_AT + k + 1)
                            ins = product(bank[:, u or 7, :], u, k, mid_hi[:, k, :], mid_lo[:, k, :],
                                          k == 0, k == NT - 1)
                            if k == NT - 1:
                                ins.then_inc(unit_done, 1)

                    for n in range(QH + 3):
                        if n + 1 < QH:
                            scores_of(n + 1)
                        if 2 <= n <= QH + 1:
                            m = n - 2
                            pe.wait_ge(p_r, m + 1)
                            if m == 0:
                                pe.wait_ge(v_ok, 2)
                            else:
                                pe.wait_ge(pta_r, m)
                                pe.wait_ge(ptb_r, m)
                            for blk in range(TT):
                                for side in range(2):
                                    at_ = (blk % 2) * 2 * P + side * P
                                    ins = pe.transpose(bank[:, 4 + blk // 2, at_:at_ + P],
                                                       scores[m % 3][:, blk, side * P:(side + 1) * P], ident[:, :])
                            ins.then_inc(t_done, 1)
                        j = (n + 4) // 2
                        if j < NT:
                            query_tile(j, range(NT // 2, NT) if n % 2 else range(NT // 2))
                        for u, ks in OUT_AT.get(n, ()):
                            out_unit(u, ks)
                        if 3 <= n:
                            m = n - 3
                            kvh, t = m // G, m // 2
                            rows = slice(HD * (m % 2), HD * (m % 2) + HD)
                            vs = slice(HD * kvh, HD * kvh + HD)
                            pe.wait_ge(pta_r, m + 1)
                            pe.wait_ge(ptb_r, m + 1)
                            if t >= 1:
                                pe.wait_ge(mid_ready, M_AT + t)
                            for blk in range(TT):
                                to, probs = bank[rows, 6, blk * P:(blk + 1) * P], p_t[m % 2]
                                if blk:
                                    pe.matmul(to, v_all[:, blk - 1, vs], probs[:, blk, 0, :], start=True, stop=False)
                                ins = pe.matmul(to, v_all[:, blk, vs], probs[:, blk, 1, :], start=blk == 0, stop=True)
                            ins.then_inc(pv_done, 1)
                    turn_embedding(1)
                    for u, ks in OUT_AT[QH + 3]:
                        out_unit(u, ks)
                    pair(R_AO + 1, 0, NT, mid_hi, mid_lo, None, 0, taken=(biased, 2))
                    closing(R_AO + 1, NT, mid_hi, mid_lo, None, 0, 3)
                for part, n in enumerate(PARTS):
                    r = R_GU[layer][part]
                    if part == 0:
                        opening(r, 3 * layer)
                        pair(r, 1, NT, x_hi, x_lo, None, 0)
                    rounds(r + (part == 0), n // 2 - (part == 0), NT, x_hi, x_lo, None, 0)
                    r, base = R_DN[layer][part], M_GU[layer][part]
                    if part < len(PARTS) - 1:
                        rounds(r, 2, n, mid_hi, mid_lo, mid_ready, base)
                    else:
                        rounds(r, 1, n, mid_hi, mid_lo, mid_ready, base)
                        pair(r + 1, 0, n, mid_hi, mid_lo, None, 0)
                        closing(r + 1, n, mid_hi, mid_lo, None, 0, 3 * layer + 1)
                n = 3 * layer + 2
                for pp in range(NT // 2 - 1):
                    r, par = R_PLE[layer] + pp // 2, pp % 2
                    if pp == 0:
                        opening(r, n - 1, up=True)
                        pe.wait_ge(p_lo_ready, PT * (layer + 1))
                    else:
                        free(r, par)
                        for k in range(NT):
                            for s in (2 * par, 2 * par + 1):
                                if k == 0:
                                    pe.wait_ge(w_lo_ready, 4 * r + s + 1)
                                product(bank[:, s, :], s, k, x_hi[:, k, :], x_lo[:, k, :], k == 0, k == NT - 1)
                        pe.wait_ge(bank_free[1 - par], freed(r + par))
                    for u in range(2):
                        up_product(bank[:, 4 + u, :], 2 * par + u, slice(0, S)).then_inc(unit_done, 1)
                closing(R_PLE[layer] + 1, NT, x_hi, x_lo, None, 0, n, up=True)
            for hf in range(2):
                for k in range(NT):
                    pe.wait_ge(x_f32, x_before(3 * LAYERS - 1) + NT * hf + k + 1)
                    for t in (2 * hf, 2 * hf + 1):
                        ins = pe.transpose(bank[:, 2 * t + k // 4, (k % 4) * P:(k % 4 + 1) * P],
                                           x[:, k, t * P:(t + 1) * P], ident[:, :])
                    if k % 4 == 3:
                        ins.then_inc(fin_t, 1)


_INS = ['x', 'p', 'a_w_in', 'a_lower_bound', 'a_norm_gain', 'a_w_out', 'kv_w', 'kv_b', 'b_w_q', 'b_b_q', 'b_sinks',
        'b_w_out', 'b_b_out', 'ffn_w_gate_up', 'ffn_w_down', 'ple_w_up', 'ple_w_gate', 'ple_b_gate', 'ln_gain',
        'ln_bias']


def kernel(**inputs):
    import numpy as _np
    import concourse.bacc as _bacc
    from concourse import mybir as _mybir
    from concourse.bass_utils import run_bass_kernel_spmd as _run

    nc = _bacc.Bacc("TRN2", target_bir_lowering=False, num_devices=1)
    arrays, args = {}, []
    for name in _INS:
        a = _np.ascontiguousarray(inputs[name])
        arrays[f"in_{name}_dram"] = a
        args.append(nc.dram_tensor(f"in_{name}_dram", a.shape, _mybir.dt.from_np(a.dtype), kind="ExternalInput").ap())
    shape = inputs['x'].shape
    args.append(nc.dram_tensor("out_0_dram", shape, _mybir.dt.float32, kind="ExternalOutput").ap())
    yoco_trunk(nc, *args)
    r = _run(nc, [arrays], core_ids=[0])
    return r.results[0]["out_0_dram"]
```

```python
from contextlib import ExitStack

import concourse.bass as bass
from concourse import mybir

F32 = mybir.dt.float32
F32R = mybir.dt.float32r
BF16 = mybir.dt.bfloat16
U16 = mybir.dt.uint16
ALU = mybir.AluOpType
ACT = mybir.ActivationFunctionType
AX_X = mybir.AxisListType.X

P = 128


def yoco_trunk(nc, x_in, p_in, a_w_in, a_lb, a_gain, a_w_out, kv_w, kv_b, w_q, b_q, sinks, w_o, b_o,
               w_gu, w_dn, w_up, w_gate, b_gate, ln_g, ln_b, out):
    S, D = x_in.shape[1:]
    NT = D // P
    TT = S // P
    HEADS = NT
    KVD = kv_w.shape[1] // 2
    KVH, HD = 4, 64
    G = D // HD // KVH
    QH = KVH * G
    WIN = P
    F = w_dn.shape[1]
    PT = w_up.shape[1] // P
    LAYERS = w_gu.shape[0]
    ALPHA = (2.0 * LAYERS) ** 0.25
    QSCALE = float(P) ** -0.5
    ASCALE = float(HD) ** -0.5
    LEVELS = P.bit_length() - 1
    FT = F // P
    PARTS = [8, 8, FT - 16]
    KMAX = NT + PT
    HALF = S // 2
    FAR = 1e30
    assert S == 512 and TT == 4 and NT == 8 and PARTS[2] % 2 == 0

    SPLIT_AT = {1: 4, 3: 5, 5: 6, 7: 7, 9: 8, 11: 9, 12: 10, 13: 11}
    OUT_AT = {13: [(0, [0, 1, 2])], 14: [(0, [3, 4])], 15: [(1, [0, 1, 2, 3, 4])],
              16: [(0, [5]), (1, [5]), (2, [0, 1, 2])], 17: [(2, [3, 4, 5]), (3, [0, 1, 2])], 18: [(3, [3])],
              19: [(3, [4]), (0, [6]), (1, [6]), (0, [7]), (1, [7]), (3, [5]), (2, [6]), (3, [6]), (2, [7]), (3, [7])]}
    RESULT = [(0, 0), (1, 0), (0, 1), (1, 1), (2, 0), (2, 1), (3, 0), (3, 1)]

    R_HG = 0
    R_WO = R_HG + HEADS
    at = R_WO + NT // 4
    R_GU, R_DN, R_PLE = [], [], []
    for layer in range(LAYERS):
        if layer == 1:
            R_KV = at
            R_Q = R_KV + 1
            R_AO = R_Q + 2
            at = R_AO + 2
        R_GU.append([])
        R_DN.append([])
        for n in PARTS:
            R_GU[layer].append(at)
            R_DN[layer].append(at + n // 2)
            at += n // 2 + 2
        R_PLE.append(at)
        at += 2
    ROUNDS = at
    M_HG, M_GU, M_AT = 0, [[8, 16, 24], [38, 46, 54]], 30

    with ExitStack() as ctx:
        def sb(name, shape, dt=F32):
            return ctx.enter_context(nc.sbuf_tensor(name, shape, dt))

        def sem(name):
            return ctx.enter_context(nc.semaphore(name))

        bank = ctx.enter_context(nc.psum_tensor("bank", [P, 8, S], F32))

        x = sb("x", [P, NT, S])
        x_hi = sb("x_hi", [P, NT, S], F32R)
        x_lo = sb("x_lo", [P, NT, S], F32R)
        mid_hi = sb("mid_hi", [P, NT, S], F32R)
        mid_lo = sb("mid_lo", [P, NT, S], F32R)
        w_raw = sb("w_raw", [P, 4, KMAX * P])
        w_hi = sb("w_hi", [P, 4, KMAX * P], F32R)
        w_lo = sb("w_lo", [P, 4, KMAX * P], F32R)
        p_rows = sb("p_rows", [P, TT, PT * P])
        pe_hi = sb("pe_hi", [P, PT, S], F32R)
        pe_lo = sb("pe_lo", [P, PT, S], F32R)
        ident = sb("ident", [P, P])
        ones_d = sb("ones_d", [P, P])
        ones_v = sb("ones_v", [P, P])
        vec = sb("vec", [P, 160])
        lbs = sb("lbs", [P, 3, HEADS])
        sink = sb("sink", [P, QH])
        stat = sb("stat", [P, 2, 5, TT])
        token = sb("token", [P, 2, 3, 2])
        arena = sb("arena", [P, 12288])

        taken = [0]

        def carve(words):
            taken[0] += words
            assert taken[0] <= 12288
            return arena[:, taken[0] - words:taken[0]]

        q_t, f_t, k_raw, k_dec, q_dec, g_t = (carve(S) for _ in range(6))
        s_q, s_f, s_n, v_t, s_g = (carve(S) for _ in range(5))
        v_row = carve(S).rearrange("p (c v) -> p c v", c=TT)
        a_mat = carve(S)
        kd_row = carve(3 * P).rearrange("p (c k) -> p c k", c=3)
        state = carve(3 * P).rearrange("p (c v) -> p c v", c=3)
        tot = [f_t] + [carve(S >> l) for l in range(1, LEVELS + 1)]
        o_sq, o_row, o_rms, o_inv, o_n, o_g = (carve(S) for _ in range(6))
        eye_m = carve(S // 2).bitcast(BF16)
        lvl_m = [carve(S // 4).bitcast(BF16) for _ in range(LEVELS)]
        x_rows = arena[:, 0:TT * D].rearrange("p (t d) -> p t d", t=TT)
        vec_rows = arena[:, TT * D:TT * D + 2 * P].rearrange("p (a c) -> p a c", a=2)
        taken[0] = 0
        k_pad = carve(KVH * (WIN + S)).rearrange("p (h s) -> p h s", h=KVH)
        v_all = carve(TT * KVD).rearrange("p (b v) -> p b v", b=TT)
        dist = carve(TT * 2 * WIN)
        shared = taken[0]
        scores = [carve(TT * 2 * WIN).rearrange("p (b s) -> p b s", b=TT) for _ in range(3)]
        p_t = [carve(TT * 2 * WIN).rearrange("p (b h t) -> p b h t", b=TT, h=2) for _ in range(2)]
        q_s = [carve(S) for _ in range(2)]
        v_cols = p_t[0].rearrange("p b h t -> p (b h t)").rearrange("p (u t) -> p u t", u=2)
        taken[0] = shared
        sq = [carve(S) for _ in range(2)]
        act_t = [carve(S) for _ in range(2)]
        hid = [carve(S) for _ in range(2)]
        sum_y, sum_sq, mean, diag = (carve(S) for _ in range(4))
        out_rows = arena[:, 0:TT * D].rearrange("p (t d) -> p t d", t=TT)

        C_G, C_B = 0, LAYERS * 3 * NT
        C_KV = 2 * LAYERS * 3 * NT
        C_BQ = C_KV + 2 * KVD // P
        C_BO = C_BQ + NT
        N_A = C_BO + NT
        C_PG = N_A
        C_LB = C_PG + LAYERS * NT
        C_NG = C_LB + 2 * NT
        N_ALL = C_NG + 1

        w_landed = [sem(f"w_landed{s}") for s in range(4)]
        up_landed = [sem(f"up_landed{s}") for s in range(4)]
        w_hi_ready, w_lo_ready = sem("w_hi_ready"), sem("w_lo_ready")
        unit_done = sem("unit_done")
        bank_free = [sem("bank_free0"), sem("bank_free1")]
        rows_landed = [sem("rows_landed0"), sem("rows_landed1")]
        vecs_landed, sink_landed = sem("vecs_landed"), sem("sink_landed")
        p_landed = [sem("p_landed0"), sem("p_landed1")]
        consts, masks, far_ready = sem("consts"), sem("masks"), sem("far_ready")
        turned, turn_read = sem("turned"), sem("turn_read")
        lb_ready = sem("lb_ready")
        p_hi_ready, p_lo_ready = sem("p_hi_ready"), sem("p_lo_ready")
        x_f32, x_hi_ready, x_ready = sem("x_f32"), sem("x_hi_ready"), sem("x_ready")
        x_kept = sem("x_kept")
        mid_ready = sem("mid_ready")
        sq_r, sf_r, sn_r, sg_r, vt_r = (sem(n) for n in ("sig_q", "sig_f", "sig_n", "sig_g", "v_copied"))
        q_r, f_r, k_r, g_r = (sem(n) for n in ("q_ready", "forget_ready", "k_ready", "gate_ready"))
        kd0_r, kd_r, qd_r, tot_r = (sem(n) for n in ("kdec_begun", "kdec_ready", "qdec_ready", "totals"))
        pe_vtr, vrow_r, pe_diag, pe_lvl, a_r = (sem(n) for n in
                                                ("v_turned", "v_rows", "diag_done", "level_done", "a_ready"))
        pe_kt, kt_r, pe_ds, st_r, pe_o = (sem(n) for n in
                                          ("k_turned", "k_rows", "state_terms", "states", "o_done"))
        osq_r, orow_r, pe_ms, rms_r, oinv_r, on_r, og_r, oh_r = (
            sem(n) for n in ("o_squared", "o_copied", "o_mean_sq", "o_rms_r", "o_inv_r", "o_normed", "o_gated", "o_hi"))
        silu_r = [sem(f"silu{i}") for i in range(LAYERS)]
        hhi_r = [sem(f"hidden_hi{i}") for i in range(LAYERS)]
        gate_r = sem("ple_gate")
        biased = sem("ao_biased")
        y_r, sq_done, sumy_r, sumsq_r = (sem(n) for n in ("y_ready", "y_squared", "sum_y_r", "sum_sq_r"))
        moments_mm, mean_mm, mean_r, var_r, std_r, inv_r, diag_r, spread_mm = (
            sem(n) for n in ("moments_mm", "mean_mm", "mean_r", "var_r", "std_r", "inv_r", "diag_r", "spread_mm"))
        cen_r, nrm_r = sem("centred"), sem("normed")
        half_done = sem("half_done")
        q_ok = sem("query_tile")
        up_r = sem("ple_last_product")
        k_w, k_ok, v_w, v_turn, v_ok = (sem(n) for n in ("k_biased", "k_both", "v_biased", "v_turned_b", "v_ok"))
        s_done, sc_r, mx_r, nmx_r, exp_r, den_r, rden_r, p_r = (
            sem(n) for n in ("scores_done", "scores_r", "max_r", "neg_max_r", "exp_r", "den_r", "rden_r", "p_r"))
        t_done, pta_r, ptb_r, pv_done, ohi_r = (sem(n) for n in ("p_turned", "pt_a", "pt_b", "pv_done", "att_hi"))
        fin_t, stored = sem("out_turned"), sem("stored")
        fin_c = [sem("out_copied_dve"), sem("out_copied_act")]

        block = ctx.enter_context(nc.Block())

        def freed(r):
            return r - (HEADS - 1)

        def x_before(n):
            return NT + 2 * NT * n

        def bank_of(hf, u):
            return u if hf == 0 else 2 + u

        def half(hf):
            return slice(hf * HALF, (hf + 1) * HALF)

        def f32(ap):
            return ap.bitcast(F32)

        def second(ap, l):
            return ap.rearrange("p (b two r) -> p b two r", two=2, r=1 << l)[:, :, 1, :]

        def first(ap, l):
            return ap.rearrange("p (b two r) -> p b two r", two=2, r=1 << l)[:, :, 0, :]

        def totals(l, which):
            t = tot[l].rearrange("p (b two) -> p b two", two=2)[:, :, which:which + 1]
            return t.to_broadcast([P, S >> (l + 1), 1 << l])

        @block.sync
        def _(sp):

            def load(r, par, u, src, kt):
                s = 2 * par + u
                if not (isinstance(r, int) and r == 0):
                    sp.wait_ge(w_lo_ready, 4 * r + s - 3)
                sp.dma_start(w_raw[:, s, 0:kt * P].rearrange("p (k n) -> p k n", k=kt), src
                             ).then_inc(w_landed[s], 16)

            def tile_of(w, n, k0, kt):
                return w[k0 * P:(k0 + kt) * P, bass.ds(n, P)].rearrange("(k p) n -> p k n", p=P)

            def square(r, w):
                for i in range(2):
                    for s in range(4):
                        load(r + i, s // 2, s % 2, tile_of(w, (4 * i + s) * P, 0, NT), NT)

            def head_units(h):
                for s in range(4):
                    load(h, s // 2, s % 2, tile_of(a_w_in[0], s * D + h * P, 0, NT), NT)

            def rows(side):
                at_ = slice(side * S, (side + 1) * S)
                sp.dma_start(x_rows[:, :, at_], x_in[:, :, at_].rearrange("b (t p) d -> p (b t) d", p=P)
                             ).then_inc(rows_landed[side], 16)

            rows(0)
            for s in range(4):
                if s == 2:
                    rows(1)
                load(0, s // 2, s % 2, tile_of(a_w_in[0], s * D, 0, NT), NT)
            sp.dma_start(p_rows[:, :, :], p_in[0].rearrange("b (t p) d -> p (b t) d", p=P)).then_inc(p_landed[0], 16)
            sp.dma_start(sink[:, :], sinks[0:1, :].to_broadcast([P, QH])).then_inc(sink_landed, 16)
            with sp.Fori(1, HEADS) as h:
                head_units(h)
            square(R_WO, a_w_out[0])
            for layer in range(LAYERS):
                if layer == 1:
                    for s in range(4):
                        load(R_KV, s // 2, s % 2, tile_of(kv_w, s * P, 0, NT), NT)
                    square(R_Q, w_q[0])
                    square(R_AO, w_o[0])
                    sp.wait_ge(p_lo_ready, PT)
                    sp.dma_start(p_rows[:, :, :], p_in[1].rearrange("b (t p) d -> p (b t) d", p=P)
                                 ).then_inc(p_landed[1], 16)
                j0 = 0
                for part, n in enumerate(PARTS):
                    with sp.Fori(0, n // 2) as i:
                        for s in range(4):
                            col = (s % 2) * F + (j0 + s // 2) * P
                            load(R_GU[layer][part] + i, s // 2, s % 2,
                                 tile_of(w_gu[layer], i * (2 * P) + col, 0, NT), NT)
                    for i in range(2):
                        for s in range(4):
                            load(R_DN[layer][part] + i, s // 2, s % 2,
                                 tile_of(w_dn[layer], (4 * i + s) * P, j0, n), n)
                    j0 += n
                for i in range(2):
                    for s in range(4):
                        n0 = (4 * i + s) * P
                        load(R_PLE[layer] + i, s // 2, s % 2, tile_of(w_gate[layer], n0, 0, NT), NT)
                        sp.dma_start(w_raw[:, s, NT * P:KMAX * P].rearrange("p (k n) -> p k n", k=PT),
                                     tile_of(w_up[layer], n0, 0, PT)).then_inc(up_landed[s], 16)
            for n, (t, side) in enumerate(RESULT):
                sp.wait_ge(fin_c[n % 2], n // 2 + 1)
                sp.dma_start(out[0, t * P:(t + 1) * P, side * S:(side + 1) * S],
                             out_rows[:, t, side * S:(side + 1) * S]).then_inc(stored, 16)
            sp.wait_ge(stored, 16 * 2 * TT)

        @block.gpsimd
        def _(pool):
            pool.memset(ident[:, :], 0.0).then_inc(consts, 1)
            pool.memset(ones_d[:, :], 1.0 / D).then_inc(consts, 1)
            pool.memset(ones_v[:, :], 1.0 / P).then_inc(consts, 1)
            pool.wait_ge(consts, 3)
            pool.affine_select(out=ident[:, :], in_=ident[:, :], compare_op=ALU.not_equal, fill=1.0, base=0,
                               pattern=[[-1, P]], channel_multiplier=1).then_inc(consts, 1)
            pool.memset(eye_m, 0.0).then_inc(masks, 1)
            for l in range(LEVELS):
                pool.memset(lvl_m[l], 1.0).then_inc(masks, 1)
            pool.wait_ge(masks, 1 + LEVELS)
            pool.affine_select(out=eye_m, in_=eye_m, compare_op=ALU.not_equal, fill=1.0, base=0,
                               pattern=[[0, TT], [-1, P]], channel_multiplier=1).then_inc(masks, 1)
            for l in range(LEVELS):
                pool.affine_select(out=lvl_m[l], in_=lvl_m[l], compare_op=ALU.is_ge, fill=0.0, base=0,
                                   pattern=[[0, TT], [-(2 << l), 64 >> l], [0, 1 << l]],
                                   channel_multiplier=1).then_inc(masks, 1)
            pool.wait_ge(masks, 2 + 2 * LEVELS)
            for l in range(LEVELS):
                pool.affine_select(out=lvl_m[l], in_=lvl_m[l], compare_op=ALU.is_ge, fill=0.0,
                                   base=(1 << l) - 1, pattern=[[0, TT], [2 << l, 64 >> l], [0, 1 << l]],
                                   channel_multiplier=-1).then_inc(masks, 1)

            def head(h):
                pool.wait_ge(k_r, h + 1)
                if not isinstance(h, int):
                    pool.wait_ge(pe_kt, h)
                    pool.wait_ge(st_r, 3 * h)
                for l in range(LEVELS):
                    if l == 0:
                        pool.wait_ge(f_r, h + 1)
                    else:
                        pool.wait_ge(tot_r, LEVELS * h + l)
                    pair = tot[l].rearrange("p (b two) -> p b two", two=2)
                    pool.tensor_tensor(tot[l + 1], pair[:, :, 0], pair[:, :, 1], ALU.mult).then_inc(tot_r, 1)
                    if l == 0:
                        pool.tensor_copy(k_dec, k_raw).then_inc(kd0_r, 1)

            head(0)
            with pool.Fori(1, HEADS) as h:
                head(h)

            def centre(n):
                for hf in range(2):
                    pool.wait_ge(mean_r, 2 * n + hf + 1)
                    for k in range(NT):
                        if k == NT - 1:
                            pool.wait_ge(moments_mm, 2 * n + hf + 1)
                        pool.tensor_tensor(x[:, k, half(hf)], x[:, k, half(hf)], mean[:, half(hf)], ALU.subtract
                                           ).then_inc(cen_r, 1)

            def keep(n):
                for k in range(NT):
                    c = C_B + NT * n + k
                    pool.wait_ge(x_ready, x_before(n) + NT + k + 1)
                    pool.tensor_tensor(x[:, k, :], x[:, k, :], vec[:, c:c + 1].to_broadcast([P, S]), ALU.add
                                       ).then_inc(x_kept, 1)

            def split_lo(r, kt):
                for s in (2, 3):
                    pool.wait_ge(w_hi_ready, 4 * r + s + 1)
                    pool.wait_ge(w_lo_ready, 4 * r + s)
                    pool.tensor_tensor(w_lo[:, s, 0:kt * P], w_raw[:, s, 0:kt * P], f32(w_hi[:, s, 0:kt * P]),
                                       ALU.subtract).then_inc(w_lo_ready, 1)

            last_round = [R_WO + 1]
            for layer in range(LAYERS):
                last_round += [R_DN[layer][-1] + 1, R_PLE[layer] + 1] + ([R_AO + 1] if layer == 0 else [])
            for n in range(3 * LAYERS):
                centre(n)
                if n < 3 * LAYERS - 1:
                    split_lo(last_round[n] + 1, KMAX if n % 3 == 1 else NT)
                    keep(n)
                if n == 0:
                    pool.wait_ge(x_ready, x_before(1))
                    pool.memset(k_pad[:, :, 0:WIN], 0.0).then_inc(far_ready, 1)
                    d = dist.rearrange("p (b s) -> p b s", b=TT)
                    pool.iota(dist, pattern=[[0, TT], [-1, 2 * WIN]], base=WIN, channel_multiplier=1,
                              allow_small_or_imprecise_dtypes=True).then_inc(far_ready, 1)
                    pool.wait_ge(far_ready, 2)
                    pool.affine_select(out=dist, in_=dist, compare_op=ALU.is_ge, fill=FAR, base=WIN,
                                       pattern=[[0, TT], [-1, 2 * WIN]], channel_multiplier=1
                                       ).then_inc(far_ready, 1)
                    pool.wait_ge(far_ready, 3)
                    pool.affine_select(out=dist, in_=dist, compare_op=ALU.is_ge, fill=FAR, base=-1,
                                       pattern=[[0, TT], [1, 2 * WIN]], channel_multiplier=-1
                                       ).then_inc(far_ready, 1)
                    pool.wait_ge(far_ready, 4)
                    pool.memset(d[:, 0, 0:WIN], FAR).then_inc(far_ready, 1)

        @block.scalar
        def _(act):
            def split_unit_hi(r, s, kt):
                act.wait_ge(w_landed[s], 16 * (r + 1))
                act.activation(w_hi[:, s, 0:kt * P], w_raw[:, s, 0:kt * P], ACT.Copy).then_inc(w_hi_ready, 1)

            def split_hi(r, par, kt):
                for u in range(2):
                    s = 2 * par + u
                    act.wait_ge(w_landed[s], 16 * (r + 1))
                    if kt > NT:
                        layer = R_PLE.index(r if r in R_PLE else r - 1)
                        act.wait_ge(up_landed[s], 16 * (2 * layer + r - R_PLE[layer] + 1))
                    if not (isinstance(r, int) and r == 0):
                        act.wait_ge(unit_done, 4 * r + 2 * par - 2)
                    act.activation(w_hi[:, s, 0:kt * P], w_raw[:, s, 0:kt * P], ACT.Copy).then_inc(w_hi_ready, 1)

            act.dma_start(vec_rows[0:C_B, 0, :], ln_g.rearrange("l c (t p) -> (l c t) p", p=P)
                         ).then_inc(vecs_landed, 16)
            act.dma_start(vec_rows[C_B:C_KV, 0, :], ln_b.rearrange("l c (t p) -> (l c t) p", p=P)
                         ).then_inc(vecs_landed, 16)
            act.dma_start(vec_rows[C_KV:C_BQ, 0, :], kv_b.rearrange("(t p) -> t p", p=P)).then_inc(vecs_landed, 16)
            act.dma_start(vec_rows[C_BQ:C_BO, 0, :], b_q.rearrange("l (t p) -> (l t) p", p=P)
                         ).then_inc(vecs_landed, 16)
            act.dma_start(vec_rows[C_BO:N_A, 0, :], b_o.rearrange("l (t p) -> (l t) p", p=P)
                         ).then_inc(vecs_landed, 16)
            act.dma_start(vec_rows[0:C_LB - N_A, 1, :], b_gate.rearrange("l (t p) -> (l t) p", p=P)
                         ).then_inc(vecs_landed, 16)
            act.dma_start(vec_rows[C_LB - N_A:C_NG - N_A, 1, :], a_lb.rearrange("l (t p) -> (l t) p", p=P)
                         ).then_inc(vecs_landed, 16)
            act.dma_start(vec_rows[C_NG - N_A:N_ALL - N_A, 1, :], a_gain).then_inc(vecs_landed, 16)
            for k in range(NT):
                act.wait_ge(turned, k + 1)
                act.activation(x[:, k, :], bank[:, 4 + k % 4, :], ACT.Copy).then_inc(x_f32, 1)
                act.activation(x_hi[:, k, :], bank[:, 4 + k % 4, :], ACT.Copy).then_inc(x_hi_ready, 1)
                if k == 0:
                    split_hi(0, 0, NT)
            act.wait_ge(lb_ready, 1)
            act.activation(lbs[:, 0, :], lbs[:, 2, :], ACT.Sigmoid).then_inc(lb_ready, 1)

            def embedding_hi(layer):
                for k in range(PT):
                    act.wait_ge(turned, 1 + NT + PT * layer + k + 1)
                    act.activation(pe_hi[:, k, :], bank[:, 4 + k, :], ACT.Copy).then_inc(p_hi_ready, 1)

            def project(i):
                act.wait_ge(unit_done, 4 * i + 2)
                act.activation(s_q, bank[:, 0, :], ACT.Sigmoid).then_inc(sq_r, 1)
                act.activation(s_f, bank[:, 1, :], ACT.Sigmoid).then_inc(sf_r, 1)
                act.activation(s_n, bank[:, 1, :], ACT.Sigmoid, scale=-1.0).then_inc(sn_r, 1)

            def project_vg(i):
                act.wait_ge(unit_done, 4 * i + 4)
                act.activation(v_t, bank[:, 2, :], ACT.Copy).then_inc(vt_r, 1)
                act.activation(s_g, bank[:, 3, :], ACT.Sigmoid).then_inc(sg_r, 1)

            def keys(h):
                act.wait_ge(pe_kt, h + 1)
                act.activation(kd_row[:, :, :], bank[:, 6, 0:3 * P].rearrange("p (c k) -> p c k", c=3), ACT.Copy
                               ).then_inc(kt_r, 1)

            def readout(h):
                act.wait_ge(pe_o, h + 1)
                act.activation(o_sq, bank[:, 6, :], ACT.Square).then_inc(osq_r, 1)
                act.activation(o_row, bank[:, 6, :], ACT.Copy).then_inc(orow_r, 1)
                act.wait_ge(pe_ms, h + 1)
                act.activation(o_rms, bank[:, 7, :], ACT.Sqrt, bias=eps_rms).then_inc(rms_r, 1)

            def mixed(h):
                act.wait_ge(og_r, h + 1)
                act.activation(mid_hi[:, bass.ds(h, 1), :].rearrange("p a s -> p (a s)"), o_g, ACT.Copy
                               ).then_inc(oh_r, 1)

            eps_rms = vec[:, N_ALL:N_ALL + 1]

            split_hi(0, 1, NT)
            project(0)
            split_hi(1, 0, NT)
            project_vg(0)
            embedding_hi(0)

            def head(i):
                split_hi(i, 1, NT)
                if not (isinstance(i, int) and i == 1):
                    mixed(i - 2)
                split_hi(i + 1, 0, NT)
                act.wait_ge(q_r, i)
                act.wait_ge(k_r, i)
                project(i)
                keys(i - 1)
                readout(i - 1)
                act.wait_ge(pe_vtr, i)
                act.wait_ge(g_r, i)
                project_vg(i)

            head(1)
            with act.Fori(2, HEADS) as i:
                head(i)
            split_hi(R_WO, 1, NT)
            mixed(HEADS - 2)
            keys(HEADS - 1)
            act.activation(vec[0:1, N_ALL + 7:N_ALL + 8], eps_rms[0:1, :], ACT.Sqrt)
            readout(HEADS - 1)
            for hf in range(2):
                act.wait_ge(og_r, HEADS + hf)
                act.activation(mid_hi[:, HEADS - 1, half(hf)], o_g[:, half(hf)], ACT.Copy).then_inc(oh_r, 1)

            def squares(n, i, par):
                for u in range(2):
                    j = 4 * i + 2 * par + u
                    act.wait_ge(y_r, 10 * n + j + 1)
                    if j >= 2:
                        act.wait_ge(sumsq_r, 7 * n + max(1, j - 2))
                    act.activation(sq[u], x[:, j, :], ACT.Square).then_inc(sq_done, 1)

            def norm(n, r, next_kt, take=None):
                def square(hf, u):
                    if take is not None:
                        take(hf, u)
                    at_ = half(hf)
                    act.wait_ge(y_r, 10 * n + 5 + 2 * hf + u)
                    if hf == 0:
                        act.wait_ge(sumsq_r, 7 * n + 2 + u)
                    act.activation(sq[u % 2][:, at_], x[:, NT // 2 + u, at_], ACT.Square).then_inc(sq_done, 1)

                def root(hf):
                    act.wait_ge(var_r, 8 * n + 4 * hf + 4)
                    act.activation(token[:, hf, 1, :], token[:, hf, 0, :], ACT.Sqrt).then_inc(std_r, 1)

                def copy_mean(hf):
                    act.wait_ge(mean_mm, 2 * n + hf + 1)
                    act.activation(mean[:, half(hf)], bank[:, 6 + hf, 0:HALF], ACT.Copy).then_inc(mean_r, 1)

                def apply(hf, ks):
                    for k in ks:
                        at_, c = half(hf), C_B + NT * n + k
                        act.wait_ge(nrm_r, 2 * NT * n + NT * hf + k + 1)
                        if n < 3 * LAYERS - 1:
                            act.activation(x_hi[:, k, at_], x[:, k, at_], ACT.Identity, bias=vec[:, c:c + 1]
                                           ).then_inc(x_hi_ready, 1)
                        else:
                            act.activation(x[:, k, at_], x[:, k, at_], ACT.Identity, bias=vec[:, c:c + 1]
                                           ).then_inc(x_f32, 1)

                square(0, 2)
                square(0, 3)
                act.activation(vec[0:1, N_ALL + 1 + n:N_ALL + 2 + n], eps_rms[0:1, :], ACT.Sqrt)
                copy_mean(0)
                root(0)
                square(1, 2)
                apply(0, [0])
                square(1, 3)
                apply(0, [1])
                copy_mean(1)
                apply(0, [2])
                root(1)
                apply(0, range(3, NT - 1))
                if next_kt is not None:
                    split_hi(r + 1, 1, next_kt)
                apply(0, [NT - 1])
                apply(1, range(NT))

            def rounds(r0, n, kt, next_kt, take):
                for i in range(n):
                    if i:
                        split_hi(r0 + i, 1, kt)
                    take(i, 0)
                    split_hi(r0 + i + 1, 0, kt if i < n - 1 else next_kt)
                    take(i, 1)

            def last_rounds(r, kt, next_kt, take):
                take(0, 0)
                split_hi(r + 1, 0, kt)
                take(0, 1)
                split_hi(r + 1, 1, kt)
                take(1, 0)
                if next_kt is not None:
                    split_hi(r + 2, 0, next_kt)

            def hidden(layer, part, i, par):
                r = R_GU[layer][part] + i
                n = sum(PARTS[:part]) + 2 * i + par
                act.wait_ge(unit_done, 4 * r + 2 * par + 2)
                act.activation(act_t[par], bank[:, 2 * par, :], ACT.Silu).then_inc(silu_r[layer], 1)
                act.wait_ge(bank_free[par], freed(r + 1))
                act.activation(mid_hi[:, bass.ds(2 * i + par, 1), :].rearrange("p a s -> p (a s)"), hid[par],
                               ACT.Copy).then_inc(hhi_r[layer], 1)

            def last_pair(to, hf, u, r, n, func, bias):
                if hf == 0:
                    act.wait_ge(half_done, 2 * n + u - 1)
                else:
                    act.wait_ge(unit_done, 4 * r + u + 1)
                return act.activation(to[:, half(hf)], bank[:, bank_of(hf, u), 0:HALF], func, bias=bias)

            def gate(layer, i, par):
                r = R_PLE[layer] + i
                if i or par:
                    act.wait_ge(bank_free[1 - par], freed(r + par))
                for u in range(2):
                    j = 4 * i + 2 * par + u
                    act.wait_ge(unit_done, 4 * r + 2 * par + 2)
                    c = C_PG + NT * layer + j
                    act.activation(act_t[u], bank[:, 2 * par + u, :], ACT.Sigmoid, bias=vec[:, c:c + 1]
                                   ).then_inc(gate_r, 1)

            last_rounds(R_WO, NT, NT, lambda i, par: squares(0, i, par))
            norm(0, R_WO + 1, NT)
            for layer in range(LAYERS):
                if layer == 1:
                    act.wait_ge(unit_done, 4 * R_KV + 2)
                    act.wait_ge(far_ready, 1)
                    for u in range(2):
                        for side in range(2):
                            at_ = slice(HD * side, HD * side + HD)
                            ins = act.activation(k_pad[at_, 2 * u + side, WIN:], bank[at_, u, :], ACT.Identity,
                                                 bias=vec[at_, C_KV + u:C_KV + u + 1])
                            ins.then_inc(bank_free[0] if u and side else k_w, 1)
                    split_hi(R_Q, 0, NT)
                    act.wait_ge(unit_done, 4 * R_KV + 4)
                    for u in range(2):
                        act.activation(v_cols[:, u, :], bank[:, 2 + u, :], ACT.Identity,
                                       bias=vec[:, C_KV + 2 + u:C_KV + 3 + u]
                                       ).then_inc(bank_free[1] if u else v_w, 1)
                    split_hi(R_Q, 1, NT)
                    for n in range(QH + 4):
                        if n >= 5 and n % 2:
                            t = (n - 5) // 2
                            act.wait_ge(pv_done, 2 * t + 2)
                            act.activation(mid_hi[:, t, :], bank[:, 6, :], ACT.Copy).then_inc(ohi_r, 1)
                        if 3 <= n < QH + 3:
                            act.wait_ge(t_done, n - 2)
                            if n > 4:
                                act.wait_ge(pv_done, n - 4)
                            turned_to = p_t[(n - 3) % 2][:, 0:2, :, :].rearrange("p b h t -> p (b h t)")
                            act.activation(turned_to, bank[:, 4, :], ACT.Copy).then_inc(pta_r, 1)
                        if n < QH:
                            b, at_ = n % 2, scores[n % 3]
                            act.wait_ge(nmx_r, n + 1)
                            act.activation(stat[:, b, 3, :], stat[:, b, 1, :], ACT.Exp, bias=sink[:, n:n + 1])
                            for blk in range(TT):
                                ins = act.activation(at_[:, blk, :], at_[:, blk, :], ACT.Exp,
                                                     bias=stat[:, b, 1, blk:blk + 1],
                                                     accum_out=stat[:, b, 2, blk:blk + 1])
                            ins.then_inc(exp_r, 1)
                        if 1 <= n <= QH:
                            c, at_ = (n - 1) % 2, scores[(n - 1) % 3]
                            act.wait_ge(exp_r, n)
                            act.wait_ge(rden_r, n)
                            for blk in range(TT):
                                ins = act.activation(at_[:, blk, :], at_[:, blk, :], ACT.Copy,
                                                     scale=stat[:, c, 4, blk:blk + 1])
                            ins.then_inc(p_r, 1)
                        if n in SPLIT_AT:
                            j = SPLIT_AT[n]
                            act.wait_ge(unit_done, 4 * R_Q + j - 3)
                            split_unit_hi(R_Q + j // 4, j % 4, NT)

                    def bias_out(i, par):
                        for u in range(2):
                            j = 4 * i + 2 * par + u
                            act.wait_ge(unit_done, 4 * R_AO + 4 * i + 2 * par + 2)
                            if i or par:
                                act.wait_ge(y_r, 10 * 3 + j - 1)
                            act.activation(act_t[u], bank[:, 2 * par + u if j else 7, :], ACT.Identity,
                                           bias=vec[:, C_BO + j:C_BO + j + 1]).then_inc(biased, 1)

                    def bias_last(hf, u):
                        if hf == 0:
                            act.wait_ge(y_r, 10 * 3 + 3 + u)
                        c = C_BO + NT // 2 + u
                        last_pair(act_t[u % 2], hf, u, R_AO + 1, 3, ACT.Identity, vec[:, c:c + 1]
                                  ).then_inc(biased, 1)

                    bias_out(0, 0)
                    split_hi(R_AO + 1, 0, NT)
                    squares(3, 0, 0)
                    bias_out(0, 1)
                    squares(3, 0, 1)
                    split_hi(R_AO + 1, 1, NT)
                    embedding_hi(1)
                    bias_out(1, 0)
                    squares(3, 1, 0)
                    split_hi(R_AO + 2, 0, NT)
                    norm(3, R_AO + 1, NT, bias_last)
                for part, n in enumerate(PARTS):
                    r = R_GU[layer][part]

                    def gate_up(i, next_kt):
                        hidden(layer, part, i, 0)
                        split_hi(r + i + 1, 0, next_kt)
                        hidden(layer, part, i, 1)
                        split_hi(r + i + 1, 1, next_kt)

                    if part:
                        split_hi(r, 1, NT)
                    with act.Fori(0, n // 2 - 1) as i:
                        gate_up(i, NT)
                    gate_up(n // 2 - 1, n)
                    if part < len(PARTS) - 1:
                        rounds(R_DN[layer][part], 2, n, NT, lambda i, par: None)
                r = R_DN[layer][-1] + 1
                last_rounds(r - 1, PARTS[-1], KMAX, lambda i, par: squares(3 * layer + 1, i, par))
                norm(3 * layer + 1, r, KMAX)

                def embed(i, par):
                    gate(layer, i, par)
                    squares(3 * layer + 2, i, par)

                def gate_last(hf, u):
                    if hf == 0:
                        act.wait_ge(bank_free[0], freed(R_PLE[layer] + 2))
                    c = C_PG + NT * layer + NT // 2 + u
                    last_pair(act_t[u % 2], hf, u, R_PLE[layer] + 1, 3 * layer + 2, ACT.Sigmoid, vec[:, c:c + 1]
                              ).then_inc(gate_r, 1)
                next_kt = NT if layer == 0 else None
                last_rounds(R_PLE[layer], KMAX, next_kt, embed)
                norm(3 * layer + 2, R_PLE[layer] + 1, next_kt, gate_last)

            for n, (t, side) in enumerate(RESULT):
                if n % 2:
                    act.wait_ge(fin_t, n + 1)
                    act.activation(out_rows[:, t, side * S:(side + 1) * S], bank[:, 2 * t + side, :], ACT.Copy
                                   ).then_inc(fin_c[1], 1)

        @block.vector
        def _(dve):
            def split_unit_lo(r, s, kt):
                dve.wait_ge(w_hi_ready, 4 * r + s + 1)
                dve.tensor_tensor(w_lo[:, s, 0:kt * P], w_raw[:, s, 0:kt * P], f32(w_hi[:, s, 0:kt * P]),
                                  ALU.subtract).then_inc(w_lo_ready, 1)

            def split_lo(r, par, kt):
                for u in range(2):
                    split_unit_lo(r, 2 * par + u, kt)

            dve.memset(vec[:, N_ALL:N_ALL + 1], 1e-6)
            for k in range(NT):
                dve.wait_ge(x_f32, k + 1)
                dve.wait_ge(x_hi_ready, k + 1)
                dve.tensor_tensor(x_lo[:, k, :], x[:, k, :], f32(x_hi[:, k, :]), ALU.subtract).then_inc(x_ready, 1)
                if k == 0:
                    split_lo(0, 0, NT)
            dve.wait_ge(turned, NT + 1)
            dve.tensor_copy(vec[:, 0:N_A], bank[:, 4, 0:N_A])
            dve.tensor_copy(vec[:, N_A:N_ALL], bank[:, 4, P:P + N_ALL - N_A]).then_inc(turn_read, 1)
            dve.wait_ge(turn_read, 1)
            dve.tensor_tensor(lbs[:, 2, :], vec[:, C_LB:C_LB + NT], vec[:, C_LB + NT:C_LB + 2 * NT], ALU.subtract
                              ).then_inc(lb_ready, 1)
            dve.wait_ge(lb_ready, 2)
            dve.tensor_scalar(lbs[:, 1, :], lbs[:, 0, :], -1.0, 1.0, ALU.mult, ALU.add).then_inc(lb_ready, 1)

            def embedding_lo(layer):
                for k in range(PT):
                    dve.wait_ge(p_hi_ready, PT * layer + k + 1)
                    dve.tensor_tensor(pe_lo[:, k, :], bank[:, 4 + k, :], f32(pe_hi[:, k, :]), ALU.subtract
                                      ).then_inc(p_lo_ready, 1)

            dve.memset(a_mat, 0.0).then_inc(a_r, 1)

            def project(i):
                dve.wait_ge(sq_r, i + 1)
                dve.scalar_tensor_tensor(q_t, bank[:, 0, :], QSCALE, s_q, ALU.mult, ALU.mult).then_inc(q_r, 1)
                dve.wait_ge(sf_r, i + 1)
                dve.tensor_scalar(f_t, s_f, lbs[:, 1, bass.ds(i, 1)], lbs[:, 0, bass.ds(i, 1)], ALU.mult, ALU.add
                                  ).then_inc(f_r, 1)
                dve.wait_ge(sn_r, i + 1)
                dve.tensor_scalar(k_raw, s_n, lbs[:, 1, bass.ds(i, 1)], None, ALU.mult).then_inc(k_r, 1)

            def gate_of(i):
                dve.wait_ge(sg_r, i + 1)
                dve.tensor_tensor(g_t, bank[:, 3, :], s_g, ALU.mult).then_inc(g_r, 1)

            def query(i):
                dve.wait_ge(q_r, i + 1)
                dve.wait_ge(f_r, i + 1)
                dve.tensor_tensor(q_dec, q_t, f_t, ALU.mult).then_inc(qd_r, 1)

            def scores_of(h, read_before):
                dve.wait_ge(pe_diag, h + 1)
                dve.tensor_copy(v_row[:, :, :].rearrange("p c v -> p (c v)"), bank[:, 6, :]).then_inc(vrow_r, 1)
                dve.copy_predicated(a_mat, eye_m.bitcast(U16), bank[:, 7, :]).then_inc(a_r, 1)
                dve.wait_ge(kd0_r, h + 1)
                for l in range(LEVELS):
                    dve.wait_ge(pe_lvl, LEVELS * h + l + 1)
                    dve.wait_ge(a_r, (LEVELS + 1) * h + l + 2)
                    if l:
                        dve.wait_ge(tot_r, LEVELS * h + l)
                        dve.wait_ge(kd_r, LEVELS * h + l)
                    dve.wait_ge(qd_r, (LEVELS + 1) * h + l + 1)
                    dve.tensor_tensor(second(q_dec, l), second(q_dec, l), totals(l, 0), ALU.mult).then_inc(qd_r, 1)
                    dve.tensor_tensor(first(k_dec, l), first(k_dec, l), totals(l, 1), ALU.mult).then_inc(kd_r, 1)
                    shape = "p (b r) -> p b r"
                    dve.copy_predicated(second(a_mat, l), lvl_m[l].bitcast(U16).rearrange(shape, r=1 << l),
                                        bank[:, 4 + l % 2, 0:S // 2].rearrange(shape, r=1 << l)).then_inc(a_r, 1)
                    if read_before:
                        readout(h - 1, l)
                    if l == 0:
                        gate_of(h)

            def states(h):
                dve.wait_ge(pe_ds, h + 1)
                dve.wait_ge(tot_r, LEVELS * h + LEVELS)
                term = bank[:, 7, 0:3 * P].rearrange("p (c v) -> p c v", c=3)
                dve.tensor_copy(state[:, 0, :], term[:, 0, :]).then_inc(st_r, 1)
                for c in (1, 2):
                    dve.wait_ge(st_r, 3 * h + c)
                    dve.scalar_tensor_tensor(state[:, c, :], state[:, c - 1, :], tot[LEVELS][:, c:c + 1],
                                             term[:, c, :], ALU.mult, ALU.add).then_inc(st_r, 1)

            def gated(h):
                dve.wait_ge(orow_r, h + 1)
                dve.wait_ge(g_r, h + 1)
                dve.scalar_tensor_tensor(o_n, o_row, vec[:, C_NG:C_NG + 1], g_t, ALU.mult, ALU.mult
                                         ).then_inc(on_r, 1)

            def readout(h, piece):
                if 1 <= piece <= 4:
                    if piece == 1:
                        dve.wait_ge(rms_r, h + 1)
                    at_ = slice((piece - 1) * P, piece * P)
                    dve.reciprocal(o_inv[:, at_], o_rms[:, at_]).then_inc(oinv_r, 1)
                elif piece == 5:
                    dve.wait_ge(oinv_r, 4 * h + 4)
                    dve.wait_ge(on_r, h + 1)
                    dve.tensor_tensor(o_g, o_n, o_inv, ALU.mult).then_inc(og_r, 1)
                elif piece == 6:
                    dve.wait_ge(oh_r, h + 1)
                    at_ = bass.ds(h, 1)
                    dve.tensor_tensor(mid_lo[:, at_, :].rearrange("p a s -> p (a s)"), o_g,
                                      f32(mid_hi[:, at_, :]).rearrange("p a s -> p (a s)"), ALU.subtract
                                      ).then_inc(mid_ready, 1)

            split_lo(0, 1, NT)
            dve.wait_ge(masks, 2 + 3 * LEVELS)
            dve.wait_ge(lb_ready, 3)
            project(0)
            split_lo(1, 0, NT)
            query(0)
            embedding_lo(0)

            def head(i):
                split_lo(i, 1, NT)
                scores_of(i - 1, not (isinstance(i, int) and i == 1))
                split_lo(i + 1, 0, NT)
                project(i)
                states(i - 1)
                dve.wait_ge(pe_o, i)
                query(i)
                gated(i - 1)

            head(1)
            with dve.Fori(2, HEADS) as i:
                head(i)
            dve.wait_ge(k_r, HEADS)
            dve.engine_nop().then_inc(bank_free[0], 1)
            split_lo(R_WO, 1, NT)
            scores_of(HEADS - 1, True)
            dve.wait_ge(g_r, HEADS)
            dve.engine_nop().then_inc(bank_free[1], 1)
            states(HEADS - 1)
            gated(HEADS - 1)
            for hf in range(2):
                for piece in (2 * hf + 1, 2 * hf + 2):
                    readout(HEADS - 1, piece)
                dve.wait_ge(oinv_r, 4 * HEADS - 2 + 2 * hf)
                dve.wait_ge(on_r, HEADS)
                dve.tensor_tensor(o_g[:, half(hf)], o_n[:, half(hf)], o_inv[:, half(hf)], ALU.mult).then_inc(og_r, 1)
            for hf in range(2):
                dve.wait_ge(oh_r, HEADS + hf)
                ins = dve.tensor_tensor(mid_lo[:, HEADS - 1, half(hf)], o_g[:, half(hf)],
                                        f32(mid_hi[:, HEADS - 1, half(hf)]), ALU.subtract)
            ins.then_inc(mid_ready, 1)

            def sums(n, i, par):
                pp = 2 * i + par
                dve.wait_ge(y_r, 10 * n + 2 * pp + 2)
                if pp == 0:
                    dve.tensor_tensor(sum_y, x[:, 0, :], x[:, 1, :], ALU.add).then_inc(sumy_r, 1)
                    dve.wait_ge(sq_done, 10 * n + 2)
                    dve.tensor_tensor(sum_sq, sq[0], sq[1], ALU.add).then_inc(sumsq_r, 1)
                else:
                    for j in (2 * pp, 2 * pp + 1):
                        dve.wait_ge(sumy_r, 7 * n + j - 1)
                        dve.tensor_tensor(sum_y, sum_y, x[:, j, :], ALU.add).then_inc(sumy_r, 1)
                    for j in (2 * pp, 2 * pp + 1):
                        dve.wait_ge(sq_done, 10 * n + j + 1)
                        dve.wait_ge(sumsq_r, 7 * n + j - 1)
                        dve.tensor_tensor(sum_sq, sum_sq, sq[j % 2], ALU.add).then_inc(sumsq_r, 1)

            def sums_half(n, hf):
                at_ = half(hf)
                dve.wait_ge(y_r, 10 * n + 7 + 2 * hf)
                dve.wait_ge(sumy_r, 7 * n + 5 + hf)
                dve.tensor_tensor(sum_y[:, at_], sum_y[:, at_], x[:, NT - 2, at_], ALU.add).then_inc(sumy_r, 1)
                dve.wait_ge(sq_done, 10 * n + 7 + 2 * hf)
                dve.wait_ge(sumsq_r, 7 * n + 5 + hf)
                dve.tensor_tensor(sum_sq[:, at_], sum_sq[:, at_], sq[0][:, at_], ALU.add).then_inc(sumsq_r, 1)

            def free_bank(par):
                dve.engine_nop().then_inc(bank_free[par], 1)

            def norm(n, r, next_kt, take):
                def variance(hf):
                    moments, var, counted = bank[:, 2 + hf, 0:4], token[:, hf, 0, :], 8 * n + 4 * hf
                    dve.wait_ge(moments_mm, 2 * n + hf + 1)
                    dve.tensor_copy(var, moments[:, 0:2]).then_inc(var_r, 1)
                    dve.wait_ge(var_r, counted + 1)
                    dve.tensor_tensor(var, var, moments[:, 0:2], ALU.mult).then_inc(var_r, 1)
                    dve.wait_ge(var_r, counted + 2)
                    dve.tensor_tensor(var, moments[:, 2:4], var, ALU.subtract).then_inc(var_r, 1)
                    dve.wait_ge(var_r, counted + 3)
                    dve.tensor_scalar(var, var, 0.0, 1e-5, ALU.max, ALU.add).then_inc(var_r, 1)

                def diagonal(hf):
                    dve.wait_ge(std_r, 2 * n + hf + 1)
                    dve.reciprocal(token[:, hf, 2, :], token[:, hf, 1, :]).then_inc(inv_r, 1)
                    dve.wait_ge(inv_r, 2 * n + hf + 1)
                    for c in range(2):
                        at_ = slice((2 * hf + c) * P, (2 * hf + c + 1) * P)
                        ins = dve.tensor_scalar(diag[:, at_], ident[:, :], token[:, hf, 2, c:c + 1], float(P),
                                                ALU.mult, ALU.mult)
                    ins.then_inc(diag_r, 1)

                def low(hf, k):
                    if n < 3 * LAYERS - 1:
                        c = C_B + NT * n + k
                        dve.wait_ge(x_hi_ready, x_before(n) + NT * hf + k + 1)
                        dve.scalar_tensor_tensor(x_lo[:, k, half(hf)], x[:, k, half(hf)], vec[:, c:c + 1],
                                                 f32(x_hi[:, k, half(hf)]), ALU.add, ALU.subtract
                                                 ).then_inc(x_ready, 1)

                def scale(hf, k):
                    c = C_G + NT * n + k
                    dve.wait_ge(spread_mm, 2 * n + hf + 1)
                    dve.wait_ge(cen_r, 2 * NT * n + NT * hf + k + 1)
                    dve.scalar_tensor_tensor(x[:, k, half(hf)], x[:, k, half(hf)], vec[:, c:c + 1],
                                             bank[:, 6 + hf, HALF:S], ALU.mult, ALU.mult).then_inc(nrm_r, 1)

                take(0, 2)
                sums_half(n, 0)
                take(0, 3)
                variance(0)
                diagonal(0)
                take(1, 2)
                sums_half(n, 1)
                halves = [(hf, k) for hf in range(2) for k in range(NT)]
                for i, tile in enumerate(halves):
                    scale(*tile)
                    if i >= 2:
                        low(*halves[i - 2])
                    if i == 0:
                        take(1, 3)
                        free_bank(1)
                    if i == 3:
                        variance(1)
                    if i == 5:
                        diagonal(1)
                low(*halves[-2])
                low(*halves[-1])
                if next_kt is not None:
                    dve.wait_ge(w_lo_ready, 4 * r + 8)

            def rounds(r0, n, kt, next_kt, take):
                for i in range(n):
                    if i:
                        split_lo(r0 + i, 1, kt)
                    take(i, 0)
                    split_lo(r0 + i + 1, 0, kt if i < n - 1 else next_kt)
                    take(i, 1)

            def last_rounds(r, kt, next_kt, take):
                take(0, 0)
                split_lo(r + 1, 0, kt)
                take(0, 1)
                split_lo(r + 1, 1, kt)
                take(1, 0)
                if next_kt is not None:
                    split_lo(r + 2, 0, next_kt)

            def add_to_stream(n, r0, scale, final, kept=None):
                def take(i, par):
                    r = r0 + i
                    for u in range(2):
                        j = 4 * i + 2 * par + u
                        dve.wait_ge(unit_done, 4 * r + 2 * par + u + 1)
                        if kept is not None:
                            dve.wait_ge(x_kept, kept + j + 1)
                        ins = dve.scalar_tensor_tensor(x[:, j, :], x[:, j, :], scale, bank[:, 2 * par + u, :],
                                                       ALU.mult, ALU.add)
                        if final:
                            ins.then_inc(y_r, 1)
                    if not final:
                        ins.then_inc(bank_free[par], 1)
                    else:
                        sums(n, i, par)
                        free_bank(par)
                return take

            def add_half(n, r, scale):
                def take(hf, u):
                    if hf == 0:
                        dve.wait_ge(half_done, 2 * n + u - 1)
                    else:
                        dve.wait_ge(unit_done, 4 * r + u + 1)
                    at_ = x[:, NT // 2 + u, half(hf)]
                    dve.scalar_tensor_tensor(at_, at_, scale, bank[:, bank_of(hf, u), 0:HALF],
                                             ALU.mult, ALU.add).then_inc(y_r, 1)
                return take

            def hidden(layer, part, i, par):
                r = R_GU[layer][part] + i
                n = sum(PARTS[:part]) + 2 * i + par
                dve.wait_ge(silu_r[layer], n + 1)
                dve.tensor_tensor(hid[par], bank[:, 2 * par + 1, :], act_t[par], ALU.mult
                                  ).then_inc(bank_free[par], 1)
                dve.wait_ge(hhi_r[layer], n + 1)
                at_ = bass.ds(2 * i + par, 1)
                dve.tensor_tensor(mid_lo[:, at_, :].rearrange("p a s -> p (a s)"), hid[par],
                                  f32(mid_hi[:, at_, :]).rearrange("p a s -> p (a s)"), ALU.subtract
                                  ).then_inc(mid_ready, 1)

            last_rounds(R_WO, NT, NT, add_to_stream(0, R_WO, ALPHA, True))
            norm(0, R_WO + 1, NT, add_half(0, R_WO + 1, ALPHA))
            for layer in range(LAYERS):
                if layer == 1:
                    dve.wait_ge(k_w, 3)
                    dve.wait_ge(bank_free[0], freed(R_KV + 1))
                    for kvh in range(KVH):
                        own, other = HD * (kvh % 2), HD * (1 - kvh % 2)
                        dve.tensor_copy(k_pad[other:other + HD, kvh, WIN:], k_pad[own:own + HD, kvh, WIN:]
                                        ).then_inc(k_ok, 1)
                    split_lo(R_Q, 0, NT)
                    dve.wait_ge(far_ready, 5)
                    dve.wait_ge(sink_landed, 16)
                    def query_tile(j):
                        dve.wait_ge(unit_done, 4 * R_Q + j + 1)
                        dve.tensor_scalar(q_s[j % 2], bank[:, 7, :], vec[:, C_BQ + j:C_BQ + j + 1], ASCALE,
                                          ALU.add, ALU.mult).then_inc(q_ok, 1)
                        if j % 2:
                            free_bank(j // 2 % 2)

                    query_tile(0)
                    dve.wait_ge(v_turn, 1)
                    for u in range(2):
                        dve.tensor_copy(v_all[:, 2 * u:2 * u + 2, :].rearrange("p b v -> p (b v)"),
                                        bank[:, 4 + u, :]).then_inc(v_ok, 1)
                    query_tile(1)
                    split_lo(R_Q, 1, NT)
                    for n in range(QH + 4):
                        b = n % 2
                        if 3 <= n < QH + 3:
                            dve.wait_ge(t_done, n - 2)
                            if n > 4:
                                dve.wait_ge(pv_done, n - 4)
                            turned_to = p_t[(n - 3) % 2][:, 2:4, :, :].rearrange("p b h t -> p (b h t)")
                            dve.tensor_copy(turned_to, bank[:, 5, :]).then_inc(ptb_r, 1)
                        if n < QH:
                            slope = 2.0 ** (-8.0 * (n + 1) / QH)
                            dve.wait_ge(s_done, n + 1)
                            if n >= 3:
                                dve.wait_ge(t_done, n - 2)
                            dve.scalar_tensor_tensor(scores[n % 3].rearrange("p b s -> p (b s)"), dist, -slope,
                                                     bank[:, 2 * b:2 * b + 2, :].rearrange("p a s -> p (a s)"),
                                                     ALU.mult, ALU.add).then_inc(sc_r, 1)
                            dve.wait_ge(sc_r, n + 1)
                            dve.tensor_reduce(stat[:, b, 0, :], scores[n % 3], AX_X, ALU.max).then_inc(mx_r, 1)
                            dve.wait_ge(mx_r, n + 1)
                            dve.tensor_scalar(stat[:, b, 1, :], stat[:, b, 0, :], sink[:, n:n + 1], -1.0,
                                              ALU.max, ALU.mult).then_inc(nmx_r, 1)
                        if 1 <= n <= QH:
                            m, c = n - 1, (n - 1) % 2
                            dve.wait_ge(exp_r, m + 1)
                            dve.tensor_tensor(stat[:, c, 3, :], stat[:, c, 3, :], stat[:, c, 2, :], ALU.add
                                              ).then_inc(den_r, 1)
                            dve.wait_ge(den_r, m + 1)
                            dve.reciprocal(stat[:, c, 4, :], stat[:, c, 3, :]).then_inc(rden_r, 1)
                        if n - 1 in SPLIT_AT:
                            split_unit_lo(R_Q + SPLIT_AT[n - 1] // 4, SPLIT_AT[n - 1] % 4, NT)
                        if n >= 5 and n % 2:
                            t = (n - 5) // 2
                            dve.wait_ge(ohi_r, t + 1)
                            dve.tensor_tensor(mid_lo[:, t, :], bank[:, 6, :], f32(mid_hi[:, t, :]),
                                              ALU.subtract).then_inc(mid_ready, 1)
                        if n % 2 and (n + 3) // 2 < NT:
                            query_tile((n + 3) // 2)

                    def project_out(i, par):
                        for u in range(2):
                            j = 4 * i + 2 * par + u
                            dve.wait_ge(biased, j + 1)
                            dve.wait_ge(x_kept, NT * 2 + j + 1)
                            dve.scalar_tensor_tensor(x[:, j, :], x[:, j, :], ALPHA, act_t[u], ALU.mult, ALU.add
                                                     ).then_inc(y_r, 1)
                        free_bank(par)
                        sums(3, i, par)

                    def project_last(hf, u):
                        dve.wait_ge(biased, 5 + 2 * hf + u)
                        dve.wait_ge(x_kept, NT * 2 + NT // 2 + u + 1)
                        at_ = x[:, NT // 2 + u, half(hf)]
                        dve.scalar_tensor_tensor(at_, at_, ALPHA, act_t[u % 2][:, half(hf)], ALU.mult, ALU.add
                                                 ).then_inc(y_r, 1)
                    split_lo(R_AO + 1, 0, NT)
                    project_out(0, 0)
                    project_out(0, 1)
                    split_lo(R_AO + 1, 1, NT)
                    embedding_lo(1)
                    project_out(1, 0)
                    split_lo(R_AO + 2, 0, NT)
                    norm(3, R_AO + 1, NT, project_last)
                for part, n in enumerate(PARTS):
                    r = R_GU[layer][part]

                    def gate_up(i, next_kt):
                        hidden(layer, part, i, 0)
                        split_lo(r + i + 1, 0, next_kt)
                        hidden(layer, part, i, 1)
                        split_lo(r + i + 1, 1, next_kt)

                    if part:
                        split_lo(r, 1, NT)
                    with dve.Fori(0, n // 2 - 1) as i:
                        gate_up(i, NT)
                    gate_up(n // 2 - 1, n)
                    if part < len(PARTS) - 1:
                        rounds(R_DN[layer][part], 2, n, NT,
                               add_to_stream(3 * layer + 1, R_DN[layer][part], ALPHA if part == 0 else 1.0, False,
                                             NT * 3 * layer if part == 0 else None))
                r = R_DN[layer][-1] + 1
                last_rounds(r - 1, PARTS[-1], KMAX, add_to_stream(3 * layer + 1, r - 1, 1.0, True))
                norm(3 * layer + 1, r, KMAX, add_half(3 * layer + 1, r, 1.0))

                def embed(i, par):
                    for u in range(2):
                        dve.wait_ge(gate_r, 10 * layer + 4 * i + 2 * par + u + 1)
                        ins = dve.tensor_tensor(hid[u], bank[:, 4 + u, :], act_t[u], ALU.mult)
                    ins.then_inc(bank_free[par], 1)
                    dve.wait_ge(bank_free[par], freed(R_PLE[layer] + i + 1))
                    for u in range(2):
                        j = 4 * i + 2 * par + u
                        dve.wait_ge(x_kept, NT * (3 * layer + 1) + j + 1)
                        dve.scalar_tensor_tensor(x[:, j, :], x[:, j, :], ALPHA, hid[u], ALU.mult, ALU.add
                                                 ).then_inc(y_r, 1)
                    sums(3 * layer + 2, i, par)

                def embed_last(hf, u):
                    at_ = half(hf)
                    dve.wait_ge(gate_r, 10 * layer + 5 + 2 * hf + u)
                    dve.tensor_tensor(hid[u % 2][:, at_], bank[:, bank_of(hf, u), HALF:S], act_t[u % 2][:, at_],
                                      ALU.mult).then_inc(up_r, 1)
                    dve.wait_ge(up_r, 4 * layer + 2 * hf + u - 1)
                    dve.wait_ge(x_kept, NT * (3 * layer + 1) + NT // 2 + u + 1)
                    y = x[:, NT // 2 + u, at_]
                    dve.scalar_tensor_tensor(y, y, ALPHA, hid[u % 2][:, at_], ALU.mult, ALU.add).then_inc(y_r, 1)
                next_kt = NT if layer == 0 else None
                last_rounds(R_PLE[layer], KMAX, next_kt, embed)
                norm(3 * layer + 2, R_PLE[layer] + 1, next_kt, embed_last)
            for n, (t, side) in enumerate(RESULT):
                if n % 2 == 0:
                    dve.wait_ge(fin_t, n + 1)
                    dve.tensor_copy(out_rows[:, t, side * S:(side + 1) * S], bank[:, 2 * t + side, :]
                                    ).then_inc(fin_c[0], 1)

        @block.tensor
        def _(pe):
            def product(to, s, k, hi, lo, start, stop):
                cols = slice(k * P, (k + 1) * P)
                pe.matmul(to, w_hi[:, s, cols], hi, start=start, stop=False)
                pe.matmul(to, w_hi[:, s, cols], lo, start=False, stop=False)
                return pe.matmul(to, w_lo[:, s, cols], hi, start=False, stop=stop)

            def free(r, par, taken=None):
                if isinstance(taken, tuple):
                    pe.wait_ge(*taken)
                elif taken is not None:
                    pe.wait_ge(taken, r)
                elif not isinstance(r, int) or r > 0:
                    pe.wait_ge(bank_free[par], freed(r))

            def pair(r, par, kt, hi, lo, ready, base, also=None, taken=None, ks=None):
                for k in range(kt) if ks is None else ks:
                    if k == 0:
                        free(r, par, taken)
                    if ready is not None:
                        pe.wait_ge(ready, base + k + 1)
                    for u in range(2):
                        s = 2 * par + u
                        if k == 0:
                            pe.wait_ge(w_lo_ready, 4 * r + s + 1)
                        ins = product(bank[:, s, :], s, k, hi[:, k, :], lo[:, k, :], k == 0, k == kt - 1)
                        if k == kt - 1:
                            ins.then_inc(unit_done, 1)
                    if also is not None:
                        also(k)

            def opening(r, n, up=None):
                free(r, 0)
                for hf in range(2):
                    for k in range(NT):
                        if hf == 0 and k == 5:
                            spread(n, 1)
                        pe.wait_ge(x_ready, x_before(n) + NT * hf + k + 1)
                        for s in range(2):
                            if k == 0 and hf == 0:
                                pe.wait_ge(w_lo_ready, 4 * r + s + 1)
                            ins = product(bank[:, s, half(hf)], s, k, x_hi[:, k, half(hf)], x_lo[:, k, half(hf)],
                                          k == 0, k == NT - 1)
                            if up is None and hf and k == NT - 1:
                                ins.then_inc(unit_done, 1)

            def up_product(to, s, cols):
                for k in range(PT):
                    ins = product(to, s, NT + k, pe_hi[:, k, cols], pe_lo[:, k, cols], k == 0, k == PT - 1)
                return ins

            def statistics(n, hf):
                at_, moments, to = half(hf), bank[:, 2 + hf, :], bank[:, 6 + hf, 0:HALF]
                pe.wait_ge(sumy_r, 7 * n + 6 + hf)
                pe.matmul(to, ones_d[:, :], sum_y[:, at_], start=True, stop=False)
                pe.wait_ge(y_r, 10 * n + 8 + 2 * hf)
                pe.matmul(to, ones_d[:, :], x[:, NT - 1, at_], start=False, stop=True).then_inc(mean_mm, 1)
                for m, (total, last_tile) in enumerate(((sum_y, x[:, NT - 1, :]), (sum_sq, sq[1]))):
                    pe.wait_ge((sumy_r, sumsq_r)[m], 7 * n + 6 + hf)
                    pe.wait_ge((y_r, sq_done)[m], 10 * n + 8 + 2 * hf)
                    for c in range(2):
                        chunk, col = slice((2 * hf + c) * P, (2 * hf + c + 1) * P), slice(2 * m + c, 2 * m + c + 1)
                        pe.matmul(moments[:, col], total[:, chunk], ones_d[:, 0:1], start=True, stop=False)
                        ins = pe.matmul(moments[:, col], last_tile[:, chunk], ones_d[:, 0:1], start=False, stop=True)
                ins.then_inc(moments_mm, 1)

            def spread(n, hf):
                pe.wait_ge(mean_r, 2 * n + hf + 1)
                pe.wait_ge(diag_r, 2 * n + hf + 1)
                pe.matmul(bank[:, 6 + hf, HALF:S], ones_v[:, :], diag[:, half(hf)], start=True, stop=True
                          ).then_inc(spread_mm, 1)

            def closing(r, kt, hi, lo, n, up=False):
                stat_at, spread_at = ((2, 4), (3, 2)) if n % 3 == 0 else ((3, 0), (3, 4))
                free(r, 1)
                for hf in range(2):
                    if hf:
                        pe.wait_ge(bank_free[0], freed(r + 1))
                    for u in (2, 3):
                        pe.wait_ge(w_lo_ready, 4 * r + u + 1)
                        to = bank[:, bank_of(hf, u), :]
                        for k in range(kt):
                            ins = product(to[:, 0:HALF], u, k, hi[:, k, half(hf)], lo[:, k, half(hf)],
                                          k == 0, k == kt - 1)
                            if hf and (u, k) == stat_at:
                                statistics(n, 0)
                            if hf and (u, k) == spread_at:
                                spread(n, 0)
                        if up:
                            ins = up_product(to[:, HALF:S], u, half(hf))
                        ins.then_inc(unit_done if hf else half_done, 1)
                statistics(n, 1)

            def turn_stream(ks):
                for k in ks:
                    if k >= 4:
                        pe.wait_ge(x_hi_ready, k - 3)
                    for t in range(TT):
                        ins = pe.transpose(bank[:, 4 + k % 4, t * P:(t + 1) * P],
                                           x_rows[:, t, k * P:(k + 1) * P], ident[:, :])
                    ins.then_inc(turned, 1)

            pe.wait_ge(consts, 4)
            pe.wait_ge(rows_landed[0], 16)
            turn_stream(range(4))
            pair(0, 0, NT, x_hi, x_lo, x_ready, 0, ks=range(4))
            pe.wait_ge(rows_landed[1], 16)
            turn_stream(range(4, NT))
            pe.wait_ge(vecs_landed, 16 * 8)
            pe.wait_ge(x_hi_ready, 5)
            pe.transpose(bank[:, 4, 0:N_A], vec_rows[0:N_A, 0, :], ident[0:N_A, 0:N_A])
            pe.transpose(bank[:, 4, P:P + N_ALL - N_A], vec_rows[0:N_ALL - N_A, 1, :],
                         ident[0:N_ALL - N_A, 0:N_ALL - N_A]).then_inc(turned, 1)

            def turn_embedding(layer):
                pe.wait_ge(p_landed[layer], 16)
                for k in range(PT):
                    for t in range(TT):
                        ins = pe.transpose(bank[:, 4 + k, t * P:(t + 1) * P], p_rows[:, t, k * P:(k + 1) * P],
                                           ident[:, :])
                    ins.then_inc(turned, 1)

            def recur(h, step):
                if step == 1:
                    pe.wait_ge(vt_r, h + 1)
                    for c in range(TT):
                        ins = pe.transpose(bank[:, 6, c * P:(c + 1) * P], v_t[:, c * P:(c + 1) * P], ident[:, :])
                    ins.then_inc(pe_vtr, 1)
                    pe.wait_ge(k_r, h + 1)
                    pe.wait_ge(q_r, h + 1)
                    for c in range(TT):
                        at_ = slice(c * P, (c + 1) * P)
                        ins = pe.matmul(bank[:, 7, at_], k_raw[:, at_], q_t[:, at_], start=True, stop=True)
                    ins.then_inc(pe_diag, 1)
                elif 2 <= step <= LEVELS + 1:
                    l = step - 2
                    pe.wait_ge(qd_r, (LEVELS + 1) * h + l + 1)
                    if l == 0:
                        pe.wait_ge(kd0_r, h + 1)
                    else:
                        pe.wait_ge(kd_r, LEVELS * h + l)
                    pe.wait_ge(a_r, (LEVELS + 1) * h + (l + 1 if l >= 2 else 1))
                    for c in range(TT):
                        at_ = slice(c * P, (c + 1) * P)
                        ins = pe.matmul(bank[:, 4 + l % 2, c * 64:(c + 1) * 64].rearrange(
                            "p (b r) -> p b r", r=1 << l), k_dec[:, at_], second(q_dec[:, at_], l),
                            start=True, stop=True)
                    ins.then_inc(pe_lvl, 1)
                elif step == LEVELS + 2:
                    pe.wait_ge(kd_r, LEVELS * h + LEVELS)
                    pe.wait_ge(vrow_r, h + 1)
                    for c in range(3):
                        ins = pe.transpose(bank[:, 6, c * P:(c + 1) * P], k_dec[:, c * P:(c + 1) * P], ident[:, :])
                    ins.then_inc(pe_kt, 1)
                elif step == LEVELS + 4:
                    pe.wait_ge(kt_r, h + 1)
                    pe.wait_ge(a_r, (LEVELS + 1) * h + 2)
                    for c in range(3):
                        ins = pe.matmul(bank[:, 7, c * P:(c + 1) * P], kd_row[:, c, :], v_row[:, c, :],
                                        start=True, stop=True)
                    ins.then_inc(pe_ds, 1)
                elif step == LEVELS + 6:
                    pe.wait_ge(a_r, (LEVELS + 1) * (h + 1) + 1)
                    pe.wait_ge(qd_r, (LEVELS + 1) * (h + 1))
                    pe.wait_ge(st_r, 3 * h + 3)
                    for c in range(TT):
                        at_ = slice(c * P, (c + 1) * P)
                        ins = pe.matmul(bank[:, 6, at_], v_row[:, c, :], a_mat[:, at_], start=True, stop=c == 0)
                        if c:
                            ins = pe.matmul(bank[:, 6, at_], state[:, c - 1, :], q_dec[:, at_],
                                            start=False, stop=True)
                    ins.then_inc(pe_o, 1)
                elif step == LEVELS + 7:
                    pe.wait_ge(osq_r, h + 1)
                    pe.matmul(bank[:, 7, :], ones_v[:, :], o_sq, start=True, stop=True).then_inc(pe_ms, 1)

            pair(0, 0, NT, x_hi, x_lo, x_ready, 0, ks=range(4, NT))
            pair(0, 1, NT, x_hi, x_lo, x_ready, 0)
            pe.wait_ge(turn_read, 1)
            pe.wait_ge(x_hi_ready, 6)
            turn_embedding(0)
            pe.wait_ge(p_lo_ready, PT)
            with pe.Fori(1, HEADS) as i:
                h = i - 1
                pair(i, 0, NT, x_hi, x_lo, None, 0, lambda k: recur(h, k), k_r)
                pair(i, 1, NT, x_hi, x_lo, None, 0, lambda k: recur(h, NT + k), g_r)
            last = HEADS - 1
            steps = [(0, range(last - 1), 0), (1, range(last - 1), last - 1), (0, [last - 1], last - 1),
                     (1, [last - 1], last)]
            for par, ks, first_step in steps:
                pair(R_WO, par, NT, mid_hi, mid_lo, mid_ready, M_HG, lambda k: recur(last, first_step + k),
                     (k_r, g_r)[par], ks)
            recur(last, 2 * last)
            pair(R_WO, 0, NT, mid_hi, mid_lo, mid_ready, M_HG, ks=[last])
            pair(R_WO, 1, NT, mid_hi, mid_lo, mid_ready, M_HG, ks=[last])

            def rounds(r0, n, kt, hi, lo, ready, base):
                if n:
                    with pe.Fori(r0, r0 + n) as r:
                        pair(r, 0, kt, hi, lo, ready, base)
                        pair(r, 1, kt, hi, lo, ready, base)

            pair(R_WO + 1, 0, NT, mid_hi, mid_lo, None, 0)
            closing(R_WO + 1, NT, mid_hi, mid_lo, 0)
            for layer in range(LAYERS):
                if layer == 1:
                    opening(R_KV, 2)
                    pair(R_KV, 1, NT, x_hi, x_lo, None, 0)
                    def query_tile(j, ks):
                        for k in ks:
                            if k == 0:
                                pe.wait_ge(w_lo_ready, 4 * R_Q + j + 1)
                                if j:
                                    pe.wait_ge(q_ok, j)
                            ins = product(bank[:, 7, :], j % 4, k, x_hi[:, k, :], x_lo[:, k, :],
                                          k == 0, k == NT - 1)
                        if NT - 1 in ks:
                            ins.then_inc(unit_done, 1)

                    def scores_of(n):
                        b, g = n % 2, n // G
                        rows = slice(HD * (n % 2), HD * (n % 2) + HD)
                        pe.wait_ge(q_ok, n // 2 + 1)
                        if n == 0:
                            pe.wait_ge(k_ok, KVH)
                        if n >= 2:
                            pe.wait_ge(sc_r, n - 1)
                        for blk in range(TT):
                            ins = pe.matmul(bank[:, 2 * b + blk // 2, (blk % 2) * 2 * WIN:(blk % 2 + 1) * 2 * WIN],
                                            q_s[n // 2 % 2][rows, blk * P:(blk + 1) * P],
                                            k_pad[rows, g, blk * WIN:(blk + 2) * WIN], start=True, stop=True)
                        ins.then_inc(s_done, 1)

                    query_tile(0, range(NT))
                    pe.wait_ge(v_w, 1)
                    pe.wait_ge(bank_free[1], freed(R_KV + 1))
                    for blk in range(TT):
                        for u in range(2):
                            at_ = (blk % 2) * KVD + u * P
                            ins = pe.transpose(bank[:, 4 + blk // 2, at_:at_ + P],
                                               v_cols[:, u, blk * P:(blk + 1) * P], ident[:, :])
                    ins.then_inc(v_turn, 1)
                    query_tile(1, range(NT))
                    pe.wait_ge(bank_free[1], freed(R_KV + 1))
                    scores_of(0)
                    def out_unit(u, ks):
                        for k in ks:
                            if k == 0:
                                pe.wait_ge(w_lo_ready, 4 * R_AO + u + 1)
                                pe.wait_ge(bank_free[u // 2], freed(R_AO))
                                if u == 0:
                                    pe.wait_ge(q_ok, NT)
                                else:
                                    pe.wait_ge(sc_r, QH - 1 + u // 2)
                            pe.wait_ge(mid_ready, M_AT + k + 1)
                            ins = product(bank[:, u or 7, :], u, k, mid_hi[:, k, :], mid_lo[:, k, :],
                                          k == 0, k == NT - 1)
                            if k == NT - 1:
                                ins.then_inc(unit_done, 1)

                    for n in range(QH + 3):
                        if n + 1 < QH:
                            scores_of(n + 1)
                        if 2 <= n <= QH + 1:
                            m = n - 2
                            pe.wait_ge(p_r, m + 1)
                            if m == 0:
                                pe.wait_ge(v_ok, 2)
                            else:
                                pe.wait_ge(pta_r, m)
                                pe.wait_ge(ptb_r, m)
                            for blk in range(TT):
                                for side in range(2):
                                    at_ = (blk % 2) * 2 * P + side * P
                                    ins = pe.transpose(bank[:, 4 + blk // 2, at_:at_ + P],
                                                       scores[m % 3][:, blk, side * P:(side + 1) * P], ident[:, :])
                            ins.then_inc(t_done, 1)
                        j = (n + 4) // 2
                        if j < NT:
                            query_tile(j, range(NT // 2, NT) if n % 2 else range(NT // 2))
                        for u, ks in OUT_AT.get(n, ()):
                            out_unit(u, ks)
                        if 3 <= n:
                            m = n - 3
                            kvh, t = m // G, m // 2
                            rows = slice(HD * (m % 2), HD * (m % 2) + HD)
                            vs = slice(HD * kvh, HD * kvh + HD)
                            pe.wait_ge(pta_r, m + 1)
                            pe.wait_ge(ptb_r, m + 1)
                            if t >= 1:
                                pe.wait_ge(mid_ready, M_AT + t)
                            for blk in range(TT):
                                to, probs = bank[rows, 6, blk * P:(blk + 1) * P], p_t[m % 2]
                                if blk:
                                    pe.matmul(to, v_all[:, blk - 1, vs], probs[:, blk, 0, :], start=True, stop=False)
                                ins = pe.matmul(to, v_all[:, blk, vs], probs[:, blk, 1, :], start=blk == 0, stop=True)
                            ins.then_inc(pv_done, 1)
                    turn_embedding(1)
                    for u, ks in OUT_AT[QH + 3]:
                        out_unit(u, ks)
                    pair(R_AO + 1, 0, NT, mid_hi, mid_lo, None, 0, taken=(biased, 2))
                    pe.wait_ge(p_lo_ready, 2 * PT)
                    closing(R_AO + 1, NT, mid_hi, mid_lo, 3)
                for part, n in enumerate(PARTS):
                    r = R_GU[layer][part]
                    if part == 0:
                        opening(r, 3 * layer)
                        pair(r, 1, NT, x_hi, x_lo, None, 0)
                    rounds(r + (part == 0), n // 2 - (part == 0), NT, x_hi, x_lo, None, 0)
                    r, base = R_DN[layer][part], M_GU[layer][part]
                    if part < len(PARTS) - 1:
                        rounds(r, 2, n, mid_hi, mid_lo, mid_ready, base)
                    else:
                        rounds(r, 1, n, mid_hi, mid_lo, mid_ready, base)
                        pair(r + 1, 0, n, mid_hi, mid_lo, None, 0)
                        closing(r + 1, n, mid_hi, mid_lo, 3 * layer + 1)
                n = 3 * layer + 2
                for pp in range(NT // 2 - 1):
                    r, par = R_PLE[layer] + pp // 2, pp % 2
                    if pp == 0:
                        opening(r, n - 1, up=True)
                        pe.wait_ge(p_lo_ready, PT * (layer + 1))
                    else:
                        free(r, par)
                        for k in range(NT):
                            for s in (2 * par, 2 * par + 1):
                                if k == 0:
                                    pe.wait_ge(w_lo_ready, 4 * r + s + 1)
                                product(bank[:, s, :], s, k, x_hi[:, k, :], x_lo[:, k, :], k == 0, k == NT - 1)
                        pe.wait_ge(bank_free[1 - par], freed(r + par))
                    for u in range(2):
                        up_product(bank[:, 4 + u, :], 2 * par + u, slice(0, S)).then_inc(unit_done, 1)
                closing(R_PLE[layer] + 1, NT, x_hi, x_lo, n, up=True)
            for n, (t, side) in enumerate(RESULT):
                if n == 2:
                    spread(3 * LAYERS - 1, 1)
                if t == TT - 1:
                    pe.wait_ge(nrm_r, 2 * NT * 3 * LAYERS)
                for k in range(4 * side, 4 * side + 4):
                    pe.wait_ge(x_f32, NT + NT * (t // 2) + k + 1)
                    ins = pe.transpose(bank[:, 2 * t + side, (k % 4) * P:(k % 4 + 1) * P],
                                       x[:, k, t * P:(t + 1) * P], ident[:, :])
                ins.then_inc(fin_t, 1)


_INS = ['x', 'p', 'a_w_in', 'a_lower_bound', 'a_norm_gain', 'a_w_out', 'kv_w', 'kv_b', 'b_w_q', 'b_b_q', 'b_sinks',
        'b_w_out', 'b_b_out', 'ffn_w_gate_up', 'ffn_w_down', 'ple_w_up', 'ple_w_gate', 'ple_b_gate', 'ln_gain',
        'ln_bias']


def kernel(**inputs):
    import numpy as _np
    import concourse.bacc as _bacc
    from concourse import mybir as _mybir
    from concourse.bass_utils import run_bass_kernel_spmd as _run

    nc = _bacc.Bacc("TRN2", target_bir_lowering=False, num_devices=1)
    arrays, args = {}, []
    for name in _INS:
        a = _np.ascontiguousarray(inputs[name])
        arrays[f"in_{name}_dram"] = a
        args.append(nc.dram_tensor(f"in_{name}_dram", a.shape, _mybir.dt.from_np(a.dtype), kind="ExternalInput").ap())
    shape = inputs['x'].shape
    args.append(nc.dram_tensor("out_0_dram", shape, _mybir.dt.float32, kind="ExternalOutput").ap())
    yoco_trunk(nc, *args)
    r = _run(nc, [arrays], core_ids=[0])
    return r.results[0]["out_0_dram"]
```
